# Optimizing a Trainium2 kernel written in Bass

```python
import jax, jax.numpy as jnp
from jax import lax
import numpy as np

D_MODEL = 1024
BATCH = 1
SEQ = 1024
DEPTH = 1
DEC_BATCH = 8
DEC_SEQ = 16
PAST_LEN = 256

CHUNK = 64
D_RNN = D_MODEL
RNN_HEADS = 16
RNN_HEAD_DIM = D_RNN // RNN_HEADS
CONV_WIDTH = 4
RG_C = 8.0
D_SGU = D_MODEL
SGU_HEADS = 8
SGU_HEAD_DIM = D_SGU // SGU_HEADS
SGU_CHUNK = 128
D_FF = 2816
D_IN = 2 * D_RNN + 2 * D_SGU + 2 * D_MODEL
N_MOD = 9
EPS = 1e-6

kernel_name = 'hybrid_rglru_sgu_stream_step'

def _rms(x, g):
    xf = x.astype(jnp.float32)
    y = xf * lax.rsqrt(jnp.mean(xf * xf, axis=-1, keepdims=True) + EPS)
    return (y * g.astype(jnp.float32)).astype(x.dtype)

def _layernorm(x, g, b):
    xf = x.astype(jnp.float32)
    mu = jnp.mean(xf, axis=-1, keepdims=True)
    var = jnp.mean(jnp.square(xf - mu), axis=-1, keepdims=True)
    y = (xf - mu) * lax.rsqrt(var + EPS)
    return (y * g.astype(jnp.float32) + b.astype(jnp.float32)).astype(x.dtype)

def _modulate(xn, shift, scale):
    return xn * (1.0 + scale[:, None, :]) + shift[:, None, :]

def _swiglu(x, w_gate, w_up, w_down):
    return (jax.nn.silu(x @ w_gate) * (x @ w_up)) @ w_down

def _rg_lru(xc, h0, w_a, b_a, w_x, b_x, lam):
    B, T, _ = xc.shape
    xh = xc.reshape(B, T, RNN_HEADS, RNN_HEAD_DIM)
    r = jax.nn.sigmoid(jnp.einsum('bthi,hij->bthj', xh, w_a).reshape(B, T, D_RNN) + b_a)
    i = jax.nn.sigmoid(jnp.einsum('bthi,hij->bthj', xh, w_x).reshape(B, T, D_RNN) + b_x)
    log_a = -RG_C * r.astype(jnp.float32) * jax.nn.softplus(-lam.astype(jnp.float32))
    a = jnp.exp(log_a)
    mult = jnp.sqrt(-jnp.expm1(2.0 * log_a))
    b = mult * (i * xc).astype(jnp.float32)
    b = b.at[:, 0].add(a[:, 0] * h0.astype(jnp.float32))

    def combine(left, right):
        a1, b1 = left
        a2, b2 = right
        return a1 * a2, a2 * b1 + b2

    _, h = lax.associative_scan(combine, (a, b), axis=1)
    return h, h[:, -1]

def _sgu(u, v, g_v, b_v, w_s, b_s):
    B, T, _ = v.shape
    vn = _layernorm(v, g_v, b_v)
    n = -(-T // SGU_CHUNK)
    pad = n * SGU_CHUNK - T
    vp = jnp.pad(vn, ((0, 0), (0, pad), (0, 0))).reshape(B, n, SGU_CHUNK, SGU_HEADS, SGU_HEAD_DIM)
    mask = jnp.tril(jnp.ones((SGU_CHUNK, SGU_CHUNK), dtype=bool))
    w = jnp.where(mask[None], w_s, 0.0).astype(vp.dtype)
    s = jnp.einsum('hts,bnshc->bnthc', w, vp)
    s = s + jnp.transpose(b_s)[None, None, :, :, None].astype(vp.dtype)
    s = s.reshape(B, n * SGU_CHUNK, D_SGU)[:, :T]
    v_state = vn[:, (n - 1) * SGU_CHUNK:]
    return u * s, v_state

def _mixer(xn, conv_buf, h0, w_in, w_conv, b_conv, w_rg_a, b_rg_a, w_rg_x, b_rg_x,
           rg_lambda, ln_v_g, ln_v_b, w_spatial, b_spatial, w_out):
    T = xn.shape[1]
    z = xn @ w_in
    x_r = z[..., :D_RNN]
    gate_r = z[..., D_RNN:2 * D_RNN]
    uv = z[..., 2 * D_RNN:2 * D_RNN + 2 * D_SGU]
    g_a = z[..., 2 * D_RNN + 2 * D_SGU:2 * D_RNN + 2 * D_SGU + D_MODEL]
    g_b = z[..., 2 * D_RNN + 2 * D_SGU + D_MODEL:]
    xp = jnp.concatenate([conv_buf.astype(x_r.dtype), x_r], axis=1)
    xc = b_conv + sum(xp[:, k:k + T] * w_conv[k] for k in range(CONV_WIDTH))
    new_buf = xp[:, -(CONV_WIDTH - 1):]
    h, h_last = _rg_lru(xc, h0, w_rg_a, b_rg_a, w_rg_x, b_rg_x, rg_lambda)
    y_a = h.astype(xn.dtype) * jax.nn.gelu(gate_r)
    uv = jax.nn.gelu(uv)
    u, v = uv[..., :D_SGU], uv[..., D_SGU:]
    y_b, v_state = _sgu(u, v, ln_v_g, ln_v_b, w_spatial, b_spatial)
    merged = jax.nn.sigmoid(g_a) * y_a + jax.nn.sigmoid(g_b) * y_b
    return merged @ w_out, new_buf, h_last, v_state

def _layer(x, c, conv_buf, h0, w_ada, b_ada, g_ffn1, w_ffn1_gate, w_ffn1_up, w_ffn1_down,
           g_mix, w_in, w_conv, b_conv, w_rg_a, b_rg_a, w_rg_x, b_rg_x, rg_lambda,
           ln_v_g, ln_v_b, w_spatial, b_spatial, w_out,
           g_ffn2, w_ffn2_gate, w_ffn2_up, w_ffn2_down):
    B = x.shape[0]
    ada = (jax.nn.silu(c) @ w_ada + b_ada).reshape(B, N_MOD, D_MODEL)
    xn = _modulate(_rms(x, g_ffn1), ada[:, 0], ada[:, 1])
    x = x + 0.5 * ada[:, 2][:, None] * _swiglu(xn, w_ffn1_gate, w_ffn1_up, w_ffn1_down)
    xn = _modulate(_rms(x, g_mix), ada[:, 3], ada[:, 4])
    m, new_buf, h_last, v_state = _mixer(xn, conv_buf, h0, w_in, w_conv, b_conv, w_rg_a, b_rg_a,
                                         w_rg_x, b_rg_x, rg_lambda, ln_v_g, ln_v_b,
                                         w_spatial, b_spatial, w_out)
    x = x + ada[:, 5][:, None] * m
    xn = _modulate(_rms(x, g_ffn2), ada[:, 6], ada[:, 7])
    x = x + 0.5 * ada[:, 8][:, None] * _swiglu(xn, w_ffn2_gate, w_ffn2_up, w_ffn2_down)
    return x, new_buf, h_last, v_state

def _final(x, c, w_ada_final, b_ada_final, g_final):
    B = x.shape[0]
    ada = (jax.nn.silu(c) @ w_ada_final + b_ada_final).reshape(B, 2, D_MODEL)
    return _modulate(_rms(x, g_final), ada[:, 0], ada[:, 1])

def setup_inputs(seed: int = 0) -> dict:
    key = jax.random.key(seed)
    ks = iter(jax.random.split(key, 48))

    def nrm(shape, scale):
        return jax.random.normal(next(ks), shape, jnp.float32) * scale

    L, D = DEPTH, D_MODEL
    inp = {}
    inp['x_prompt'] = nrm((BATCH, SEQ, D), 1.0)
    inp['x_sample'] = nrm((DEC_BATCH, DEC_SEQ, D), 1.0)
    inp['cache_conv'] = nrm((L, DEC_BATCH, CONV_WIDTH - 1, D_RNN), 1.0)
    inp['state_rglru'] = nrm((L, DEC_BATCH, D_RNN), 0.5)
    inp['c_prompt'] = nrm((BATCH, D), 1.0)
    inp['c_sample'] = nrm((DEC_BATCH, D), 1.0)
    inp['w_ada_final'] = nrm((D, 2 * D), 0.5 * D ** -0.5)
    inp['b_ada_final'] = nrm((2 * D,), 0.01)
    inp['g_final'] = 1.0 + nrm((D,), 0.02)
    inp['w_ada'] = nrm((L, D, N_MOD * D), 0.5 * D ** -0.5)
    inp['b_ada'] = nrm((L, N_MOD * D), 0.01)
    inp['g_ffn1'] = 1.0 + nrm((L, D), 0.02)
    inp['w_ffn1_gate'] = nrm((L, D, D_FF), D ** -0.5)
    inp['w_ffn1_up'] = nrm((L, D, D_FF), D ** -0.5)
    inp['w_ffn1_down'] = nrm((L, D_FF, D), D_FF ** -0.5)
    inp['g_mix'] = 1.0 + nrm((L, D), 0.02)
    inp['w_in'] = nrm((L, D, D_IN), D ** -0.5)
    inp['w_conv'] = nrm((L, CONV_WIDTH, D_RNN), CONV_WIDTH ** -0.5)
    inp['b_conv'] = nrm((L, D_RNN), 0.01)
    inp['w_rg_a'] = nrm((L, RNN_HEADS, RNN_HEAD_DIM, RNN_HEAD_DIM), RNN_HEAD_DIM ** -0.5)
    inp['b_rg_a'] = nrm((L, D_RNN), 0.01)
    inp['w_rg_x'] = nrm((L, RNN_HEADS, RNN_HEAD_DIM, RNN_HEAD_DIM), RNN_HEAD_DIM ** -0.5)
    inp['b_rg_x'] = nrm((L, D_RNN), 0.01)
    a_c = jax.random.uniform(next(ks), (L, D_RNN), jnp.float32, minval=0.9, maxval=0.999)
    s = a_c ** (1.0 / RG_C)
    inp['rg_lambda'] = jnp.log(s) - jnp.log1p(-s)
    inp['ln_v_g'] = 1.0 + nrm((L, D_SGU), 0.02)
    inp['ln_v_b'] = nrm((L, D_SGU), 0.01)
    inp['w_spatial'] = nrm((L, SGU_HEADS, SGU_CHUNK, SGU_CHUNK), SGU_CHUNK ** -0.5)
    inp['b_spatial'] = 1.0 + nrm((L, SGU_HEADS, SGU_CHUNK), 0.02)
    inp['w_out'] = nrm((L, D, D), D ** -0.5)
    inp['g_ffn2'] = 1.0 + nrm((L, D), 0.02)
    inp['w_ffn2_gate'] = nrm((L, D, D_FF), D ** -0.5)
    inp['w_ffn2_up'] = nrm((L, D, D_FF), D ** -0.5)
    inp['w_ffn2_down'] = nrm((L, D_FF, D), D_FF ** -0.5)
    return inp

def reference(x_prompt, x_sample, cache_conv, state_rglru, c_prompt, c_sample,
              w_ada_final, b_ada_final, g_final, w_ada, b_ada, g_ffn1, w_ffn1_gate,
              w_ffn1_up, w_ffn1_down, g_mix, w_in, w_conv, b_conv, w_rg_a, b_rg_a,
              w_rg_x, b_rg_x, rg_lambda, ln_v_g, ln_v_b, w_spatial, b_spatial, w_out,
              g_ffn2, w_ffn2_gate, w_ffn2_up, w_ffn2_down):
    hp, hs = x_prompt, x_sample
    conv_p, rg_p, v_p, conv_s, rg_s, v_s = [], [], [], [], [], []
    for l in range(DEPTH):
        lw = (w_ada[l], b_ada[l], g_ffn1[l], w_ffn1_gate[l], w_ffn1_up[l], w_ffn1_down[l],
              g_mix[l], w_in[l], w_conv[l], b_conv[l], w_rg_a[l], b_rg_a[l], w_rg_x[l],
              b_rg_x[l], rg_lambda[l], ln_v_g[l], ln_v_b[l], w_spatial[l], b_spatial[l],
              w_out[l], g_ffn2[l], w_ffn2_gate[l], w_ffn2_up[l], w_ffn2_down[l])
        zero_buf = jnp.zeros((hp.shape[0], CONV_WIDTH - 1, D_RNN), hp.dtype)
        zero_h = jnp.zeros((hp.shape[0], D_RNN), jnp.float32)
        hp, cb, hl, vs = _layer(hp, c_prompt, zero_buf, zero_h, *lw)
        conv_p.append(cb); rg_p.append(hl); v_p.append(vs)
        hs, cb, hl, vs = _layer(hs, c_sample, cache_conv[l], state_rglru[l], *lw)
        conv_s.append(cb); rg_s.append(hl); v_s.append(vs)
    y_prompt = _final(hp, c_prompt, w_ada_final, b_ada_final, g_final)
    y_sample = _final(hs, c_sample, w_ada_final, b_ada_final, g_final)
    return (y_prompt, y_sample, jnp.stack(conv_p), jnp.stack(rg_p), jnp.stack(v_p),
            jnp.stack(conv_s), jnp.stack(rg_s), jnp.stack(v_s))


_drawn_inputs = setup_inputs


def setup_inputs(seed=0):
    import zlib

    import numpy as np

    out = dict(_drawn_inputs(seed))
    spreads = {}
    factors = {'b_ada_final': 4.344,
     'g_final': 27.879,
     'g_ffn1': 8.0,
     'b_rg_a': 31.585,
     'b_rg_x': 8.0,
     'ln_v_g': 23.375,
     'ln_v_b': 45.931,
     'b_spatial': 198.806,
     'g_ffn2': 23.647}
    for name, (base, spread) in spreads.items():
        noise = np.random.default_rng([zlib.crc32(name.encode()), seed]).standard_normal(out[name].shape)
        drawn = base * np.exp(spread * noise) if base else spread * noise
        out[name] = __import__('jax').numpy.asarray(drawn.astype(out[name].dtype))
    for name, factor in factors.items():
        out[name] = (out[name] * factor).astype(out[name].dtype)
    return out
```

```python
import numpy as np
import concourse.bass as bass
from concourse import mybir

F32 = mybir.dt.float32
F32R = mybir.dt.float32r
ALU = mybir.AluOpType
ACT = mybir.ActivationFunctionType
ds = bass.ds

P = 128
D = 1024
KT = D // P
SEQ = 1024
NS, LS = 8, 16
NSEQ = 1 + NS
TOK = SEQ + NS * LS
CH = 384
NCH = TOK // CH
PC2 = SEQ - 2 * CH
NT = TOK // P
DFF = 2816
NF = DFF // P
GROUPS = NF // 2
TAPS = 4
HIST = TAPS - 1
EPS = 1e-6
UNIT = D
RING = 6
NADA = 11 * KT
HALF = D // 2
TAIL = NSEQ + HIST * NSEQ

U_FFN1 = 0
U_V = U_FFN1 + 6 * GROUPS
U_MIX = U_V + 8
U_OUT = U_MIX + 6 * KT
U_FFN2 = U_OUT + 8
U_END = U_FFN2 + 6 * GROUPS

SHIFT1, SCALE1, GATE1, SHIFTM, SCALEM, GATEM, SHIFT2, SCALE2, GATE2, SHIFTF, SCALEF = range(11)
V_G1, V_GM, V_G2, V_GF, V_BCONV, V_WCONV, V_BA, V_BX, V_LAM = 0, 8, 16, 24, 32, 40, 72, 80, 88
NVEC = 96

XW_IN = 2 * NT
XW_FFN1 = XW_IN + 24 * GROUPS
XW_OUT = XW_FFN1 + 24
XW_FFN2 = XW_OUT + 24 * GROUPS


def build(nc, ins, outs):
    cursor = [1152]

    def at(name, shape, dtype=F32, offset=None):
        size = 4 * int(np.prod(shape[1:]))
        if offset is None:
            offset = cursor[0]
            cursor[0] += -(-size // 32) * 32
        return nc.alloc_sbuf_tensor_at(name, shape, dtype, offset=offset, align_bytes=32)

    ident = at("ident", [P, P])
    ones = at("ones", [P, P])
    ada = at("ada", [P, NADA, NSEQ])
    vecT = at("vecT", [P, NVEC])
    badaT = at("badaT", [P, NADA])
    cT = at("cT", [P, KT, NSEQ + 1])
    histT = at("histT", [P, KT, 32])
    blk = at("blk", [P, 3])
    epst = at("epst", [P, 8])
    tails = at("tails", [P, KT, TAIL])
    mv = at("mv", [P, NT, 2])
    vstd = at("vstd", [P, NT + 1])
    bnst = at("bnst", [P, NT, 2, 6])
    raw = at("raw", [P, 2, UNIT])
    w_hi = at("w_hi", [P, RING, UNIT], F32R)
    w_lo = at("w_lo", [P, RING, UNIT], F32R)
    xn_at = cursor[0]
    xn_hi = at("xn_hi", [P, KT, TOK], F32R)
    xn_lo = at("xn_lo", [P, KT, TOK], F32R)
    region = cursor[0]

    x = at("x", [P, KT, TOK])
    h_at = cursor[0]
    h_hi = at("h_hi", [P, 2, TOK], F32R)
    h_lo = at("h_lo", [P, 2, TOK], F32R)
    silu = at("silu", [P, 2, CH])
    hfull = at("hfull", [P, 2, CH])
    sq = at("sq", [P, 2, CH])
    std = at("std", [P, 2, CH])
    gtmp = at("gtmp", [P, 2, P])
    end_ffn = cursor[0]
    tbuf, xfull = silu, hfull
    merged_in = at("merged_in", [P, KT, TOK], offset=h_at)
    yT = at("yT", [P, KT, CH], offset=xn_at)
    yrow = at("yrow", [P, 2, D], offset=xn_at + 4 * KT * CH)
    tailrow = at("tailrow", [TAIL, D], offset=xn_at + 4 * KT * CH + 8 * D)
    w_ada_sb = at("w_ada_sb", [P, 2, KT, D], offset=xn_at)
    rg_sb = at("rg_sb", [P, KT, 2, P], offset=xn_at + 8 * KT * D)
    xrow = at("xrow", [P, NT // 3, D], offset=h_at)
    vrow = at("vrow", [NVEC, P], offset=h_at + 12 * D)
    brow = at("brow", [NADA, P], offset=h_at + 12 * D + 512)
    crow = at("crow", [NSEQ, D], offset=h_at + 12 * D + 1024)
    hrow = at("hrow", [32, D], offset=h_at + 16 * D + 1024)
    csil = at("csil", [NSEQ, D], offset=h_at + 20 * D + 1024)
    spw = at("spw", [P, 6, KT], offset=h_at + 24 * D + 1024)

    cursor[0] = region
    bsb = at("bsb", [P, KT, P])
    ws_hi = at("ws_hi", [P, 2, KT, P], F32R)
    ws_lo = at("ws_lo", [P, 2, KT, P], F32R)
    xr = at("xr", [P, HIST + SEQ + NS * (HIST + LS) + 1])
    xc_at = cursor[0]
    xc = at("xc", [P, TOK])
    m_at = cursor[0]
    merged = at("merged", [P, TOK])
    s_hi = at("s_hi", [P, TOK], F32R)
    s_lo = at("s_lo", [P, TOK], F32R)
    ws_raw = at("ws_raw", [P, KT, P], offset=xc_at)
    wd_raw = at("wd_raw", [P, KT, P], offset=m_at)
    v_at = cursor[0]
    gg = at("gg", [P, TOK])
    ug = at("ug", [P, TOK])
    ww = at("ww", [P, TOK])
    ii = at("ii", [P, TOK])
    qn = at("qn", [P, TOK])
    rt = at("rt", [P, TOK])
    v_in = at("v_in", [P, TOK])
    sig = at("sig", [P, NCH, CH])
    sb = at("sb", [P, 2, CH])
    end_mix = cursor[0]
    cursor[0] = v_at
    v_all = at("v_all", [P, NT, D])
    lng = at("lng", [P, D])
    lnb = at("lnb", [P, D])
    assert max(end_ffn, end_mix, cursor[0], h_at + 4 * KT * TOK) <= nc.sbuf_usable_end

    bank = [nc.alloc_psum_tensor(f"bank{i}", [P, 512], F32) for i in range(8)]

    x_dram = nc.dram_tensor("x_dram", [P, KT, TOK], F32).ap()
    vn_dram = nc.dram_tensor("vn_dram", [NT, P, D], F32).ap()
    merged_dram = nc.dram_tensor("merged_dram", [KT, P, TOK], F32).ap()
    rg_dram = nc.dram_tensor("rg_dram", [KT, P, 2 * P], F32).ap()

    def sem(name):
        return nc.alloc_semaphore(name)

    raw_loaded = [sem(f"raw_loaded{i}") for i in range(2)]
    ada_loaded = [sem(f"ada_loaded{i}") for i in range(2)]
    x_loaded = sem("x_loaded")
    rows_loaded = sem("rows_loaded")
    rg_loaded = sem("rg_loaded")
    rg_stored = sem("rg_stored")
    ws_loaded = sem("ws_loaded")
    spilled = sem("spilled")
    vn_stored = sem("vn_stored")
    v_loaded = sem("v_loaded")
    x_back = sem("x_back")
    merged_back = [sem(f"merged_back{k}") for k in range(KT)]
    y_stored = [sem(f"y_stored{i}") for i in range(2)]
    state_stored = sem("state_stored")
    rows_turned = sem("rows_turned")
    x_turned = sem("x_turned")
    ada_mm = sem("ada_mm")
    sumsq_mm = sem("sumsq_mm")
    gate_mm = sem("gate_mm")
    up_mm = sem("up_mm")
    down_mm = sem("down_mm")
    v_mm = sem("v_mm")
    ws_turned = sem("ws_turned")
    mix_mm = sem("mix_mm")
    s_mm = sem("s_mm")
    out_mm = sem("out_mm")
    y_turned = sem("y_turned")
    w_hi_ready = sem("w_hi_ready")
    c_silu = sem("c_silu")
    sp_exp = sem("sp_exp")
    squared = sem("squared")
    std_ready = sem("std_ready")
    xf_ready = sem("xf_ready")
    xn_hi_ready = sem("xn_hi_ready")
    silu_ready = sem("silu_ready")
    h_hi_ready = sem("h_hi_ready")
    act_evicted = sem("act_evicted")
    vstd_ready = sem("vstd_ready")
    ws_hi_ready = sem("ws_hi_ready")
    xc_hi_ready = sem("xc_hi_ready")
    vn_hi_ready = sem("vn_hi_ready")
    w_ready = sem("w_ready")
    root_ready = sem("root_ready")
    m_hi_ready = sem("m_hi_ready")
    yrow_act = sem("yrow_act")
    w_lo_ready = sem("w_lo_ready")
    rows_copied = sem("rows_copied")
    ada_ready = sem("ada_ready")
    sp_step = sem("sp_step")
    mod_step = sem("mod_step")
    x_written = sem("x_written")
    rstd_ready = sem("rstd_ready")
    t_ready = sem("t_ready")
    xs_step = sem("xs_step")
    xn_lo_ready = sem("xn_lo_ready")
    h_full = sem("h_full")
    h_lo_ready = sem("h_lo_ready")
    gated_tmp = sem("gated_tmp")
    v_step = sem("v_step")
    vn_ready = sem("vn_ready")
    ws_lo_ready = sem("ws_lo_ready")
    xr_free = sem("xr_free")
    conv_step = sem("conv_step")
    xc_lo_ready = sem("xc_lo_ready")
    vn_lo_ready = sem("vn_lo_ready")
    s_evicted = sem("s_evicted")
    s_applied = sem("s_applied")
    lru_step = sem("lru_step")
    gate_applied = sem("gate_applied")
    merge_step = sem("merge_step")
    merged_ready = sem("merged_ready")
    m_lo_ready = sem("m_lo_ready")
    yrow_dve = sem("yrow_dve")
    tail_ready = sem("tail_ready")
    const_ready = sem("const_ready")
    const_step = sem("const_step")
    rg_zeroed = sem("rg_zeroed")
    wd_zeroed = sem("wd_zeroed")
    ws_masked = sem("ws_masked")

    def samples(ap):
        return ap.rearrange("p (b l) -> p b l", b=NS)

    def per_sample(v, k):
        return ada[:, v * KT + k, 1:NSEQ].unsqueeze(2).broadcast_to([P, NS, LS])

    def prompt_scalar(v, k):
        return ada[:, v * KT + k, 0:1]

    def split_hi(act, n, par, slot):
        act.wait_ge(raw_loaded[par], raw_count(n, par))
        nc.scalar.activation(w_hi[:, slot, :], raw[:, par, :], ACT.Copy).then_inc(w_hi_ready, 1)

    def split_lo(dve, n, par, slot):
        dve.wait_ge(w_hi_ready, n + 1)
        nc.vector.tensor_tensor(w_lo[:, slot, :], raw[:, par, :], w_hi[:, slot, :].bitcast(F32),
                                ALU.subtract).then_inc(w_lo_ready, 1)

    def raw_count(n, par):
        if isinstance(n, int):
            return 16 * (n // 2 + 1)
        return n * 8 + (16 - 8 * par)

    def product(pe, out, hi, lo, mov_hi, mov_lo, first, last):
        nc.tensor.matmul(out, hi, mov_hi, start=first, stop=False, skip_group_check=True)
        nc.tensor.matmul(out, hi, mov_lo, start=False, stop=False, skip_group_check=True)
        return nc.tensor.matmul(out, lo, mov_hi, start=False, stop=last, skip_group_check=True)

    def ffn_written(total):
        return [total - KT * (NCH - 1 - c) for c in range(NCH)]

    def columns(w, col, width=P):
        return w.rearrange("(k p) n -> p k n", p=P)[:, :, ds(col, width)]

    def tile_rows(sp, t):
        if t > 0:
            sp.wait_ge(x_turned, 6 * t)
        for s in range(3):
            tile = 3 * t + s
            src = (ins["x_prompt"].rearrange("b s d -> (b s) d")[tile * P:(tile + 1) * P, :] if tile < NT - 1
                   else ins["x_sample"].rearrange("b s d -> (b s) d"))
            sp.dma_start(xrow[:, s, :], src).then_inc(x_loaded, 16)

    def xr_samples(t):
        return t[:, HIST + SEQ:HIST + SEQ + NS * (HIST + LS)].rearrange("p (b l) -> p b l", b=NS)

    def v_count(t, s):
        n, base = 0, 3 * NT + 1
        for u in range(NT + 2):
            if u < NT:
                n += 1
                if (u, 0) == (t, s):
                    return base + n
            if 1 <= u <= NT:
                n += 1
                if (u - 1, 1) == (t, s):
                    return base + n

    block = nc.Block()
    with block:

        @block.sync
        def _(sp):
            def unit(n, par, src, dst=None):
                if not isinstance(n, int) or n >= 2:
                    sp.wait_ge(w_lo_ready, n - 1)
                dst = raw[:, par, :] if dst is None else dst
                sp.dma_start(dst, src).then_inc(raw_loaded[par], 16)

            def wide(par):
                return raw[:, par, :].rearrange("p (k n) -> p k n", k=KT)

            for dst, src in ((vrow[V_G1:V_G1 + 8, :], ins["g_ffn1"].rearrange("o (k p) -> (o k) p", p=P)),
                             (vrow[V_GM:V_GM + 8, :], ins["g_mix"].rearrange("o (k p) -> (o k) p", p=P)),
                             (vrow[V_G2:V_G2 + 8, :], ins["g_ffn2"].rearrange("o (k p) -> (o k) p", p=P)),
                             (vrow[V_GF:V_GF + 8, :], ins["g_final"].rearrange("(k p) -> k p", p=P)),
                             (vrow[V_BCONV:V_BCONV + 8, :], ins["b_conv"].rearrange("o (k p) -> (o k) p", p=P)),
                             (vrow[V_WCONV:V_WCONV + 32, :], ins["w_conv"].rearrange("o w (k p) -> (o w k) p", p=P)),
                             (vrow[V_BA:V_BA + 8, :], ins["b_rg_a"].rearrange("o (k p) -> (o k) p", p=P)),
                             (vrow[V_BX:V_BX + 8, :], ins["b_rg_x"].rearrange("o (k p) -> (o k) p", p=P)),
                             (vrow[V_LAM:V_LAM + 8, :], ins["rg_lambda"].rearrange("o (k p) -> (o k) p", p=P)),
                             (brow[0:9 * KT, :], ins["b_ada"].rearrange("o (k p) -> (o k) p", p=P)),
                             (brow[9 * KT:NADA, :], ins["b_ada_final"].rearrange("(k p) -> k p", p=P)),
                             (crow[0:1, :], ins["c_prompt"]),
                             (crow[1:NSEQ, :], ins["c_sample"]),
                             (hrow[0:24, :], ins["cache_conv"].rearrange("o b w d -> (o b w) d")),
                             (hrow[24:32, :], ins["state_rglru"].rearrange("o b d -> (o b) d"))):
                sp.dma_start(dst, src).then_inc(rows_loaded, 16)
            w_ada = ins["w_ada"].rearrange("o k n -> (o k) n")
            for v in range(11):
                if v >= 2:
                    sp.wait_ge(ada_mm, v - 1)
                src = columns(w_ada, v * D, D) if v < 9 else columns(ins["w_ada_final"], (v - 9) * D, D)
                sp.dma_start(w_ada_sb[:, v % 2], src).then_inc(ada_loaded[v % 2], 16)
                if v == 0:
                    for t in range(3):
                        tile_rows(sp, t)
            sp.wait_ge(rg_loaded, 64)
            sp.dma_start(rg_dram.rearrange("k p n -> p k n"),
                         rg_sb[:, :, :, :].rearrange("p k g n -> p k (g n)")).then_inc(rg_stored, 16)

            def ffn_units(base, name):
                gate, up, down = (ins[f"w_{name}_{w}"].rearrange("o k n -> (o k) n") for w in ("gate", "up", "down"))

                def group(g):
                    n = base + g * 6
                    col = g * (2 * P)
                    for f in range(2):
                        unit(n + 2 * f, 0, columns(gate, col + f * P), wide(0))
                        unit(n + 2 * f + 1, 1, columns(up, col + f * P), wide(1))
                    for f in range(2):
                        unit(n + 4 + f, f, down[ds(col + f * P, P), :])
                if base == 0:
                    group(0)
                with sp.Fori(1 if base == 0 else 0, GROUPS) as g:
                    group(g)

            ffn_units(U_FFN1, "ffn1")

            w_in = ins["w_in"].rearrange("o k n -> (o k) n")
            w_v = w_in.rearrange("(k p) n -> p k n", p=P)
            for q in range(8):
                half, kp = divmod(q, 4)
                unit(U_V + q, q % 2, w_v[:, 2 * kp:2 * kp + 2, 3 * D + half * HALF:3 * D + (half + 1) * HALF],
                     raw[:, q % 2, :].rearrange("p (k n) -> p k n", k=2))
                if q == 5:
                    sp.wait_ge(x_written, XW_FFN1)
                    sp.dma_start(x_dram, x[:, :, :]).then_inc(spilled, 16)
                    sp.wait_ge(t_ready, 2 * NCH * KT)
                    sp.wait_ge(squared, 2 * NCH * KT)
                    sp.wait_ge(xn_lo_ready, 2 * NCH * KT)
                    sp.wait_ge(spilled, 16)
                    sp.dma_start(lng[:, :], ins["ln_v_g"].broadcast_to([P, D])).then_inc(ws_loaded, 16)
                    sp.dma_start(lnb[:, :], ins["ln_v_b"].broadcast_to([P, D])).then_inc(ws_loaded, 16)
                    sp.dma_start(bsb[:, :, :].rearrange("p h t -> p (h t)"),
                                 ins["b_spatial"].rearrange("o h t -> o (h t)").broadcast_to([P, D]))\
                      .then_inc(ws_loaded, 16)
                    sp.dma_start(ws_raw[:, :, :], ins["w_spatial"].rearrange("o h t s -> t (o h) s"))\
                      .then_inc(ws_loaded, 16)
                    sp.wait_ge(wd_zeroed, 1)
                    for b in range(NS):
                        sp.dma_start(wd_raw[b * LS:(b + 1) * LS, :, b * LS:(b + 1) * LS],
                                     ins["w_spatial"].rearrange("o h t s -> t (o h) s")[0:LS, :, 0:LS])\
                          .then_inc(ws_loaded, 16)

            def mix_units(j):
                n = U_MIX + j * 6
                for q, sec in ((0, 0), (1, 1), (2, 2)):
                    unit(n + q, q % 2, columns(w_in, sec * D + j * P), wide(q % 2))
                if not isinstance(j, int) or j > 0:
                    sp.wait_ge(vn_lo_ready, j)
                sp.dma_start(v_in[:, :].rearrange("p (t c) -> p t c", t=NT),
                             vn_dram.rearrange("t p n -> p t n")[:, :, ds(j * P, P)]).then_inc(v_loaded, 16)
                unit(n + 3, 1, rg_dram.rearrange("k p n -> (k p) n")[ds(j * P, P), :], raw[:, 1, 0:2 * P])
                for q, sec in ((4, 4), (5, 5)):
                    unit(n + q, q % 2, columns(w_in, sec * D + j * P), wide(q % 2))

            def store_merged(j):
                sp.wait_ge(merged_ready, j + 1)
                sp.dma_start(merged_dram.rearrange("k p n -> (k p) n")[ds(j * P, P), :],
                             merged[:, :]).then_inc(spilled, 16)

            n = U_MIX
            for q, sec in ((0, 0), (1, 1), (2, 2)):
                unit(n + q, q % 2, columns(w_in, sec * D), wide(q % 2))
            sp.wait_ge(rg_stored, 16)
            unit(n + 3, 1, rg_dram[0], raw[:, 1, 0:2 * P])
            unit(n + 4, 0, columns(w_in, 4 * D), wide(0))
            unit(n + 5, 1, columns(w_in, 5 * D), wide(1))
            for t in range(NT):
                sp.wait_ge(vn_ready, t + 1)
                sp.dma_start(vn_dram[t], v_all[:, t, :]).then_inc(vn_stored, 16)
            sp.dma_start(outs["sgu_v_prompt"].rearrange("o b s d -> (o b s) d"), v_all[:, NT - 2, :])\
              .then_inc(vn_stored, 16)
            sp.dma_start(outs["sgu_v_sample"].rearrange("o b s d -> (o b s) d"), v_all[:, NT - 1, :])\
              .then_inc(vn_stored, 16)
            sp.wait_ge(vn_stored, 16 * (NT + 2))
            sp.dma_start(v_in[:, :].rearrange("p (t c) -> p t c", t=NT),
                         vn_dram.rearrange("t p n -> p t n")[:, :, 0:P]).then_inc(v_loaded, 16)
            mix_units(1)
            with sp.Fori(2, KT) as j:
                store_merged(j - 2)
                mix_units(j)
            store_merged(KT - 2)
            for q in range(RING):
                unit(U_OUT + q, q % 2, columns(ins["w_out"].rearrange("o k n -> (o k) n"), q * P), wide(q % 2))
            store_merged(KT - 1)
            sp.wait_ge(spilled, 16 * (1 + KT))
            for k in range(KT):
                sp.dma_start(merged_in[:, k, :], merged_dram[k]).then_inc(merged_back[k], 16)
            sp.dma_start(x[:, :, :], x_dram).then_inc(x_back, 16)
            for q in range(RING, KT):
                unit(U_OUT + q, q % 2, columns(ins["w_out"].rearrange("o k n -> (o k) n"), q * P), wide(q % 2))
            ffn_units(U_FFN2, "ffn2")
            sp.wait_ge(tail_ready, 2)
            sp.dma_start(outs["rglru_prompt"].rearrange("o b d -> (o b) d"), tailrow[0:1, :]).then_inc(state_stored, 16)
            sp.dma_start(outs["rglru_sample"].rearrange("o b d -> (o b) d"), tailrow[1:NSEQ, :]).then_inc(state_stored, 16)
            sp.dma_start(outs["conv_prompt"].rearrange("o b w d -> (o b w) d"), tailrow[NSEQ:NSEQ + HIST, :])\
              .then_inc(state_stored, 16)
            sp.dma_start(outs["conv_sample"].rearrange("o b w d -> (o b w) d"), tailrow[NSEQ + HIST:TAIL, :])\
              .then_inc(state_stored, 16)
            for t in range(NT):
                sp.wait_ge(yrow_act, t + 1)
                sp.wait_ge(yrow_dve, t + 1)
                dst = (outs["y_prompt"].rearrange("b s d -> (b s) d")[t * P:(t + 1) * P, :] if t < NT - 1
                       else outs["y_sample"].rearrange("b s d -> (b s) d"))
                sp.dma_start(dst, yrow[:, t % 2, :]).then_inc(y_stored[t % 2], 16)
            sp.wait_ge(state_stored, 16 * 4)
            sp.wait_ge(y_stored[0], 16 * ((NT + 1) // 2))
            sp.wait_ge(y_stored[1], 16 * (NT // 2))

        @block.gpsimd
        def _(pool):
            nc.gpsimd.memset(ident[:, :], 0.0).then_inc(const_step, 1)
            nc.gpsimd.memset(ones[:, :], 1.0).then_inc(const_step, 1)
            nc.gpsimd.memset(epst[:, 0:1], EPS).then_inc(const_step, 1)
            pool.wait_ge(const_step, 3)
            nc.gpsimd.affine_select(out=ident[:, :], in_=ident[:, :], compare_op=ALU.not_equal, fill=1.0,
                                    base=0, pattern=[[-1, P]], channel_multiplier=1).then_inc(const_ready, 1)
            nc.gpsimd.memset(rg_sb[:, :, :, :], 0.0).then_inc(rg_zeroed, 1)
            pool.wait_ge(xn_lo_ready, 2 * NCH * KT)
            pool.wait_ge(spilled, 16)
            nc.gpsimd.memset(wd_raw[:, :, :], 0.0).then_inc(wd_zeroed, 1)
            pool.wait_ge(ws_loaded, 16 * (4 + NS))
            for w in (ws_raw, wd_raw):
                nc.gpsimd.affine_select(out=w[:, :, :], in_=w[:, :, :], compare_op=ALU.is_ge, fill=0.0,
                                        base=0, pattern=[[0, KT], [-1, P]], channel_multiplier=1)\
                  .then_inc(ws_masked, 1)

        @block.scalar
        def _(act):
            act.wait_ge(rg_zeroed, 1)
            for g, name in enumerate(("w_rg_a", "w_rg_x")):
                for h in range(2):
                    src = ins[name].rearrange("o (k h) i j -> h i (o k) j", h=2)[h]
                    act.dma_start(rg_sb[64 * h:64 * h + 64, :, g, 64 * h:64 * h + 64], src).then_inc(rg_loaded, 16)
            act.wait_ge(rows_loaded, 16 * 15)
            nc.scalar.activation(csil[:, :], crow[:, :], ACT.Silu).then_inc(c_silu, 1)
            act.wait_ge(sp_step, 1)
            nc.scalar.activation(spw[:, 1, :], spw[:, 0, :], ACT.Exp, scale=-1.0).then_inc(sp_exp, 1)
            for n in range(RING):
                split_hi(act, n, n % 2, n % RING)

            def norm(i, v_shift, v_scale, written, final=False):
                act.wait_ge(const_ready, 1)
                for c in range(NCH):
                    act.wait_ge(x_written, written[c])
                    cols = slice(c * CH, (c + 1) * CH)
                    n0 = (i * NCH + c) * KT
                    for k in range(KT):
                        n = n0 + k
                        if n >= 2:
                            act.wait_ge(sumsq_mm, n - 1)
                        nc.scalar.activation(sq[:, k % 2, :], x[:, k, cols], ACT.Square).then_inc(squared, 1)
                    act.wait_ge(sumsq_mm, n0 + KT)
                    if i * NCH + c >= 2:
                        act.wait_ge(t_ready, n0 - KT)
                    nc.scalar.activation(std[:, c % 2, :], bank[6 + c % 2][:, 0:CH], ACT.Sqrt,
                                         scale=1.0 / D, bias=epst[:, 0:1]).then_inc(std_ready, 1)
                    if final and c > 0:
                        act.wait_ge(y_turned, 6 * c)
                    width = CH if c < NCH - 1 else PC2
                    for k in range(KT):
                        n = n0 + k
                        act.wait_ge(t_ready, n + 1)
                        dst = yT[:, k, 0:width] if final else xfull[:, k % 2, 0:width]
                        nc.scalar.activation(dst, tbuf[:, k % 2, 0:width], ACT.Identity,
                                             scale=prompt_scalar(v_scale, k), bias=prompt_scalar(v_shift, k))\
                          .then_inc(xf_ready, 1)
                        if not final:
                            act.wait_ge(xf_ready, n + 1)
                            if c == NCH - 1:
                                act.wait_ge(xs_step, (i * KT + k + 1) * 2)
                            nc.scalar.activation(xn_hi[:, k, cols], xfull[:, k % 2, :], ACT.Copy)\
                              .then_inc(xn_hi_ready, 1)
                    if final:
                        out_rows(c)

            def out_rows(c):
                for s in range(NCH):
                    t = NCH * c + s
                    act.wait_ge(y_turned, 2 * t + 1)
                    if t >= 2:
                        act.wait_ge(y_stored[t % 2], 16 * (t // 2))
                    nc.scalar.activation(yrow[:, t % 2, 0:HALF], bank[(2 * t) % RING][:, :], ACT.Copy)\
                      .then_inc(yrow_act, 1)

            def ffn(base, h0, last):
                def group(g, ahead=True):
                    def silus(q):
                        act.wait_ge(gate_mm, g * 6 + (h0 + q + 1))
                        nc.scalar.activation(silu[:, q % 2, :], bank[q % 3][:, 0:CH], ACT.Silu)\
                          .then_inc(silu_ready, 1)

                    def high(q):
                        f, c = divmod(q, NCH)
                        act.wait_ge(h_full, g * 6 + (h0 + q + 1))
                        nc.scalar.activation(h_hi[:, f, c * CH:(c + 1) * CH], hfull[:, q % 2, :], ACT.Copy)\
                          .then_inc(h_hi_ready, 1)

                    def ahead_units(*qs):
                        if ahead:
                            for q in qs:
                                split_hi(act, g * 6 + (base + RING + q), q % 2, (base + q) % RING)
                    for q in range(6):
                        silus(q)
                        if q > 0:
                            high(q - 1)
                        if q == 3:
                            ahead_units(0, 1)
                    high(5)
                    ahead_units(2, 3)
                    act.wait_ge(down_mm, g * 24 + (h0 * 4 + 24))
                    ahead_units(4, 5)
                with act.Fori(0, GROUPS - last) as g:
                    group(g)
                if last:
                    group(GROUPS - 1, ahead=False)

            norm(0, SHIFT1, SCALE1, (XW_IN,) * NCH)
            ffn(U_FFN1, 0, 0)
            norm(1, SHIFTM, SCALEM, ffn_written(XW_FFN1))
            act.wait_ge(spilled, 16)
            act.wait_ge(xn_lo_ready, 2 * NCH * KT)
            for half in range(2):
                for t in range(NT):
                    m = half * NT + t
                    act.wait_ge(v_mm, m + 1)
                    nc.scalar.activation(v_all[:, t, half * HALF:(half + 1) * HALF], bank[m % RING][:, :],
                                         ACT.Gelu_apprx_tanh).then_inc(act_evicted, 1)
                for n in range(U_V + 6 + 4 * half, U_V + 10 + 4 * half):
                    split_hi(act, n, n % 2, n % RING)
                if half == 0:
                    for w in range(2):
                        for b in range(2):
                            act.wait_ge(ws_turned, 2 * w + b + 1)
                            nc.scalar.activation(
                                ws_hi[:, w, 4 * b:4 * b + 4, :].rearrange("p h t -> p (h t)"),
                                bank[6 + b][:, :], ACT.Copy).then_inc(ws_hi_ready, 1)
            act.wait_ge(v_step, NT * 2 + NT)
            nc.scalar.activation(vstd[:, 0:NT], mv[:, :, 1], ACT.Sqrt, bias=epst[:, 0:1]).then_inc(vstd_ready, 1)
            act.wait_ge(vn_stored, 16 * (NT + 2))

            def mix(j):
                def evicts(m, dst, src_bank, func, **kw):
                    return nc.scalar.activation(dst, src_bank, func, **kw).then_inc(act_evicted, 1)

                def section(first, count):
                    act.wait_ge(mix_mm, j * 21 + (first + count))

                def ahead_unit(q):
                    n = j * 6 + (U_MIX + RING + q)
                    split_hi(act, n, q % 2, (U_MIX + q) % RING)

                act.wait_ge(xr_free, j + 2)
                for c in range(NCH):
                    section(c, 1)
                    if c < NCH - 1:
                        evicts(c, xr[:, HIST + c * CH:HIST + (c + 1) * CH], bank[c][:, 0:CH], ACT.Copy)
                    else:
                        nc.scalar.activation(xr[:, HIST + c * CH:HIST + SEQ], bank[c][:, 0:PC2], ACT.Copy)
                        evicts(c, xr_samples(xr)[:, :, HIST:HIST + LS], samples(bank[c][:, PC2:CH]), ACT.Copy)
                ahead_unit(0)
                section(3, 1)
                evicts(3, gg[:, 0:CH], bank[3][:, 0:CH], ACT.Gelu_apprx_tanh)
                act.wait_ge(conv_step, j * 8 + 8)
                nc.scalar.activation(s_hi[:, :], xc[:, :], ACT.Copy).then_inc(xc_hi_ready, 1)
                for c in (1, 2):
                    section(3 + c, 1)
                    evicts(3 + c, gg[:, c * CH:(c + 1) * CH], bank[3 + c][:, 0:CH], ACT.Gelu_apprx_tanh)
                ahead_unit(1)
                for c in range(NCH):
                    section(6 + c, 1)
                    evicts(6 + c, ug[:, c * CH:(c + 1) * CH], bank[c][:, 0:CH], ACT.Gelu_apprx_tanh)
                ahead_unit(2)
                for c in range(NCH):
                    cols = slice(c * CH, (c + 1) * CH)
                    section(9 + 2 * c, 1)
                    evicts(9, ww[:, cols], bank[(9 + 2 * c) % RING][:, 0:CH], ACT.Sigmoid,
                           bias=blk[:, 0:1])
                    section(10 + 2 * c, 1)
                    evicts(10, ii[:, cols], bank[(10 + 2 * c) % RING][:, 0:CH], ACT.Sigmoid,
                           bias=blk[:, 1:2])
                act.wait_ge(v_loaded, j * 16 + 16)
                nc.scalar.activation(s_hi[:, :], v_in[:, :], ACT.Copy).then_inc(vn_hi_ready, 1)
                act.wait_ge(act_evicted, j * 21 + (2 * NT + 15))
                nc.scalar.activation(ww[:, :], ww[:, :], ACT.Tanh, scale=blk[:, 2:3]).then_inc(w_ready, 1)
                act.wait_ge(w_ready, j + 1)
                nc.scalar.activation(rt[:, :], ww[:, :], ACT.Sqrt, scale=4.0).then_inc(root_ready, 1)
                ahead_unit(3)
                for s in range(2):
                    for c in range(NCH):
                        section(15 + 3 * s + c, 1)
                        if s == 1:
                            act.wait_ge(gate_applied, j * 6 + (c + 1))
                        evicts(18 + 3 * s + c, sig[:, c, :], bank[3 * s + c][:, 0:CH], ACT.Sigmoid)
                    ahead_unit(4 + s)
            with act.Fori(0, KT) as j:
                mix(j)

            for k in range(KT):
                act.wait_ge(merged_back[k], 16)
                nc.scalar.activation(xn_hi[:, k, :], merged_in[:, k, :], ACT.Copy).then_inc(m_hi_ready, 1)
            for p in range(KT // 2):
                act.wait_ge(out_mm, p + 1)
                for n in (U_OUT + 2 * p + 6, U_OUT + 2 * p + 7):
                    split_hi(act, n, n % 2, n % RING)
            norm(2, SHIFT2, SCALE2, (XW_OUT,) * NCH)
            ffn(U_FFN2, 6 * GROUPS, 1)
            norm(3, SHIFTF, SCALEF, ffn_written(XW_FFN2), final=True)

        @block.vector
        def _(dve):
            dve.wait_ge(rows_turned, 1)
            nc.vector.tensor_copy(vecT[:, :], bank[6][:, 0:NVEC])
            nc.vector.tensor_copy(badaT[:, :], bank[6][:, 128:128 + NADA])
            nc.vector.tensor_copy(histT[:, :, :], bank[7][:, 256:512].rearrange("p (k n) -> p k n", k=KT))
            nc.vector.tensor_copy(cT[:, :, 0:NSEQ],
                                  bank[7][:, 0:KT * NSEQ].rearrange("p (k n) -> p k n", k=KT))\
              .then_inc(rows_copied, 1)
            dve.wait_ge(rows_copied, 1)
            lam = vecT[:, V_LAM:V_LAM + KT]
            steps = [0]

            def step(ins_):
                steps[0] += 1
                ins_.then_inc(sp_step, 1)

            def after():
                dve.wait_ge(sp_step, steps[0])
            nc.vector.tensor_scalar(spw[:, 5, :], lam, -1.0, 0.0, ALU.mult, ALU.max)
            step(nc.vector.scalar_tensor_tensor(spw[:, 0, :], lam, -1.0, lam, ALU.mult, ALU.max))
            dve.wait_ge(sp_exp, 1)
            step(nc.vector.tensor_scalar(spw[:, 2, :], spw[:, 1, :], 2.0, None, ALU.add))
            after()
            step(nc.vector.reciprocal(spw[:, 3, :], spw[:, 2, :]))
            after()
            step(nc.vector.tensor_tensor(spw[:, 0, :], spw[:, 1, :], spw[:, 3, :], ALU.mult))
            after()
            step(nc.vector.tensor_tensor(spw[:, 1, :], spw[:, 0, :], spw[:, 0, :], ALU.mult))
            after()
            step(nc.vector.tensor_scalar(spw[:, 2, :], spw[:, 1, :], 1.0 / 17, 1.0 / 15, ALU.mult, ALU.add))
            for d in (13, 11, 9, 7, 5, 3, 1):
                after()
                step(nc.vector.tensor_tensor(spw[:, 3, :], spw[:, 2, :], spw[:, 1, :], ALU.mult))
                after()
                step(nc.vector.tensor_scalar(spw[:, 2, :], spw[:, 3, :], 1.0 / d, None, ALU.add))
            after()
            step(nc.vector.scalar_tensor_tensor(spw[:, 3, :], spw[:, 2, :], 2.0, spw[:, 0, :], ALU.mult, ALU.mult))
            after()
            step(nc.vector.tensor_tensor(spw[:, 4, :], spw[:, 3, :], spw[:, 5, :], ALU.add))
            after()
            step(nc.vector.tensor_scalar(lam, spw[:, 4, :], 4.0, None, ALU.mult))

            def x_in(t):
                for s in range(3):
                    for b in range(2):
                        dve.wait_ge(x_turned, 6 * t + 2 * s + b + 1)
                        tile = 3 * t + s
                        nc.vector.tensor_copy(
                            x[:, 4 * b:4 * b + 4, tile * P:(tile + 1) * P],
                            bank[2 * s + b][:, :].rearrange("p (k n) -> p k n", k=4)).then_inc(x_written, 1)
            for t in range(3):
                x_in(t)
            for v in range(11):
                dve.wait_ge(ada_mm, v + 1)
                nc.vector.tensor_tensor(
                    ada[:, v * KT:(v + 1) * KT, :],
                    bank[6 + v % 2][:, 0:KT * NSEQ].rearrange("p (k n) -> p k n", k=KT),
                    badaT[:, v * KT:(v + 1) * KT].unsqueeze(2).broadcast_to([P, KT, NSEQ]), ALU.add)\
                  .then_inc(ada_ready, 1)
            dve.wait_ge(ada_ready, 11)
            for v, gain in ((SCALE1, V_G1), (SCALEM, V_GM), (SCALE2, V_G2), (SCALEF, V_GF)):
                a = ada[:, v * KT:(v + 1) * KT, :]
                nc.vector.scalar_tensor_tensor(
                    a, a, 1.0, vecT[:, gain:gain + KT].unsqueeze(2).broadcast_to([P, KT, NSEQ]), ALU.add, ALU.mult)\
                  .then_inc(mod_step, 1)
            for v in (GATE1, GATE2):
                a = ada[:, v * KT:(v + 1) * KT, :]
                nc.vector.tensor_scalar(a, a, 0.5, None, ALU.mult).then_inc(mod_step, 1)
            for n in range(RING):
                split_lo(dve, n, n % 2, n % RING)
            dve.wait_ge(mod_step, 6)

            def norm(i, v_shift, v_scale, final=False):
                def low(c, k):
                    n = (i * NCH + c) * KT + k
                    cols = slice(c * CH, (c + 1) * CH)
                    dve.wait_ge(xn_hi_ready, n + 1)
                    nc.vector.tensor_tensor(xn_lo[:, k, cols], xfull[:, k % 2, :],
                                            xn_hi[:, k, cols].bitcast(F32), ALU.subtract).then_inc(xn_lo_ready, 1)
                for c in range(NCH):
                    cols = slice(c * CH, (c + 1) * CH)
                    dve.wait_ge(std_ready, i * NCH + c + 1)
                    nc.vector.reciprocal(std[:, c % 2, :], std[:, c % 2, :]).then_inc(rstd_ready, 1)
                    dve.wait_ge(rstd_ready, i * NCH + c + 1)
                    for k in range(KT):
                        n = (i * NCH + c) * KT + k
                        if final and n >= 2:
                            dve.wait_ge(xf_ready, n - 1)
                        nc.vector.tensor_tensor(tbuf[:, k % 2, :], x[:, k, cols], std[:, c % 2, :], ALU.mult)\
                          .then_inc(t_ready, 1)
                        if c == NCH - 1:
                            s0 = (i * KT + k) * 2
                            dve.wait_ge(t_ready, n + 1)
                            ts = samples(tbuf[:, k % 2, PC2:CH])
                            nc.vector.tensor_tensor(ts, ts, per_sample(v_scale, k), ALU.mult).then_inc(xs_step, 1)
                            dve.wait_ge(xs_step, s0 + 1)
                            dst = yT[:, k, PC2:CH] if final else xfull[:, k % 2, PC2:CH]
                            nc.vector.tensor_tensor(samples(dst), ts, per_sample(v_shift, k), ALU.add)\
                              .then_inc(xs_step, 1)
                        if not final and k > 0:
                            low(c, k - 1)
                    if not final:
                        low(c, KT - 1)
                    else:
                        out_rows(c)

            def out_rows(c):
                for s in range(NCH):
                    t = NCH * c + s
                    dve.wait_ge(y_turned, 2 * t + 2)
                    if t >= 2:
                        dve.wait_ge(y_stored[t % 2], 16 * (t // 2))
                    nc.vector.tensor_copy(yrow[:, t % 2, HALF:D], bank[(2 * t + 1) % RING][:, :])\
                      .then_inc(yrow_dve, 1)

            tmps = [0]

            def add_gated(ps, v, o, c, tmp_count, tmp_slot):
                if c < NCH - 1:
                    cols = slice(c * CH, (c + 1) * CH)
                    nc.vector.scalar_tensor_tensor(x[:, o, cols], ps[:, 0:CH], prompt_scalar(v, o), x[:, o, cols],
                                                   ALU.mult, ALU.add).then_inc(x_written, 1)
                    return
                nc.vector.tensor_tensor(samples(gtmp[:, tmp_slot, :]), samples(ps[:, PC2:CH]), per_sample(v, o),
                                        ALU.mult).then_inc(gated_tmp, 1)
                nc.vector.scalar_tensor_tensor(x[:, o, c * CH:SEQ], ps[:, 0:PC2], prompt_scalar(v, o),
                                               x[:, o, c * CH:SEQ], ALU.mult, ALU.add)
                dve.wait_ge(gated_tmp, tmp_count)
                nc.vector.tensor_tensor(x[:, o, SEQ:TOK], x[:, o, SEQ:TOK], gtmp[:, tmp_slot, :], ALU.add)\
                  .then_inc(x_written, 1)

            def ffn(base, h0, xw0, tmp0, v_gate, last):
                def group(g, ahead=True):
                    def full(q):
                        dve.wait_ge(up_mm, g * 6 + (h0 + q + 1))
                        dve.wait_ge(silu_ready, g * 6 + (h0 + q + 1))
                        if q >= 2:
                            dve.wait_ge(h_lo_ready, g * 6 + (h0 + q - 1))
                        nc.vector.tensor_tensor(hfull[:, q % 2, :], silu[:, q % 2, :], bank[3 + q % 3][:, 0:CH],
                                                ALU.mult).then_inc(h_full, 1)

                    def low(q):
                        f, c = divmod(q, NCH)
                        dve.wait_ge(h_hi_ready, g * 6 + (h0 + q + 1))
                        cols = slice(c * CH, (c + 1) * CH)
                        nc.vector.tensor_tensor(h_lo[:, f, cols], hfull[:, q % 2, :],
                                                h_hi[:, f, cols].bitcast(F32), ALU.subtract)\
                          .then_inc(h_lo_ready, 1)

                    def ahead_units(*qs):
                        if ahead:
                            for q in qs:
                                split_lo(dve, g * 6 + (base + RING + q), q % 2, (base + q) % RING)
                    for q in range(6):
                        full(q)
                        if q > 0:
                            low(q - 1)
                        if q == 3:
                            ahead_units(0, 1)
                    low(5)
                    dve.wait_ge(h_lo_ready, g * 6 + (h0 + 6))
                    dve.wait_ge(x_written, g * 24 + xw0)
                    for c in range(NCH):
                        for o in range(KT):
                            m = c * KT + o
                            dve.wait_ge(down_mm, g * 24 + (h0 * 4 + m + 1))
                            add_gated(bank[m % RING], v_gate, o, c, g * KT + (tmp0 + o + 1), o % 2)
                        if c == 0:
                            ahead_units(2, 3)
                    ahead_units(4, 5)
                with dve.Fori(0, GROUPS - last) as g:
                    group(g)
                if last:
                    group(GROUPS - 1, ahead=False)
                dve.wait_ge(x_written, xw0 + 24 * GROUPS)

            dve.wait_ge(x_written, XW_IN)
            norm(0, SHIFT1, SCALE1)
            ffn(U_FFN1, 0, XW_IN, 0, GATE1, 0)
            norm(1, SHIFTM, SCALEM)

            for half in range(2):
                for t in range(NT):
                    dve.wait_ge(act_evicted, half * NT + t + 1)
                    nc.vector.bn_stats(bnst[:, t, half, :], v_all[:, t, half * HALF:(half + 1) * HALF])\
                      .then_inc(v_step, 1)
                for n in range(U_V + 6 + 4 * half, U_V + 10 + 4 * half):
                    split_lo(dve, n, n % 2, n % RING)
                if half == 0:
                    for w in range(2):
                        for b in range(2):
                            dve.wait_ge(ws_hi_ready, 2 * w + b + 1)
                            nc.vector.tensor_tensor(
                                ws_lo[:, w, 4 * b:4 * b + 4, :].rearrange("p h t -> p (h t)"), bank[6 + b][:, :],
                                ws_hi[:, w, 4 * b:4 * b + 4, :].rearrange("p h t -> p (h t)").bitcast(F32),
                                ALU.subtract).then_inc(ws_lo_ready, 1)
            dve.wait_ge(v_step, 2 * NT)
            for t in range(NT):
                nc.vector.bn_aggr(mv[:, t, :], bnst[:, t, :, :]).then_inc(v_step, 1)
            dve.wait_ge(vstd_ready, 1)
            nc.vector.reciprocal(vstd[:, 0:NT], vstd[:, 0:NT]).then_inc(v_step, 1)
            dve.wait_ge(v_step, 3 * NT + 1)
            dve.wait_ge(ws_loaded, 16 * (4 + NS))
            for t in range(NT + 2):
                if t < NT:
                    nc.vector.tensor_scalar(v_all[:, t, :], v_all[:, t, :], mv[:, t, 0:1], vstd[:, t:t + 1],
                                            ALU.subtract, ALU.mult).then_inc(v_step, 1)
                if 1 <= t <= NT:
                    dve.wait_ge(v_step, v_count(t - 1, 0))
                    nc.vector.tensor_tensor(v_all[:, t - 1, :], v_all[:, t - 1, :], lng[:, :], ALU.mult)\
                      .then_inc(v_step, 1)
                if t >= 2:
                    dve.wait_ge(v_step, v_count(t - 2, 1))
                    nc.vector.tensor_tensor(v_all[:, t - 2, :], v_all[:, t - 2, :], lnb[:, :], ALU.add)\
                      .then_inc(vn_ready, 1)
            nc.vector.memset(xr[:, 0:HIST], 0.0).then_inc(xr_free, 1)

            def mix(j):
                def ahead_unit(q):
                    split_lo(dve, j * 6 + (U_MIX + RING + q), q % 2, (U_MIX + q) % RING)
                xs = xr_samples(xr)
                nc.vector.tensor_copy(blk[:, :], vecT[:, V_BA:V_BA + 3 * KT].rearrange(
                    "p (v k) -> p v k", k=KT)[:, :, ds(j, 1)].rearrange("p v o -> p (v o)"))
                nc.vector.tensor_copy(xs[:, :, 0:HIST],
                                      histT[:, ds(j, 1), 0:NS * HIST].rearrange("p o (b w) -> p (o b) w", b=NS))\
                  .then_inc(xr_free, 1)
                dve.wait_ge(act_evicted, j * 21 + (2 * NT + NCH))
                dve.wait_ge(xr_free, j + 2)
                for w in range(TAPS):
                    tap = vecT[:, ds(j + (V_WCONV + w * KT), 1)]
                    if w > 0:
                        dve.wait_ge(conv_step, j * 8 + 2 * w)
                    pairs = ((xc[:, 0:SEQ], xr[:, w:w + SEQ]), (samples(xc[:, SEQ:TOK]), xs[:, :, w:w + LS]))
                    for dst, src in pairs:
                        if w == 0:
                            nc.vector.tensor_scalar(dst, src, tap, vecT[:, ds(j + V_BCONV, 1)],
                                                    ALU.mult, ALU.add).then_inc(conv_step, 1)
                        else:
                            nc.vector.scalar_tensor_tensor(dst, src, tap, dst, ALU.mult, ALU.add)\
                              .then_inc(conv_step, 1)
                tail = tails[:, ds(j, 1), :].rearrange("p o n -> p (o n)")
                nc.vector.tensor_copy(tail[:, NSEQ:NSEQ + HIST], xr[:, SEQ:SEQ + HIST])
                nc.vector.tensor_copy(tail[:, NSEQ + HIST:TAIL].rearrange("p (b w) -> p b w", b=NS),
                                      xs[:, :, LS:LS + HIST])
                ahead_unit(0)
                dve.wait_ge(xc_hi_ready, j + 1)
                nc.vector.tensor_tensor(s_lo[:, :], xc[:, :], s_hi[:, :].bitcast(F32), ALU.subtract)\
                  .then_inc(xc_lo_ready, 1)
                ahead_unit(1)
                ahead_unit(2)
                dve.wait_ge(vn_hi_ready, j + 1)
                nc.vector.tensor_tensor(s_lo[:, :], v_in[:, :], s_hi[:, :].bitcast(F32), ALU.subtract)\
                  .then_inc(vn_lo_ready, 1)
                dve.wait_ge(w_ready, j + 1)
                nc.vector.tensor_scalar(qn[:, :], ww[:, :], 1.0, -1.0, ALU.add, ALU.mult).then_inc(lru_step, 1)
                bias = bsb[:, ds(j, 1), :]
                for c in range(NCH):
                    dve.wait_ge(s_mm, j * NCH + (c + 1))
                    tiles = 3 if c < NCH - 1 else 2
                    n = tiles * P
                    ins_ = nc.vector.tensor_tensor(
                        sb[:, c % 2, 0:n].rearrange("p (t l) -> p t l", t=tiles),
                        bank[(15 + c) % RING][:, 0:n].rearrange("p (t l) -> p t l", t=tiles),
                        bias.broadcast_to([P, tiles, P]), ALU.add)
                    if c == NCH - 1:
                        ins_ = nc.vector.tensor_tensor(samples(sb[:, c % 2, n:CH]),
                                                       samples(bank[(15 + c) % RING][:, n:CH]),
                                                       bias[:, :, 0:LS].broadcast_to([P, NS, LS]), ALU.add)
                    ins_.then_inc(s_evicted, 1)
                    dve.wait_ge(s_evicted, j * NCH + (c + 1))
                    cols = slice(c * CH, (c + 1) * CH)
                    nc.vector.tensor_tensor(ug[:, cols], ug[:, cols], sb[:, c % 2, :], ALU.mult).then_inc(s_applied, 1)
                L = lambda k: dve.wait_ge(lru_step, j * 9 + k)
                L(1)
                nc.vector.reciprocal(qn[:, :], qn[:, :]).then_inc(lru_step, 1)
                nc.vector.tensor_tensor(ii[:, :], ii[:, :], xc[:, :], ALU.mult).then_inc(lru_step, 1)
                dve.wait_ge(root_ready, j + 1)
                L(2)
                nc.vector.scalar_tensor_tensor(rt[:, :], rt[:, :], -1.0, qn[:, :], ALU.mult, ALU.mult)\
                  .then_inc(lru_step, 1)
                nc.vector.scalar_tensor_tensor(ww[:, :], ww[:, :], 1.0, qn[:, :], ALU.subtract, ALU.mult)\
                  .then_inc(lru_step, 1)
                L(4)
                nc.vector.tensor_tensor(ii[:, :], ii[:, :], rt[:, :], ALU.mult).then_inc(lru_step, 1)
                L(6)
                nc.vector.tensor_tensor_scan(qn[:, 0:SEQ], ww[:, 0:SEQ], ii[:, 0:SEQ], 0.0, ALU.mult, ALU.add)\
                  .then_inc(lru_step, 1)
                for b in range(NS):
                    cols = slice(SEQ + b * LS, SEQ + (b + 1) * LS)
                    ins_ = nc.vector.tensor_tensor_scan(
                        qn[:, cols], ww[:, cols], ii[:, cols],
                        histT[:, ds(j, 1), NS * HIST + b:NS * HIST + b + 1].rearrange("p o n -> p (o n)"),
                        ALU.mult, ALU.add)
                ins_.then_inc(lru_step, 1)
                L(8)
                nc.vector.tensor_copy(tail[:, 0:1], qn[:, SEQ - 1:SEQ])
                nc.vector.tensor_copy(tail[:, 1:NSEQ],
                                      samples(qn[:, SEQ:TOK])[:, :, LS - 1:LS].rearrange("p b o -> p (b o)"))\
                  .then_inc(lru_step, 1)
                ahead_unit(3)
                for s, dst in ((0, gg), (1, ug)):
                    if s == 1:
                        dve.wait_ge(s_applied, j * NCH + NCH)
                    for c in range(NCH):
                        cols = slice(c * CH, (c + 1) * CH)
                        dve.wait_ge(act_evicted, j * 21 + (2 * NT + 16 + 3 * s + c))
                        nc.vector.tensor_tensor(dst[:, cols], dst[:, cols], sig[:, c, :], ALU.mult)\
                          .then_inc(gate_applied, 1)
                    ahead_unit(4 + s)
                dve.wait_ge(gate_applied, j * 6 + 6)
                nc.vector.tensor_tensor(gg[:, :], gg[:, :], qn[:, :], ALU.mult).then_inc(merge_step, 1)
                dve.wait_ge(merge_step, j + 1)
                dve.wait_ge(spilled, j * 16 + 16)
                nc.vector.tensor_tensor(merged[:, :], gg[:, :], ug[:, :], ALU.add).then_inc(merged_ready, 1)
            with dve.Fori(0, KT) as j:
                mix(j)

            for k in range(KT):
                dve.wait_ge(m_hi_ready, k + 1)
                nc.vector.tensor_tensor(xn_lo[:, k, :], merged_in[:, k, :], xn_hi[:, k, :].bitcast(F32),
                                        ALU.subtract).then_inc(m_lo_ready, 1)
            dve.wait_ge(x_back, 16)
            for p in range(KT // 2):
                dve.wait_ge(out_mm, p + 1)
                for o in range(2):
                    for c in range(NCH):
                        add_gated(bank[3 * o + c], GATEM, 2 * p + o, c, KT * GROUPS + 2 * p + o + 1, o)
                for n in (U_OUT + 2 * p + 6, U_OUT + 2 * p + 7):
                    split_lo(dve, n, n % 2, n % RING)
            dve.wait_ge(x_written, XW_OUT)
            norm(2, SHIFT2, SCALE2)
            ffn(U_FFN2, 6 * GROUPS, XW_OUT, KT * GROUPS + KT, GATE2, 1)
            for b in range(2):
                dve.wait_ge(rows_turned, 2 + b)
                nc.vector.tensor_copy(tailrow[:, b * HALF:(b + 1) * HALF], bank[b][0:TAIL, :]).then_inc(tail_ready, 1)
            norm(3, SHIFTF, SCALEF, final=True)

        @block.tensor
        def _(pe):
            pe.wait_ge(rows_loaded, 16 * 15)
            pe.wait_ge(const_ready, 1)
            pe.wait_ge(c_silu, 1)
            nc.tensor.transpose(bank[6][:, 0:NVEC], vrow[:, :], ident[0:NVEC, 0:NVEC])
            nc.tensor.transpose(bank[6][:, 128:128 + NADA], brow[:, :], ident[0:NADA, 0:NADA])
            for k in range(KT):
                nc.tensor.transpose(bank[7][:, 256 + k * 32:256 + (k + 1) * 32], hrow[:, k * P:(k + 1) * P],
                                    ident[0:32, 0:32])
                last = nc.tensor.transpose(bank[7][:, k * NSEQ:(k + 1) * NSEQ], csil[:, k * P:(k + 1) * P],
                                           ident[0:NSEQ, 0:NSEQ])
            last.then_inc(rows_turned, 1)
            def x_turn(t):
                pe.wait_ge(x_loaded, 48 * (t + 1))
                for s in range(3):
                    for b in range(2):
                        if t > 0:
                            pe.wait_ge(x_written, 6 * (t - 1) + 2 * s + b + 1)
                        for k in range(4):
                            last = nc.tensor.transpose(bank[2 * s + b][:, k * P:(k + 1) * P],
                                                       xrow[:, s, (4 * b + k) * P:(4 * b + k + 1) * P], ident[:, :])
                        last.then_inc(x_turned, 1)
            pe.wait_ge(rows_copied, 1)
            for v in range(11):
                if v < 3:
                    x_turn(v)
                pe.wait_ge(ada_loaded[v % 2], 16 * (v // 2 + 1))
                if v >= 2:
                    pe.wait_ge(ada_ready, v - 1)
                for o in range(KT):
                    for k in range(KT):
                        last = nc.tensor.matmul(bank[6 + v % 2][:, o * NSEQ:(o + 1) * NSEQ],
                                                w_ada_sb[:, v % 2, k, o * P:(o + 1) * P], cT[:, k, 0:NSEQ],
                                                start=k == 0, stop=k == KT - 1)
                last.then_inc(ada_mm, 1)
            pe.wait_ge(ada_ready, 11)

            def sums(i, c):
                if i * NCH + c >= 2:
                    pe.wait_ge(std_ready, i * NCH + c - 1)
                for k in range(KT):
                    pe.wait_ge(squared, (i * NCH + c) * KT + k + 1)
                    nc.tensor.matmul(bank[6 + c % 2][:, 0:CH], ones[:, :], sq[:, k % 2, :], start=k == 0,
                                     stop=k == KT - 1).then_inc(sumsq_mm, 1)

            def norm(i):
                for c in range(NCH):
                    sums(i, c)

            def column_job(out, slot, cols, mov_hi, mov_lo):
                for k in range(KT):
                    last = product(pe, out, w_hi[:, slot, k * P:(k + 1) * P], w_lo[:, slot, k * P:(k + 1) * P],
                                   mov_hi[:, k, cols], mov_lo[:, k, cols], k == 0, k == KT - 1)
                return last

            def ffn(i, base, h0, xw0):
                def group(g):
                    n = g * 6 + base
                    for f in range(2):
                        for u, done in ((0, gate_mm), (1, up_mm)):
                            q = 2 * f + u
                            pe.wait_ge(w_lo_ready, n + (q + 1))
                            for c in range(NCH):
                                b = 3 * u + c
                                if f == 0:
                                    pe.wait_ge(x_written, g * 24 + (xw0 - 5 + b))
                                elif u == 0:
                                    pe.wait_ge(silu_ready, g * 6 + (h0 + c + 1))
                                else:
                                    pe.wait_ge(h_full, g * 6 + (h0 + c + 1))
                                pe.wait_ge(xn_lo_ready, (i * NCH + c + 1) * KT)
                                last = column_job(bank[b][:, 0:CH], (base + q) % RING,
                                                  slice(c * CH, (c + 1) * CH), xn_hi, xn_lo)
                                last.then_inc(done, 1)
                    pe.wait_ge(w_lo_ready, n + 6)
                    for c in range(NCH):
                        pe.wait_ge(h_lo_ready, g * 6 + (h0 + NCH + c + 1))
                        for o in range(KT):
                            m = c * KT + o
                            if m < 3:
                                pe.wait_ge(silu_ready, g * 6 + (h0 + 3 + m + 1))
                            elif m < 6:
                                pe.wait_ge(h_full, g * 6 + (h0 + m + 1))
                            else:
                                pe.wait_ge(x_written, g * 24 + (xw0 + m - 5))
                            for f in range(2):
                                slot = (base + 4 + f) % RING
                                cols = slice(c * CH, (c + 1) * CH)
                                last = product(pe, bank[m % RING][:, 0:CH], w_hi[:, slot, o * P:(o + 1) * P],
                                               w_lo[:, slot, o * P:(o + 1) * P], h_hi[:, f, cols],
                                               h_lo[:, f, cols], f == 0, f == 1)
                            last.then_inc(down_mm, 1)
                with pe.Fori(0, GROUPS) as g:
                    group(g)

            norm(0)
            ffn(0, U_FFN1, 0, XW_IN)
            norm(1)

            for half in range(2):
                for t in range(NT):
                    m = half * NT + t
                    pe.wait_ge(xn_lo_ready, (NCH + t // NCH + 1) * KT)
                    if m >= RING:
                        pe.wait_ge(act_evicted, m + 1 - RING)
                    else:
                        pe.wait_ge(x_written, XW_FFN1)
                    cols = slice(t * P, (t + 1) * P)
                    for k in range(KT):
                        n = U_V + 4 * half + k // 2
                        if t == 0 and k % 2 == 0:
                            pe.wait_ge(w_lo_ready, n + 1)
                        w = slice((k % 2) * HALF, (k % 2 + 1) * HALF)
                        last = product(pe, bank[m % RING][:, :], xn_hi[:, k, cols], xn_lo[:, k, cols],
                                       w_hi[:, n % RING, w], w_lo[:, n % RING, w], k == 0, k == KT - 1)
                    last.then_inc(v_mm, 1)
                if half == 0:
                    for w, src in enumerate((ws_raw, wd_raw)):
                        pe.wait_ge(ws_masked, w + 1)
                        for b in range(2):
                            if w == 1:
                                pe.wait_ge(ws_lo_ready, b + 1)
                            for h in range(4):
                                last = nc.tensor.transpose(bank[6 + b][:, h * P:(h + 1) * P], src[:, 4 * b + h, :],
                                                           ident[:, :])
                            last.then_inc(ws_turned, 1)
            pe.wait_ge(ws_lo_ready, 4)

            def mix(j):
                def free(m):
                    if m < 21:
                        pe.wait_ge(act_evicted, j * 21 + (13 + m))
                    else:
                        pe.wait_ge(s_evicted, j * NCH + (m - 20))

                def section(m, q):
                    pe.wait_ge(w_lo_ready, j * 6 + (U_MIX + q + 1))
                    for c in range(NCH):
                        free(m + c)
                        column_job(bank[(m + c) % RING][:, 0:CH], (U_MIX + q) % RING,
                                   slice(c * CH, (c + 1) * CH), xn_hi, xn_lo).then_inc(mix_mm, 1)
                section(0, 0)
                section(3, 1)
                section(6, 2)
                pe.wait_ge(w_lo_ready, j * 6 + (U_MIX + 4))
                pe.wait_ge(xc_lo_ready, j + 1)
                slot = (U_MIX + 3) % RING
                for c in range(NCH):
                    cols = slice(c * CH, (c + 1) * CH)
                    for g in range(2):
                        m = 9 + 2 * c + g
                        free(m)
                        w = slice(g * P, (g + 1) * P)
                        product(pe, bank[m % RING][:, 0:CH], w_hi[:, slot, w], w_lo[:, slot, w], s_hi[:, cols],
                                s_lo[:, cols], True, True).then_inc(mix_mm, 1)
                pe.wait_ge(vn_lo_ready, j + 1)
                for c in range(NCH):
                    free(15 + c)
                    for s in range(3):
                        t = 3 * c + s
                        cols = slice(t * P, (t + 1) * P)
                        w = int(t == NT - 1)
                        last = product(pe, bank[(15 + c) % RING][:, s * P:(s + 1) * P], s_hi[:, cols], s_lo[:, cols],
                                       ws_hi[:, w, ds(j, 1), :].rearrange("p o t -> p (o t)"),
                                       ws_lo[:, w, ds(j, 1), :].rearrange("p o t -> p (o t)"), True, True)
                    last.then_inc(s_mm, 1)
                section(18, 4)
                section(21, 5)
            with pe.Fori(0, KT) as j:
                mix(j)

            pe.wait_ge(act_evicted, 2 * NT + 21 * KT)
            for p in range(KT // 2):
                pe.wait_ge(w_lo_ready, U_OUT + 2 * p + 2)
                for k in range(KT):
                    pe.wait_ge(m_lo_ready, k + 1)
                    for o in range(2):
                        slot = (U_OUT + 2 * p + o) % RING
                        rows = slice(k * P, (k + 1) * P)
                        for c in range(NCH):
                            if p > 0 and k == 0:
                                pe.wait_ge(x_written, XW_FFN1 + 6 * (p - 1) + 3 * o + c + 1)
                            cols = slice(c * CH, (c + 1) * CH)
                            last = product(pe, bank[3 * o + c][:, 0:CH], w_hi[:, slot, rows], w_lo[:, slot, rows],
                                           xn_hi[:, k, cols], xn_lo[:, k, cols], k == 0, k == KT - 1)
                last.then_inc(out_mm, 1)
            norm(2)
            ffn(2, U_FFN2, 6 * GROUPS, XW_OUT)
            pe.wait_ge(x_written, XW_FFN2)
            for b in range(2):
                for k in range(4):
                    last = nc.tensor.transpose(bank[b][0:TAIL, k * P:(k + 1) * P], tails[:, 4 * b + k, :], ident[:, :])
                last.then_inc(rows_turned, 1)
            pe.wait_ge(tail_ready, 2)
            for c in range(NCH):
                sums(3, c)
                pe.wait_ge(xf_ready, (3 * NCH + c + 1) * KT)
                if c == NCH - 1:
                    pe.wait_ge(xs_step, 2 * KT * 4)
                for s in range(3):
                    t = 3 * c + s
                    for b in range(2):
                        m = 2 * t + b
                        if m >= RING:
                            pe.wait_ge(yrow_dve if b else yrow_act, t - 2)
                        for k in range(4):
                            last = nc.tensor.transpose(bank[m % RING][:, k * P:(k + 1) * P],
                                                       yT[:, 4 * b + k, s * P:(s + 1) * P], ident[:, :])
                        last.then_inc(y_turned, 1)
    return nc


_OUTS = (("y_prompt", (1, SEQ, D)), ("y_sample", (NS, LS, D)), ("conv_prompt", (1, 1, HIST, D)),
         ("rglru_prompt", (1, 1, D)), ("sgu_v_prompt", (1, 1, P, D)), ("conv_sample", (1, NS, HIST, D)),
         ("rglru_sample", (1, NS, D)), ("sgu_v_sample", (1, NS, LS, D)))


def kernel(**inputs):
    import concourse.bacc as bacc
    from concourse.bass_utils import run_bass_kernel_spmd

    nc = bacc.Bacc("TRN2", target_bir_lowering=False, num_devices=1, dynamic_dma_scratch_size=1024)
    arrays, ins, outs = {}, {}, {}
    for name, a in inputs.items():
        arrays[f"in_{name}"] = np.ascontiguousarray(a)
        ins[name] = nc.dram_tensor(f"in_{name}", a.shape, F32, kind="ExternalInput").ap()
    for name, shape in _OUTS:
        outs[name] = nc.dram_tensor(f"out_{name}", shape, F32, kind="ExternalOutput").ap()
    build(nc, ins, outs)
    r = run_bass_kernel_spmd(nc, [arrays], core_ids=[0])
    return tuple(r.results[0][f"out_{name}"] for name, _ in _OUTS)
```

```python
import numpy as np
import concourse.bass as bass
from concourse import mybir

F32 = mybir.dt.float32
F32R = mybir.dt.float32r
ALU = mybir.AluOpType
ACT = mybir.ActivationFunctionType
ds = bass.ds

P = 128
D = 1024
KT = D // P
SEQ = 1024
NS, LS = 8, 16
NSEQ = 1 + NS
TOK = SEQ + NS * LS
CH = 384
NCH = TOK // CH
PC2 = SEQ - 2 * CH
NT = TOK // P
DFF = 2816
NF = DFF // P
GROUPS = NF // 2
TAPS = 4
HIST = TAPS - 1
EPS = 1e-6
FIRST = 3
LATER = 11 - FIRST
UNIT = D
RING = 6
NADA = 11 * KT
HALF = D // 2
TAIL = NSEQ + HIST * NSEQ

U_FFN1 = 0
U_V = U_FFN1 + 6 * GROUPS
U_MIX = U_V + 8
U_OUT = U_MIX + 6 * KT
U_FFN2 = U_OUT + 8
U_END = U_FFN2 + 6 * GROUPS

SHIFT1, SCALE1, GATE1, SHIFTM, SCALEM, GATEM, SHIFT2, SCALE2, GATE2, SHIFTF, SCALEF = range(11)
V_G1, V_GM, V_G2, V_GF, V_BCONV, V_WCONV, V_BA, V_BX, V_LAM = 0, 8, 16, 24, 32, 40, 72, 80, 88
NVEC = 96

XW_IN = 2 * NT
XW_FFN1 = XW_IN + 24 * GROUPS
XW_OUT = XW_FFN1 + 24
XW_FFN2 = XW_OUT + 24 * GROUPS


def build(nc, ins, outs):
    cursor = [1152]

    def at(name, shape, dtype=F32, offset=None):
        size = 4 * int(np.prod(shape[1:]))
        if offset is None:
            offset = cursor[0]
            cursor[0] += -(-size // 32) * 32
        return nc.alloc_sbuf_tensor_at(name, shape, dtype, offset=offset, align_bytes=32)

    ident = at("ident", [P, P])
    ones = at("ones", [P, P])
    ada = at("ada", [P, NADA, NSEQ])
    vecT = at("vecT", [P, NVEC])
    badaT = at("badaT", [P, NADA])
    cT = at("cT", [P, KT, NSEQ + 1])
    histT = at("histT", [P, KT, 32])
    blk = at("blk", [P, 3])
    epst = at("epst", [P, 8])
    tails = at("tails", [P, KT, TAIL])
    mv = at("mv", [P, NT, 2])
    vstd = at("vstd", [P, NT + 1])
    bnst = at("bnst", [P, NT, 2, 6])
    raw = at("raw", [P, 2, UNIT])
    w_hi = at("w_hi", [P, RING, UNIT], F32R)
    w_lo = at("w_lo", [P, RING, UNIT], F32R)
    xn_at = cursor[0]
    xn_hi = at("xn_hi", [P, KT, TOK], F32R)
    xn_lo = at("xn_lo", [P, KT, TOK], F32R)
    region = cursor[0]

    x = at("x", [P, KT, TOK])
    h_at = cursor[0]
    h_hi = at("h_hi", [P, 2, TOK], F32R)
    h_lo = at("h_lo", [P, 2, TOK], F32R)
    silu = at("silu", [P, 2, CH])
    hfull = at("hfull", [P, 2, CH])
    sq = at("sq", [P, 3, CH])
    acc = at("acc", [P, NCH, CH])
    gtmp = at("gtmp", [P, 2, P])
    ada_raw = at("ada_raw", [P, UNIT])
    ada_hi = at("ada_hi", [P, UNIT], F32R)
    ada_lo = at("ada_lo", [P, UNIT], F32R)
    ada_row = at("ada_row", [2 * NSEQ, HALF])
    c_parts = at("c_parts", [P, KT, 2 * NSEQ], F32R)
    fold = at("fold", [2 * NSEQ, NSEQ])
    end_ffn = cursor[0]
    tbuf, xfull = silu, hfull
    merged_in = at("merged_in", [P, KT, TOK], offset=h_at)
    yT = at("yT", [P, KT, CH], offset=xn_at)
    yrow = at("yrow", [P, 2, D], offset=xn_at + 4 * KT * CH)
    tailrow = at("tailrow", [TAIL, D], offset=xn_at + 4 * KT * CH + 8 * D)
    w_ada_sb = at("w_ada_sb", [P, 2, KT, D], offset=xn_at)
    rg_sb = at("rg_sb", [P, KT, 2, P], offset=xn_at + 8 * KT * D)
    xrow = at("xrow", [P, NT // 3, D], offset=h_at)
    vrow = at("vrow", [NVEC, P], offset=h_at + 12 * D)
    brow = at("brow", [NADA, P], offset=h_at + 12 * D + 512)
    crow = at("crow", [NSEQ, D], offset=h_at + 12 * D + 1024)
    hrow = at("hrow", [32, D], offset=h_at + 16 * D + 1024)
    csil = at("csil", [NSEQ, D], offset=h_at + 20 * D + 1024)
    spw = at("spw", [P, 6, KT], offset=h_at + 24 * D + 1024)

    cursor[0] = region
    bsb = at("bsb", [P, KT, P])
    ws_hi = at("ws_hi", [P, 2, KT, P], F32R)
    ws_lo = at("ws_lo", [P, 2, KT, P], F32R)
    xr = at("xr", [P, HIST + SEQ + NS * (HIST + LS) + 1])
    xc_at = cursor[0]
    xc = at("xc", [P, TOK])
    m_at = cursor[0]
    merged = at("merged", [P, TOK])
    s_hi = at("s_hi", [P, TOK], F32R)
    s_lo = at("s_lo", [P, TOK], F32R)
    ws_raw = at("ws_raw", [P, KT, P], offset=xc_at)
    wd_raw = at("wd_raw", [P, KT, P], offset=m_at)
    v_at = cursor[0]
    gg = at("gg", [P, TOK])
    ug = at("ug", [P, TOK])
    ww = at("ww", [P, TOK])
    ii = at("ii", [P, TOK])
    qn = at("qn", [P, TOK])
    rt = at("rt", [P, TOK])
    v_in = at("v_in", [P, TOK])
    sig = at("sig", [P, NCH, CH])
    sb = at("sb", [P, 2, CH])
    end_mix = cursor[0]
    cursor[0] = v_at
    v_all = at("v_all", [P, NT, D])
    lng = at("lng", [P, D])
    lnb = at("lnb", [P, D])
    assert max(end_ffn, end_mix, cursor[0], h_at + 4 * KT * TOK) <= nc.sbuf_usable_end

    bank = [nc.alloc_psum_tensor(f"bank{i}", [P, 512], F32) for i in range(8)]

    x_dram = nc.dram_tensor("x_dram", [P, KT, TOK], F32).ap()
    vn_dram = nc.dram_tensor("vn_dram", [NT, P, D], F32).ap()
    merged_dram = nc.dram_tensor("merged_dram", [KT, P, TOK], F32).ap()
    rg_dram = nc.dram_tensor("rg_dram", [KT, P, 2 * P], F32).ap()

    def sem(name):
        return nc.alloc_semaphore(name)

    raw_loaded = [sem(f"raw_loaded{i}") for i in range(2)]
    ada_loaded = [sem(f"ada_loaded{i}") for i in range(2)]
    piece_loaded = sem("piece_loaded")
    c_loaded = sem("c_loaded")
    x_loaded = sem("x_loaded")
    rows_loaded = sem("rows_loaded")
    rg_loaded = sem("rg_loaded")
    rg_stored = sem("rg_stored")
    ws_loaded = sem("ws_loaded")
    spilled = sem("spilled")
    vn_stored = sem("vn_stored")
    v_loaded = sem("v_loaded")
    x_back = sem("x_back")
    merged_back = [sem(f"merged_back{k}") for k in range(KT)]
    y_stored = [sem(f"y_stored{i}") for i in range(2)]
    state_stored = sem("state_stored")
    rows_turned = sem("rows_turned")
    x_turned = sem("x_turned")
    ada_mm = sem("ada_mm")
    ada_folded = sem("ada_folded")
    sumsq_mm = sem("sumsq_mm")
    gate_mm = sem("gate_mm")
    up_mm = sem("up_mm")
    down_mm = sem("down_mm")
    v_mm = sem("v_mm")
    ws_turned = sem("ws_turned")
    mix_mm = sem("mix_mm")
    s_mm = sem("s_mm")
    out_mm = sem("out_mm")
    y_turned = sem("y_turned")
    w_hi_ready = sem("w_hi_ready")
    c_silu = sem("c_silu")
    sp_exp = sem("sp_exp")
    squared = sem("squared")
    std_ready = sem("std_ready")
    xf_ready = sem("xf_ready")
    piece_hi_ready = sem("piece_hi_ready")
    ada_row_ready = sem("ada_row_ready")
    xn_hi_ready = sem("xn_hi_ready")
    silu_ready = sem("silu_ready")
    h_hi_ready = sem("h_hi_ready")
    act_evicted = sem("act_evicted")
    vstd_ready = sem("vstd_ready")
    ws_hi_ready = sem("ws_hi_ready")
    xc_hi_ready = sem("xc_hi_ready")
    vn_hi_ready = sem("vn_hi_ready")
    w_ready = sem("w_ready")
    root_ready = sem("root_ready")
    m_hi_ready = sem("m_hi_ready")
    yrow_act = sem("yrow_act")
    w_lo_ready = sem("w_lo_ready")
    rows_copied = sem("rows_copied")
    ada_ready = sem("ada_ready")
    piece_lo_ready = sem("piece_lo_ready")
    sp_step = sem("sp_step")
    mod_step = sem("mod_step")
    x_written = sem("x_written")
    rstd_ready = sem("rstd_ready")
    t_ready = sem("t_ready")
    xs_step = sem("xs_step")
    xn_lo_ready = sem("xn_lo_ready")
    h_full = sem("h_full")
    h_lo_ready = sem("h_lo_ready")
    gated_tmp = sem("gated_tmp")
    v_step = sem("v_step")
    vn_ready = sem("vn_ready")
    ws_lo_ready = sem("ws_lo_ready")
    xr_free = sem("xr_free")
    conv_step = sem("conv_step")
    xc_lo_ready = sem("xc_lo_ready")
    vn_lo_ready = sem("vn_lo_ready")
    s_evicted = sem("s_evicted")
    s_applied = sem("s_applied")
    lru_step = sem("lru_step")
    gate_applied = sem("gate_applied")
    merge_step = sem("merge_step")
    merged_ready = sem("merged_ready")
    m_lo_ready = sem("m_lo_ready")
    yrow_dve = sem("yrow_dve")
    tail_ready = sem("tail_ready")
    const_ready = sem("const_ready")
    acc_added = sem("acc_added")
    const_step = sem("const_step")
    rg_zeroed = sem("rg_zeroed")
    wd_zeroed = sem("wd_zeroed")
    ws_masked = sem("ws_masked")

    def samples(ap):
        return ap.rearrange("p (b l) -> p b l", b=NS)

    def per_sample(v, k):
        return ada[:, v * KT + k, 1:NSEQ].unsqueeze(2).broadcast_to([P, NS, LS])

    def prompt_scalar(v, k):
        return ada[:, v * KT + k, 0:1]

    def split_hi(act, n, par, slot):
        act.wait_ge(raw_loaded[par], raw_count(n, par))
        nc.scalar.activation(w_hi[:, slot, :], raw[:, par, :], ACT.Copy).then_inc(w_hi_ready, 1)

    def split_lo(dve, n, par, slot):
        dve.wait_ge(w_hi_ready, n + 1)
        nc.vector.tensor_tensor(w_lo[:, slot, :], raw[:, par, :], w_hi[:, slot, :].bitcast(F32),
                                ALU.subtract).then_inc(w_lo_ready, 1)

    def raw_count(n, par):
        if isinstance(n, int):
            return 16 * (n // 2 + 1)
        return n * 8 + (16 - 8 * par)

    def product(pe, out, hi, lo, mov_hi, mov_lo, first, last):
        nc.tensor.matmul(out, hi, mov_hi, start=first, stop=False, skip_group_check=True)
        nc.tensor.matmul(out, hi, mov_lo, start=False, stop=False, skip_group_check=True)
        return nc.tensor.matmul(out, lo, mov_hi, start=False, stop=last, skip_group_check=True)

    def squares_order(i):
        if i == 2:
            return [(c, k) for k in range(KT) for c in range(NCH)]
        return [(c, k) for c in range(NCH) for k in range(KT)]

    def added(i, pos):
        return i * NCH * (KT - 1) + sum(k > 0 for _, k in squares_order(i)[:pos])

    def residual_written(i, c, k):
        if i == 0:
            return XW_IN
        if i == 2:
            return XW_FFN1 + 6 * (k // 2) + 3 * (k % 2) + c + 1
        return (XW_FFN1 if i == 1 else XW_FFN2) - KT * (NCH - c) + k + 1

    def columns(w, col, width=P):
        return w.rearrange("(k p) n -> p k n", p=P)[:, :, ds(col, width)]

    def add_squares(pool, i):
        for pos, (c, k) in enumerate(squares_order(i)):
            if k == 0:
                continue
            pool.wait_ge(squared, i * NCH * KT + pos + 1)
            if added(i, pos):
                pool.wait_ge(acc_added, added(i, pos))
            nc.gpsimd.tensor_tensor(acc[:, c, :], acc[:, c, :], sq[:, pos % 3, :], ALU.add).then_inc(acc_added, 1)

    def tile_rows(sp, t):
        if t > 0:
            sp.wait_ge(x_turned, 6 * t)
        for s in range(3):
            tile = 3 * t + s
            src = (ins["x_prompt"].rearrange("b s d -> (b s) d")[tile * P:(tile + 1) * P, :] if tile < NT - 1
                   else ins["x_sample"].rearrange("b s d -> (b s) d"))
            sp.dma_start(xrow[:, s, :], src).then_inc(x_loaded, 16)

    def xr_samples(t):
        return t[:, HIST + SEQ:HIST + SEQ + NS * (HIST + LS)].rearrange("p (b l) -> p b l", b=NS)

    def v_count(t, s):
        n, base = 0, 3 * NT + 1
        for u in range(NT + 2):
            if u < NT:
                n += 1
                if (u, 0) == (t, s):
                    return base + n
            if 1 <= u <= NT:
                n += 1
                if (u - 1, 1) == (t, s):
                    return base + n

    block = nc.Block()
    with block:

        @block.sync
        def _(sp):
            def unit(n, par, src, dst=None):
                if not isinstance(n, int) or n >= 2:
                    sp.wait_ge(w_lo_ready, n - 1)
                dst = raw[:, par, :] if dst is None else dst
                sp.dma_start(dst, src).then_inc(raw_loaded[par], 16)

            def wide(par):
                return raw[:, par, :].rearrange("p (k n) -> p k n", k=KT)

            sp.dma_start(crow[0:1, :], ins["c_prompt"]).then_inc(c_loaded, 16)
            sp.dma_start(crow[1:NSEQ, :], ins["c_sample"]).then_inc(c_loaded, 16)
            w_ada = ins["w_ada"].rearrange("o k n -> (o k) n")
            tile_rows(sp, 0)
            sp.dma_start(w_ada_sb[:, 0], columns(w_ada, 0, D)).then_inc(ada_loaded[0], 16)
            tile_rows(sp, 1)
            tile_rows(sp, 2)
            sp.dma_start(w_ada_sb[:, 1], columns(w_ada, D, D)).then_inc(ada_loaded[1], 16)
            sp.wait_ge(ada_mm, 1)
            sp.dma_start(w_ada_sb[:, 0], columns(w_ada, 2 * D, D)).then_inc(ada_loaded[0], 16)
            sp.wait_ge(rg_loaded, 64)
            sp.dma_start(rg_dram.rearrange("k p n -> p k n"),
                         rg_sb[:, :, :, :].rearrange("p k g n -> p k (g n)")).then_inc(rg_stored, 16)

            def ffn_units(base, name):
                gate, up, down = (ins[f"w_{name}_{w}"].rearrange("o k n -> (o k) n") for w in ("gate", "up", "down"))

                def group(g, ada_cols=None):
                    n = base + g * 6
                    col = g * (2 * P)

                    def units(*qs):
                        for q in qs:
                            f = (q // 2) % 2 if q < 4 else q - 4
                            if q >= 4:
                                unit(n + q, f, down[ds(col + f * P, P), :])
                            else:
                                unit(n + q, q % 2, columns((gate, up)[q % 2], col + f * P), wide(q % 2))

                    def pieces(*rs):
                        if ada_cols is None:
                            return
                        w, first, c0 = ada_cols
                        for r in rs:
                            sp.wait_ge(piece_lo_ready, g * 8 + r + 1)
                            src = w.rearrange("(k p) n -> p k n", p=P)[:, 2 * (r % 4):2 * (r % 4) + 2,
                                                                      ds((g - first) * D + c0 + (r // 4) * HALF, HALF)]
                            sp.dma_start(ada_raw[:, :].rearrange("p (k n) -> p k n", k=2), src)\
                              .then_inc(piece_loaded, 16)
                    return units, pieces

                def ahead(g, ada_cols=None, last=False):
                    units, _ = group(g + 1)
                    _, pieces = group(g, ada_cols)
                    pieces(0, 1, 2)
                    if not last:
                        units(0, 1)
                    pieces(3, 4, 5)
                    if not last:
                        units(2, 3)
                    pieces(6, 7)
                    if not last:
                        units(4, 5)
                group(0)[0](0, 1, 2, 3, 4, 5)
                if base == 0:
                    with sp.Fori(0, 9 - FIRST) as g:
                        ahead(g, (w_ada, 0, FIRST * D))
                    with sp.Fori(9 - FIRST, LATER) as g:
                        ahead(g, (ins["w_ada_final"], 9 - FIRST, 0))
                    with sp.Fori(LATER, GROUPS - 1) as g:
                        ahead(g)
                else:
                    with sp.Fori(0, GROUPS - 1) as g:
                        ahead(g)

            ffn_units(U_FFN1, "ffn1")

            w_in = ins["w_in"].rearrange("o k n -> (o k) n")
            w_v = w_in.rearrange("(k p) n -> p k n", p=P)
            for q in range(8):
                half, kp = divmod(q, 4)
                unit(U_V + q, q % 2, w_v[:, 2 * kp:2 * kp + 2, 3 * D + half * HALF:3 * D + (half + 1) * HALF],
                     raw[:, q % 2, :].rearrange("p (k n) -> p k n", k=2))
                if q == 5:
                    sp.wait_ge(x_written, XW_FFN1)
                    sp.dma_start(x_dram, x[:, :, :]).then_inc(spilled, 16)
                    sp.wait_ge(t_ready, 2 * NCH * KT)
                    sp.wait_ge(xn_lo_ready, 2 * NCH * KT)
                    sp.wait_ge(spilled, 16)
                    sp.dma_start(lng[:, :], ins["ln_v_g"].broadcast_to([P, D])).then_inc(ws_loaded, 16)
                    sp.dma_start(lnb[:, :], ins["ln_v_b"].broadcast_to([P, D])).then_inc(ws_loaded, 16)
                    sp.dma_start(bsb[:, :, :].rearrange("p h t -> p (h t)"),
                                 ins["b_spatial"].rearrange("o h t -> o (h t)").broadcast_to([P, D]))\
                      .then_inc(ws_loaded, 16)
                    sp.dma_start(ws_raw[:, :, :], ins["w_spatial"].rearrange("o h t s -> t (o h) s"))\
                      .then_inc(ws_loaded, 16)
                    sp.wait_ge(wd_zeroed, 1)
                    for b in range(NS):
                        sp.dma_start(wd_raw[b * LS:(b + 1) * LS, :, b * LS:(b + 1) * LS],
                                     ins["w_spatial"].rearrange("o h t s -> t (o h) s")[0:LS, :, 0:LS])\
                          .then_inc(ws_loaded, 16)

            def mix_units(j):
                n = U_MIX + j * 6
                for q, sec in ((0, 0), (1, 1), (2, 2)):
                    unit(n + q, q % 2, columns(w_in, sec * D + j * P), wide(q % 2))
                if not isinstance(j, int) or j > 0:
                    sp.wait_ge(vn_lo_ready, j)
                sp.dma_start(v_in[:, :].rearrange("p (t c) -> p t c", t=NT),
                             vn_dram.rearrange("t p n -> p t n")[:, :, ds(j * P, P)]).then_inc(v_loaded, 16)
                unit(n + 3, 1, rg_dram.rearrange("k p n -> (k p) n")[ds(j * P, P), :], raw[:, 1, 0:2 * P])
                for q, sec in ((4, 4), (5, 5)):
                    unit(n + q, q % 2, columns(w_in, sec * D + j * P), wide(q % 2))

            def store_merged(j):
                sp.wait_ge(merged_ready, j + 1)
                sp.dma_start(merged_dram.rearrange("k p n -> (k p) n")[ds(j * P, P), :],
                             merged[:, :]).then_inc(spilled, 16)

            n = U_MIX
            for q, sec in ((0, 0), (1, 1), (2, 2)):
                unit(n + q, q % 2, columns(w_in, sec * D), wide(q % 2))
            sp.wait_ge(rg_stored, 16)
            unit(n + 3, 1, rg_dram[0], raw[:, 1, 0:2 * P])
            unit(n + 4, 0, columns(w_in, 4 * D), wide(0))
            unit(n + 5, 1, columns(w_in, 5 * D), wide(1))
            for t in range(NT):
                sp.wait_ge(vn_ready, t + 1)
                sp.dma_start(vn_dram[t], v_all[:, t, :]).then_inc(vn_stored, 16)
            sp.dma_start(outs["sgu_v_prompt"].rearrange("o b s d -> (o b s) d"), v_all[:, NT - 2, :])\
              .then_inc(vn_stored, 16)
            sp.dma_start(outs["sgu_v_sample"].rearrange("o b s d -> (o b s) d"), v_all[:, NT - 1, :])\
              .then_inc(vn_stored, 16)
            sp.wait_ge(vn_stored, 16 * (NT + 2))
            sp.dma_start(v_in[:, :].rearrange("p (t c) -> p t c", t=NT),
                         vn_dram.rearrange("t p n -> p t n")[:, :, 0:P]).then_inc(v_loaded, 16)
            mix_units(1)
            with sp.Fori(2, KT) as j:
                store_merged(j - 2)
                mix_units(j)
            store_merged(KT - 2)
            for q in range(RING):
                unit(U_OUT + q, q % 2, columns(ins["w_out"].rearrange("o k n -> (o k) n"), q * P), wide(q % 2))
            store_merged(KT - 1)
            sp.wait_ge(spilled, 16 * (1 + KT))
            for k in range(KT):
                sp.dma_start(merged_in[:, k, :], merged_dram[k]).then_inc(merged_back[k], 16)
            sp.dma_start(x[:, :, :], x_dram).then_inc(x_back, 16)
            for q in range(RING, KT):
                unit(U_OUT + q, q % 2, columns(ins["w_out"].rearrange("o k n -> (o k) n"), q * P), wide(q % 2))
            ffn_units(U_FFN2, "ffn2")
            sp.wait_ge(tail_ready, 2)
            sp.dma_start(outs["rglru_prompt"].rearrange("o b d -> (o b) d"), tailrow[0:1, :]).then_inc(state_stored, 16)
            sp.dma_start(outs["rglru_sample"].rearrange("o b d -> (o b) d"), tailrow[1:NSEQ, :]).then_inc(state_stored, 16)
            sp.dma_start(outs["conv_prompt"].rearrange("o b w d -> (o b w) d"), tailrow[NSEQ:NSEQ + HIST, :])\
              .then_inc(state_stored, 16)
            sp.dma_start(outs["conv_sample"].rearrange("o b w d -> (o b w) d"), tailrow[NSEQ + HIST:TAIL, :])\
              .then_inc(state_stored, 16)
            for t in range(NT):
                sp.wait_ge(yrow_act, t + 1)
                sp.wait_ge(yrow_dve, t + 1)
                dst = (outs["y_prompt"].rearrange("b s d -> (b s) d")[t * P:(t + 1) * P, :] if t < NT - 1
                       else outs["y_sample"].rearrange("b s d -> (b s) d"))
                sp.dma_start(dst, yrow[:, t % 2, :]).then_inc(y_stored[t % 2], 16)
            sp.wait_ge(state_stored, 16 * 4)
            sp.wait_ge(y_stored[0], 16 * ((NT + 1) // 2))
            sp.wait_ge(y_stored[1], 16 * (NT // 2))

        @block.gpsimd
        def _(pool):
            nc.gpsimd.memset(ident[:, :], 0.0).then_inc(const_step, 1)
            nc.gpsimd.memset(ones[:, :], 1.0).then_inc(const_step, 1)
            nc.gpsimd.memset(epst[:, 0:1], EPS).then_inc(const_step, 1)
            pool.wait_ge(const_step, 3)
            nc.gpsimd.affine_select(out=ident[:, :], in_=ident[:, :], compare_op=ALU.not_equal, fill=1.0,
                                    base=0, pattern=[[-1, P]], channel_multiplier=1).then_inc(const_ready, 1)
            nc.gpsimd.memset(rg_sb[:, :, :, :], 0.0).then_inc(rg_zeroed, 1)
            add_squares(pool, 0)
            add_squares(pool, 1)
            pool.wait_ge(xn_lo_ready, 2 * NCH * KT)
            pool.wait_ge(spilled, 16)
            nc.gpsimd.memset(wd_raw[:, :, :], 0.0).then_inc(wd_zeroed, 1)
            pool.wait_ge(ws_loaded, 16 * (4 + NS))
            for w in (ws_raw, wd_raw):
                nc.gpsimd.affine_select(out=w[:, :, :], in_=w[:, :, :], compare_op=ALU.is_ge, fill=0.0,
                                        base=0, pattern=[[0, KT], [-1, P]], channel_multiplier=1)\
                  .then_inc(ws_masked, 1)
            add_squares(pool, 2)
            add_squares(pool, 3)

        @block.scalar
        def _(act):
            for dst, src in ((vrow[V_G1:V_G1 + 8, :], ins["g_ffn1"].rearrange("o (k p) -> (o k) p", p=P)),
                             (vrow[V_GM:V_GM + 8, :], ins["g_mix"].rearrange("o (k p) -> (o k) p", p=P)),
                             (vrow[V_G2:V_G2 + 8, :], ins["g_ffn2"].rearrange("o (k p) -> (o k) p", p=P)),
                             (vrow[V_GF:V_GF + 8, :], ins["g_final"].rearrange("(k p) -> k p", p=P)),
                             (vrow[V_BCONV:V_BCONV + 8, :], ins["b_conv"].rearrange("o (k p) -> (o k) p", p=P)),
                             (vrow[V_WCONV:V_WCONV + 32, :], ins["w_conv"].rearrange("o w (k p) -> (o w k) p", p=P)),
                             (vrow[V_BA:V_BA + 8, :], ins["b_rg_a"].rearrange("o (k p) -> (o k) p", p=P)),
                             (vrow[V_BX:V_BX + 8, :], ins["b_rg_x"].rearrange("o (k p) -> (o k) p", p=P)),
                             (vrow[V_LAM:V_LAM + 8, :], ins["rg_lambda"].rearrange("o (k p) -> (o k) p", p=P)),
                             (brow[0:9 * KT, :], ins["b_ada"].rearrange("o (k p) -> (o k) p", p=P)),
                             (brow[9 * KT:NADA, :], ins["b_ada_final"].rearrange("(k p) -> k p", p=P)),
                             (hrow[0:24, :], ins["cache_conv"].rearrange("o b w d -> (o b w) d")),
                             (hrow[24:32, :], ins["state_rglru"].rearrange("o b d -> (o b) d"))):
                act.dma_start(dst, src).then_inc(rows_loaded, 16)
            act.wait_ge(rg_zeroed, 1)
            for g, name in enumerate(("w_rg_a", "w_rg_x")):
                for h in range(2):
                    src = ins[name].rearrange("o (k h) i j -> h i (o k) j", h=2)[h]
                    act.dma_start(rg_sb[64 * h:64 * h + 64, :, g, 64 * h:64 * h + 64], src).then_inc(rg_loaded, 16)
            act.wait_ge(c_loaded, 32)
            nc.scalar.activation(csil[:, :], crow[:, :], ACT.Silu).then_inc(c_silu, 1)
            act.wait_ge(rows_copied, 1)
            nc.scalar.activation(c_parts[:, :, 0:NSEQ], cT[:, :, 0:NSEQ], ACT.Copy).then_inc(c_silu, 1)
            act.wait_ge(sp_step, 1)
            nc.scalar.activation(spw[:, 1, :], spw[:, 0, :], ACT.Exp, scale=-1.0).then_inc(sp_exp, 1)

            def squares(i, lo, hi):
                for pos, (c, k) in list(enumerate(squares_order(i)))[lo:hi]:
                    act.wait_ge(x_written, residual_written(i, c, k))
                    if pos >= 3 and k > 0 and added(i, pos - 2) > 0:
                        act.wait_ge(acc_added, added(i, pos - 2))
                    dst = sq[:, pos % 3, :] if k > 0 else acc[:, c, :]
                    nc.scalar.activation(dst, x[:, k, c * CH:(c + 1) * CH], ACT.Square).then_inc(squared, 1)

            def root(i, c):
                act.wait_ge(sumsq_mm, i * NCH + c + 1)
                nc.scalar.activation(acc[:, c, :], bank[6 + c % 2][:, 0:CH], ACT.Sqrt,
                                     scale=1.0 / D, bias=epst[:, 0:1]).then_inc(std_ready, 1)

            def modulate(i, c, v_shift, v_scale, final=False):
                if final and c > 0:
                    act.wait_ge(y_turned, 6 * c)
                width = CH if c < NCH - 1 else PC2
                for k in range(KT):
                    n = (i * NCH + c) * KT + k
                    act.wait_ge(t_ready, n + 1)
                    dst = yT[:, k, 0:width] if final else xfull[:, k % 2, 0:width]
                    nc.scalar.activation(dst, tbuf[:, k % 2, 0:width], ACT.Identity,
                                         scale=prompt_scalar(v_scale, k), bias=prompt_scalar(v_shift, k))\
                      .then_inc(xf_ready, 1)
                    if final:
                        continue
                    act.wait_ge(xf_ready, n + 1)
                    if c == NCH - 1:
                        act.wait_ge(xs_step, (i * KT + k + 1) * 2)
                    nc.scalar.activation(xn_hi[:, k, c * CH:(c + 1) * CH], xfull[:, k % 2, :], ACT.Copy)\
                      .then_inc(xn_hi_ready, 1)
                if final:
                    out_rows(c)

            def norm_in_tail(i, v_shift, v_scale, final=False):
                squares(i, 0, KT)
                squares(i, KT, 2 * KT)
                root(i, 0)
                modulate(i, 0, v_shift, v_scale, final)
                root(i, 1)
                squares(i, 2 * KT, 3 * KT)
                modulate(i, 1, v_shift, v_scale, final)
                root(i, 2)
                modulate(i, 2, v_shift, v_scale, final)

            def out_rows(c):
                for s in range(NCH):
                    t = NCH * c + s
                    act.wait_ge(y_turned, 2 * t + 1)
                    if t >= 2:
                        act.wait_ge(y_stored[t % 2], 16 * (t // 2))
                    nc.scalar.activation(yrow[:, t % 2, 0:HALF], bank[(2 * t) % RING][:, :], ACT.Copy)\
                      .then_inc(yrow_act, 1)

            def ffn(base, h0, with_ada):
                def group(g, ada_piece=False, tail=None):
                    def ahead_units(*qs):
                        for q in qs:
                            split_hi(act, g * 6 + (base + RING + q), q % 2, (base + q) % RING)

                    def piece(r):
                        if not ada_piece:
                            return
                        act.wait_ge(ada_mm, g * 8 + (FIRST + r))
                        if r == 4 or r == 8:
                            nc.scalar.activation(ada_row[:, :], bank[6][0:2 * NSEQ, :], ACT.Copy)\
                              .then_inc(ada_row_ready, 1)
                        if r < 8:
                            act.wait_ge(piece_loaded, g * 128 + 16 * (r + 1))
                            nc.scalar.activation(ada_hi[:, :], ada_raw[:, :], ACT.Copy).then_inc(piece_hi_ready, 1)
                    for q in range(6):
                        f, c = divmod(q, NCH)
                        piece(q)
                        act.wait_ge(gate_mm, g * 6 + (h0 + q + 1))
                        if q >= 2:
                            act.wait_ge(h_full, g * 6 + (h0 + q - 1))
                        nc.scalar.activation(silu[:, q % 2, :], bank[c][:, 0:CH], ACT.Silu).then_inc(silu_ready, 1)
                        act.wait_ge(h_full, g * 6 + (h0 + q + 1))
                        nc.scalar.activation(h_hi[:, f, c * CH:(c + 1) * CH], hfull[:, q % 2, :], ACT.Copy)\
                          .then_inc(h_hi_ready, 1)
                        if q == 2 and not (tail and tail[0] == 3):
                            ahead_units(0, 1)
                    if not (tail and tail[0] == 3):
                        ahead_units(2, 3)
                    piece(6)
                    piece(7)
                    piece(8)
                    if tail:
                        norm_in_tail(*tail)
                    if not (tail and tail[0] == 3):
                        act.wait_ge(down_mm, g * 24 + (h0 * 4 + 24))
                        ahead_units(4, 5)
                if with_ada:
                    with act.Fori(0, LATER) as g:
                        group(g, ada_piece=True)
                    with act.Fori(LATER, GROUPS - 1) as g:
                        group(g)
                    group(GROUPS - 1, tail=(1, SHIFTM, SCALEM))
                else:
                    with act.Fori(0, GROUPS - 1) as g:
                        group(g)
                    group(GROUPS - 1, tail=(3, SHIFTF, SCALEF, True))

            squares(0, 0, NCH * KT)
            for c in range(NCH):
                root(0, c)
            act.wait_ge(mod_step, 1)
            act.wait_ge(ada_mm, FIRST)
            for c in range(NCH):
                modulate(0, c, SHIFT1, SCALE1)
                if c == 0:
                    for n in range(RING):
                        split_hi(act, n, n % 2, n % RING)
            ffn(U_FFN1, 0, True)
            act.wait_ge(spilled, 16)
            act.wait_ge(xn_lo_ready, 2 * NCH * KT)
            for half in range(2):
                for t in range(NT):
                    m = half * NT + t
                    act.wait_ge(v_mm, m + 1)
                    nc.scalar.activation(v_all[:, t, half * HALF:(half + 1) * HALF], bank[m % RING][:, :],
                                         ACT.Gelu_apprx_tanh).then_inc(act_evicted, 1)
                for n in range(U_V + 6 + 4 * half, U_V + 10 + 4 * half):
                    split_hi(act, n, n % 2, n % RING)
                if half == 0:
                    for w in range(2):
                        for b in range(2):
                            act.wait_ge(ws_turned, 2 * w + b + 1)
                            nc.scalar.activation(
                                ws_hi[:, w, 4 * b:4 * b + 4, :].rearrange("p h t -> p (h t)"),
                                bank[6 + b][:, :], ACT.Copy).then_inc(ws_hi_ready, 1)
            act.wait_ge(v_step, NT * 2 + NT)
            nc.scalar.activation(vstd[:, 0:NT], mv[:, :, 1], ACT.Sqrt, bias=epst[:, 0:1]).then_inc(vstd_ready, 1)
            act.wait_ge(vn_stored, 16 * (NT + 2))

            def mix(j):
                def evicts(m, dst, src_bank, func, **kw):
                    return nc.scalar.activation(dst, src_bank, func, **kw).then_inc(act_evicted, 1)

                def section(first, count):
                    act.wait_ge(mix_mm, j * 21 + (first + count))

                def ahead_unit(q):
                    n = j * 6 + (U_MIX + RING + q)
                    split_hi(act, n, q % 2, (U_MIX + q) % RING)

                act.wait_ge(xr_free, j + 2)
                for c in range(NCH):
                    section(c, 1)
                    if c < NCH - 1:
                        evicts(c, xr[:, HIST + c * CH:HIST + (c + 1) * CH], bank[c][:, 0:CH], ACT.Copy)
                    else:
                        nc.scalar.activation(xr[:, HIST + c * CH:HIST + SEQ], bank[c][:, 0:PC2], ACT.Copy)
                        evicts(c, xr_samples(xr)[:, :, HIST:HIST + LS], samples(bank[c][:, PC2:CH]), ACT.Copy)
                ahead_unit(0)
                section(3, 1)
                evicts(3, gg[:, 0:CH], bank[3][:, 0:CH], ACT.Gelu_apprx_tanh)
                act.wait_ge(conv_step, j * 8 + 8)
                nc.scalar.activation(s_hi[:, :], xc[:, :], ACT.Copy).then_inc(xc_hi_ready, 1)
                for c in (1, 2):
                    section(3 + c, 1)
                    evicts(3 + c, gg[:, c * CH:(c + 1) * CH], bank[3 + c][:, 0:CH], ACT.Gelu_apprx_tanh)
                ahead_unit(1)
                for c in range(NCH):
                    section(6 + c, 1)
                    evicts(6 + c, ug[:, c * CH:(c + 1) * CH], bank[c][:, 0:CH], ACT.Gelu_apprx_tanh)
                ahead_unit(2)
                for c in range(NCH):
                    cols = slice(c * CH, (c + 1) * CH)
                    section(9 + 2 * c, 1)
                    evicts(9, ww[:, cols], bank[(9 + 2 * c) % RING][:, 0:CH], ACT.Sigmoid,
                           bias=blk[:, 0:1])
                    section(10 + 2 * c, 1)
                    evicts(10, ii[:, cols], bank[(10 + 2 * c) % RING][:, 0:CH], ACT.Sigmoid,
                           bias=blk[:, 1:2])
                act.wait_ge(v_loaded, j * 16 + 16)
                nc.scalar.activation(s_hi[:, :], v_in[:, :], ACT.Copy).then_inc(vn_hi_ready, 1)
                act.wait_ge(act_evicted, j * 21 + (2 * NT + 15))
                nc.scalar.activation(ww[:, :], ww[:, :], ACT.Tanh, scale=blk[:, 2:3]).then_inc(w_ready, 1)
                act.wait_ge(w_ready, j + 1)
                nc.scalar.activation(rt[:, :], ww[:, :], ACT.Sqrt, scale=4.0).then_inc(root_ready, 1)
                ahead_unit(3)
                for s in range(2):
                    for c in range(NCH):
                        section(15 + 3 * s + c, 1)
                        if s == 1:
                            act.wait_ge(gate_applied, j * 6 + (c + 1))
                        evicts(18 + 3 * s + c, sig[:, c, :], bank[3 * s + c][:, 0:CH], ACT.Sigmoid)
                    ahead_unit(4 + s)
            with act.Fori(0, KT) as j:
                mix(j)

            for k in range(KT):
                act.wait_ge(merged_back[k], 16)
                nc.scalar.activation(xn_hi[:, k, :], merged_in[:, k, :], ACT.Copy).then_inc(m_hi_ready, 1)
            act.wait_ge(m_lo_ready, KT)
            for p in range(KT // 2):
                act.wait_ge(out_mm, p + 1)
                if p < KT // 2 - 1:
                    squares(2, 6 * p, 6 * p + 6)
                for n in (U_OUT + 2 * p + 6, U_OUT + 2 * p + 7):
                    if p < KT // 2 - 1:
                        split_hi(act, n, n % 2, n % RING)
            squares(2, 18, 24)
            for c in range(NCH):
                root(2, c)
            for c in range(NCH):
                modulate(2, c, SHIFT2, SCALE2)
                if c == 0:
                    for n in (U_OUT + 12, U_OUT + 13):
                        split_hi(act, n, n % 2, n % RING)
            ffn(U_FFN2, 6 * GROUPS, False)

        @block.vector
        def _(dve):
            dve.wait_ge(rows_turned, 1)
            nc.vector.tensor_copy(vecT[:, :], bank[6][:, 0:NVEC])
            nc.vector.tensor_copy(badaT[:, :], bank[6][:, 128:128 + NADA])
            nc.vector.tensor_copy(histT[:, :, :], bank[7][:, 256:512].rearrange("p (k n) -> p k n", k=KT))
            nc.vector.tensor_copy(cT[:, :, 0:NSEQ],
                                  bank[7][:, 0:KT * NSEQ].rearrange("p (k n) -> p k n", k=KT))\
              .then_inc(rows_copied, 1)
            dve.wait_ge(rows_copied, 1)
            nc.vector.tensor_tensor(fold[:, :], ident[0:2 * NSEQ, 0:NSEQ], ident[0:2 * NSEQ, NSEQ:2 * NSEQ], ALU.add)
            dve.wait_ge(c_silu, 2)
            nc.vector.tensor_tensor(c_parts[:, :, NSEQ:2 * NSEQ], cT[:, :, 0:NSEQ],
                                    c_parts[:, :, 0:NSEQ].bitcast(F32), ALU.subtract).then_inc(piece_lo_ready, 1)
            lam = vecT[:, V_LAM:V_LAM + KT]
            steps = [0]

            def step(ins_):
                steps[0] += 1
                ins_.then_inc(sp_step, 1)

            def after():
                dve.wait_ge(sp_step, steps[0])
            nc.vector.tensor_scalar(spw[:, 5, :], lam, -1.0, 0.0, ALU.mult, ALU.max)
            step(nc.vector.scalar_tensor_tensor(spw[:, 0, :], lam, -1.0, lam, ALU.mult, ALU.max))
            dve.wait_ge(sp_exp, 1)
            step(nc.vector.tensor_scalar(spw[:, 2, :], spw[:, 1, :], 2.0, None, ALU.add))
            after()
            step(nc.vector.reciprocal(spw[:, 3, :], spw[:, 2, :]))
            after()
            step(nc.vector.tensor_tensor(spw[:, 0, :], spw[:, 1, :], spw[:, 3, :], ALU.mult))
            after()
            step(nc.vector.tensor_tensor(spw[:, 1, :], spw[:, 0, :], spw[:, 0, :], ALU.mult))
            after()
            step(nc.vector.tensor_scalar(spw[:, 2, :], spw[:, 1, :], 1.0 / 17, 1.0 / 15, ALU.mult, ALU.add))
            for d in (13, 11, 9, 7, 5, 3, 1):
                after()
                step(nc.vector.tensor_tensor(spw[:, 3, :], spw[:, 2, :], spw[:, 1, :], ALU.mult))
                after()
                step(nc.vector.tensor_scalar(spw[:, 2, :], spw[:, 3, :], 1.0 / d, None, ALU.add))
            after()
            step(nc.vector.scalar_tensor_tensor(spw[:, 3, :], spw[:, 2, :], 2.0, spw[:, 0, :], ALU.mult, ALU.mult))
            after()
            step(nc.vector.tensor_tensor(spw[:, 4, :], spw[:, 3, :], spw[:, 5, :], ALU.add))
            after()
            step(nc.vector.tensor_scalar(lam, spw[:, 4, :], 4.0, None, ALU.mult))

            def x_in(t):
                for s in range(3):
                    for b in range(2):
                        dve.wait_ge(x_turned, 6 * t + 2 * s + b + 1)
                        tile = 3 * t + s
                        nc.vector.tensor_copy(
                            x[:, 4 * b:4 * b + 4, tile * P:(tile + 1) * P],
                            bank[2 * s + b][:, :].rearrange("p (k n) -> p k n", k=4)).then_inc(x_written, 1)
            for t in range(3):
                x_in(t)
            gains = {SCALE1: V_G1, SCALEM: V_GM, SCALE2: V_G2, SCALEF: V_GF}

            def scale_gain(v):
                a = ada[:, v * KT:(v + 1) * KT, :]
                g = vecT[:, gains[v]:gains[v] + KT]
                nc.vector.scalar_tensor_tensor(a, a, 1.0, g.unsqueeze(2).broadcast_to([P, KT, NSEQ]),
                                               ALU.add, ALU.mult).then_inc(mod_step, 1)

            def first_vector(v):
                dve.wait_ge(ada_mm, v + 1)
                nc.vector.tensor_tensor(
                    ada[:, v * KT:(v + 1) * KT, :],
                    bank[3 + v][:, 0:KT * NSEQ].rearrange("p (k n) -> p k n", k=KT),
                    badaT[:, v * KT:(v + 1) * KT].unsqueeze(2).broadcast_to([P, KT, NSEQ]), ALU.add)\
                  .then_inc(ada_ready, 1)

            def reciprocal(i, c):
                dve.wait_ge(std_ready, i * NCH + c + 1)
                nc.vector.reciprocal(acc[:, c, :], acc[:, c, :]).then_inc(rstd_ready, 1)

            def modulate(i, c, k, v_shift, v_scale, final=False):
                cols = slice(c * CH, (c + 1) * CH)
                if k < KT:
                    n = (i * NCH + c) * KT + k
                    if k == 0:
                        dve.wait_ge(rstd_ready, i * NCH + c + 1)
                    if final:
                        dve.wait_ge(xf_ready, n - 1)
                    elif n >= 2:
                        dve.wait_ge(xn_lo_ready, n - 1)
                    nc.vector.tensor_tensor(tbuf[:, k % 2, :], x[:, k, cols], acc[:, c, :], ALU.mult)\
                      .then_inc(t_ready, 1)
                    if c == NCH - 1:
                        s0 = (i * KT + k) * 2
                        dve.wait_ge(t_ready, n + 1)
                        ts = samples(tbuf[:, k % 2, PC2:CH])
                        nc.vector.tensor_tensor(ts, ts, per_sample(v_scale, k), ALU.mult).then_inc(xs_step, 1)
                        dve.wait_ge(xs_step, s0 + 1)
                        dst = yT[:, k, PC2:CH] if final else xfull[:, k % 2, PC2:CH]
                        nc.vector.tensor_tensor(samples(dst), ts, per_sample(v_shift, k), ALU.add)\
                          .then_inc(xs_step, 1)
                if k > 0 and not final:
                    n = (i * NCH + c) * KT + k - 1
                    dve.wait_ge(xn_hi_ready, n + 1)
                    nc.vector.tensor_tensor(xn_lo[:, k - 1, cols], xfull[:, (k - 1) % 2, :],
                                            xn_hi[:, k - 1, cols].bitcast(F32), ALU.subtract)\
                      .then_inc(xn_lo_ready, 1)

            def modulate_chunk(i, c, *vs):
                for k in range(KT + 1):
                    modulate(i, c, k, *vs)
                if len(vs) == 3:
                    out_rows(c)

            def out_rows(c):
                for s in range(NCH):
                    t = NCH * c + s
                    dve.wait_ge(y_turned, 2 * t + 2)
                    if t >= 2:
                        dve.wait_ge(y_stored[t % 2], 16 * (t // 2))
                    nc.vector.tensor_copy(yrow[:, t % 2, HALF:D], bank[(2 * t + 1) % RING][:, :])\
                      .then_inc(yrow_dve, 1)

            def add_gated(ps, v, o, c, tmp_count, tmp_slot):
                if c < NCH - 1:
                    cols = slice(c * CH, (c + 1) * CH)
                    nc.vector.scalar_tensor_tensor(x[:, o, cols], ps[:, 0:CH], prompt_scalar(v, o), x[:, o, cols],
                                                   ALU.mult, ALU.add).then_inc(x_written, 1)
                    return
                nc.vector.tensor_tensor(samples(gtmp[:, tmp_slot, :]), samples(ps[:, PC2:CH]), per_sample(v, o),
                                        ALU.mult).then_inc(gated_tmp, 1)
                nc.vector.scalar_tensor_tensor(x[:, o, c * CH:SEQ], ps[:, 0:PC2], prompt_scalar(v, o),
                                               x[:, o, c * CH:SEQ], ALU.mult, ALU.add)
                dve.wait_ge(gated_tmp, tmp_count)
                nc.vector.tensor_tensor(x[:, o, SEQ:TOK], x[:, o, SEQ:TOK], gtmp[:, tmp_slot, :], ALU.add)\
                  .then_inc(x_written, 1)

            def ffn(base, h0, xw0, tmp0, v_gate, with_ada):
                def group(g, ada_piece=False, tail=None):
                    ahead = not (tail and tail[0] == 3)

                    def ahead_units(*qs):
                        if ahead:
                            for q in qs:
                                split_lo(dve, g * 6 + (base + RING + q), q % 2, (base + q) % RING)

                    def piece(r):
                        if ada_piece:
                            dve.wait_ge(piece_hi_ready, g * 8 + r + 1)
                            nc.vector.tensor_tensor(ada_lo[:, :], ada_raw[:, :], ada_hi[:, :].bitcast(F32),
                                                    ALU.subtract).then_inc(piece_lo_ready, 1)

                    def vector_half(half):
                        if ada_piece:
                            dve.wait_ge(ada_folded, g * 2 + half + 1)
                            o = g * KT + (FIRST * KT + 4 * half)
                            nc.vector.tensor_tensor(
                                ada[:, ds(o, 4), :],
                                bank[7][:, half * 4 * NSEQ:(half + 1) * 4 * NSEQ].rearrange("p (k n) -> p k n", k=4),
                                badaT[:, ds(o, 4)].unsqueeze(2).broadcast_to([P, 4, NSEQ]), ALU.add)\
                              .then_inc(ada_ready, 1)
                    for q in range(6):
                        f, c = divmod(q, NCH)
                        cols = slice(c * CH, (c + 1) * CH)
                        if q == 5:
                            vector_half(0)
                        piece(q)
                        dve.wait_ge(up_mm, g * 6 + (h0 + q + 1))
                        dve.wait_ge(silu_ready, g * 6 + (h0 + q + 1))
                        if q >= 2:
                            dve.wait_ge(h_lo_ready, g * 6 + (h0 + q - 1))
                        nc.vector.scalar_tensor_tensor(hfull[:, q % 2, :], silu[:, q % 2, :], 0.5,
                                                       bank[3 + c][:, 0:CH], ALU.mult, ALU.mult).then_inc(h_full, 1)
                        dve.wait_ge(h_hi_ready, g * 6 + (h0 + q + 1))
                        nc.vector.tensor_tensor(h_lo[:, f, cols], hfull[:, q % 2, :],
                                                h_hi[:, f, cols].bitcast(F32), ALU.subtract)\
                          .then_inc(h_lo_ready, 1)
                        if q == 2:
                            ahead_units(0, 1)
                    dve.wait_ge(h_lo_ready, g * 6 + (h0 + 6))
                    dve.wait_ge(x_written, g * 24 + xw0)
                    piece(6)
                    for c in range(NCH):
                        for o in range(KT):
                            m = c * KT + o
                            dve.wait_ge(down_mm, g * 24 + (h0 * 4 + m + 1))
                            add_gated(bank[m % RING], v_gate, o, c, g * KT + (tmp0 + o + 1), o % 2)
                            if tail and c == NCH - 1 and o >= 2:
                                if o == 2:
                                    reciprocal(tail[0], 0)
                                else:
                                    modulate(tail[0], 0, o - 3, *tail[1:])
                        if c == 0:
                            ahead_units(2, 3)
                            piece(7)
                    vector_half(1)
                    if tail:
                        for k in range(KT - 3, KT + 1):
                            modulate(tail[0], 0, k, *tail[1:])
                        if tail[0] == 3:
                            state_rows()
                            out_rows(0)
                        for c in (1, 2):
                            reciprocal(tail[0], c)
                            if c == 1:
                                dve.wait_ge(x_written, xw0 + 24 * GROUPS)
                            modulate_chunk(tail[0], c, *tail[1:])
                    ahead_units(4, 5)
                if with_ada:
                    with dve.Fori(0, LATER) as g:
                        group(g, ada_piece=True)
                    dve.wait_ge(ada_ready, FIRST + 2 * LATER)
                    for v in (SCALEM, SCALE2, SCALEF):
                        scale_gain(v)
                    with dve.Fori(LATER, GROUPS - 1) as g:
                        group(g)
                    dve.wait_ge(mod_step, 4)
                    group(GROUPS - 1, tail=(1, SHIFTM, SCALEM))
                else:
                    with dve.Fori(0, GROUPS - 1) as g:
                        group(g)
                    group(GROUPS - 1, tail=(3, SHIFTF, SCALEF, True))

            def state_rows():
                for b in range(2):
                    dve.wait_ge(rows_turned, 2 + b)
                    nc.vector.tensor_copy(tailrow[:, b * HALF:(b + 1) * HALF], bank[b][0:TAIL, :])\
                      .then_inc(tail_ready, 1)

            dve.wait_ge(x_written, XW_IN)
            first_vector(0)
            for c in range(NCH):
                reciprocal(0, c)
            first_vector(1)
            dve.wait_ge(ada_ready, 2)
            scale_gain(SCALE1)
            dve.wait_ge(mod_step, 1)
            dve.wait_ge(rg_stored, 16)
            for c in range(NCH):
                modulate_chunk(0, c, SHIFT1, SCALE1)
                if c == 0:
                    for n in range(RING):
                        split_lo(dve, n, n % 2, n % RING)
            first_vector(2)
            dve.wait_ge(ada_ready, FIRST)
            dve.wait_ge(xn_lo_ready, NCH * KT)
            ffn(U_FFN1, 0, XW_IN, 0, GATE1, True)

            for half in range(2):
                for t in range(NT):
                    dve.wait_ge(act_evicted, half * NT + t + 1)
                    nc.vector.bn_stats(bnst[:, t, half, :], v_all[:, t, half * HALF:(half + 1) * HALF])\
                      .then_inc(v_step, 1)
                for n in range(U_V + 6 + 4 * half, U_V + 10 + 4 * half):
                    split_lo(dve, n, n % 2, n % RING)
                if half == 0:
                    for w in range(2):
                        for b in range(2):
                            dve.wait_ge(ws_hi_ready, 2 * w + b + 1)
                            nc.vector.tensor_tensor(
                                ws_lo[:, w, 4 * b:4 * b + 4, :].rearrange("p h t -> p (h t)"), bank[6 + b][:, :],
                                ws_hi[:, w, 4 * b:4 * b + 4, :].rearrange("p h t -> p (h t)").bitcast(F32),
                                ALU.subtract).then_inc(ws_lo_ready, 1)
            dve.wait_ge(v_step, 2 * NT)
            for t in range(NT):
                nc.vector.bn_aggr(mv[:, t, :], bnst[:, t, :, :]).then_inc(v_step, 1)
            dve.wait_ge(vstd_ready, 1)
            nc.vector.reciprocal(vstd[:, 0:NT], vstd[:, 0:NT]).then_inc(v_step, 1)
            dve.wait_ge(v_step, 3 * NT + 1)
            dve.wait_ge(ws_loaded, 16 * (4 + NS))
            for t in range(NT + 2):
                if t < NT:
                    nc.vector.tensor_scalar(v_all[:, t, :], v_all[:, t, :], mv[:, t, 0:1], vstd[:, t:t + 1],
                                            ALU.subtract, ALU.mult).then_inc(v_step, 1)
                if 1 <= t <= NT:
                    dve.wait_ge(v_step, v_count(t - 1, 0))
                    nc.vector.tensor_tensor(v_all[:, t - 1, :], v_all[:, t - 1, :], lng[:, :], ALU.mult)\
                      .then_inc(v_step, 1)
                if t >= 2:
                    dve.wait_ge(v_step, v_count(t - 2, 1))
                    nc.vector.tensor_tensor(v_all[:, t - 2, :], v_all[:, t - 2, :], lnb[:, :], ALU.add)\
                      .then_inc(vn_ready, 1)
            nc.vector.memset(xr[:, 0:HIST], 0.0).then_inc(xr_free, 1)

            def mix(j):
                def ahead_unit(q):
                    split_lo(dve, j * 6 + (U_MIX + RING + q), q % 2, (U_MIX + q) % RING)
                xs = xr_samples(xr)
                nc.vector.tensor_copy(blk[:, :], vecT[:, V_BA:V_BA + 3 * KT].rearrange(
                    "p (v k) -> p v k", k=KT)[:, :, ds(j, 1)].rearrange("p v o -> p (v o)"))
                nc.vector.tensor_copy(xs[:, :, 0:HIST],
                                      histT[:, ds(j, 1), 0:NS * HIST].rearrange("p o (b w) -> p (o b) w", b=NS))\
                  .then_inc(xr_free, 1)
                dve.wait_ge(act_evicted, j * 21 + (2 * NT + NCH))
                dve.wait_ge(xr_free, j + 2)
                for w in range(TAPS):
                    tap = vecT[:, ds(j + (V_WCONV + w * KT), 1)]
                    if w > 0:
                        dve.wait_ge(conv_step, j * 8 + 2 * w)
                    pairs = ((xc[:, 0:SEQ], xr[:, w:w + SEQ]), (samples(xc[:, SEQ:TOK]), xs[:, :, w:w + LS]))
                    for dst, src in pairs:
                        if w == 0:
                            nc.vector.tensor_scalar(dst, src, tap, vecT[:, ds(j + V_BCONV, 1)],
                                                    ALU.mult, ALU.add).then_inc(conv_step, 1)
                        else:
                            nc.vector.scalar_tensor_tensor(dst, src, tap, dst, ALU.mult, ALU.add)\
                              .then_inc(conv_step, 1)
                tail = tails[:, ds(j, 1), :].rearrange("p o n -> p (o n)")
                nc.vector.tensor_copy(tail[:, NSEQ:NSEQ + HIST], xr[:, SEQ:SEQ + HIST])
                nc.vector.tensor_copy(tail[:, NSEQ + HIST:TAIL].rearrange("p (b w) -> p b w", b=NS),
                                      xs[:, :, LS:LS + HIST])
                ahead_unit(0)
                dve.wait_ge(xc_hi_ready, j + 1)
                nc.vector.tensor_tensor(s_lo[:, :], xc[:, :], s_hi[:, :].bitcast(F32), ALU.subtract)\
                  .then_inc(xc_lo_ready, 1)
                ahead_unit(1)
                ahead_unit(2)
                dve.wait_ge(vn_hi_ready, j + 1)
                nc.vector.tensor_tensor(s_lo[:, :], v_in[:, :], s_hi[:, :].bitcast(F32), ALU.subtract)\
                  .then_inc(vn_lo_ready, 1)
                dve.wait_ge(w_ready, j + 1)
                nc.vector.tensor_scalar(qn[:, :], ww[:, :], 1.0, -1.0, ALU.add, ALU.mult).then_inc(lru_step, 1)
                bias = bsb[:, ds(j, 1), :]
                for c in range(NCH):
                    dve.wait_ge(s_mm, j * NCH + (c + 1))
                    tiles = 3 if c < NCH - 1 else 2
                    n = tiles * P
                    ins_ = nc.vector.tensor_tensor(
                        sb[:, c % 2, 0:n].rearrange("p (t l) -> p t l", t=tiles),
                        bank[(15 + c) % RING][:, 0:n].rearrange("p (t l) -> p t l", t=tiles),
                        bias.broadcast_to([P, tiles, P]), ALU.add)
                    if c == NCH - 1:
                        ins_ = nc.vector.tensor_tensor(samples(sb[:, c % 2, n:CH]),
                                                       samples(bank[(15 + c) % RING][:, n:CH]),
                                                       bias[:, :, 0:LS].broadcast_to([P, NS, LS]), ALU.add)
                    ins_.then_inc(s_evicted, 1)
                    dve.wait_ge(s_evicted, j * NCH + (c + 1))
                    cols = slice(c * CH, (c + 1) * CH)
                    nc.vector.tensor_tensor(ug[:, cols], ug[:, cols], sb[:, c % 2, :], ALU.mult).then_inc(s_applied, 1)
                L = lambda k: dve.wait_ge(lru_step, j * 9 + k)
                L(1)
                nc.vector.reciprocal(qn[:, :], qn[:, :]).then_inc(lru_step, 1)
                nc.vector.tensor_tensor(ii[:, :], ii[:, :], xc[:, :], ALU.mult).then_inc(lru_step, 1)
                dve.wait_ge(root_ready, j + 1)
                L(2)
                nc.vector.scalar_tensor_tensor(rt[:, :], rt[:, :], -1.0, qn[:, :], ALU.mult, ALU.mult)\
                  .then_inc(lru_step, 1)
                nc.vector.scalar_tensor_tensor(ww[:, :], ww[:, :], 1.0, qn[:, :], ALU.subtract, ALU.mult)\
                  .then_inc(lru_step, 1)
                L(4)
                nc.vector.tensor_tensor(ii[:, :], ii[:, :], rt[:, :], ALU.mult).then_inc(lru_step, 1)
                L(6)
                nc.vector.tensor_tensor_scan(qn[:, 0:SEQ], ww[:, 0:SEQ], ii[:, 0:SEQ], 0.0, ALU.mult, ALU.add)\
                  .then_inc(lru_step, 1)
                for b in range(NS):
                    cols = slice(SEQ + b * LS, SEQ + (b + 1) * LS)
                    ins_ = nc.vector.tensor_tensor_scan(
                        qn[:, cols], ww[:, cols], ii[:, cols],
                        histT[:, ds(j, 1), NS * HIST + b:NS * HIST + b + 1].rearrange("p o n -> p (o n)"),
                        ALU.mult, ALU.add)
                ins_.then_inc(lru_step, 1)
                L(8)
                nc.vector.tensor_copy(tail[:, 0:1], qn[:, SEQ - 1:SEQ])
                nc.vector.tensor_copy(tail[:, 1:NSEQ],
                                      samples(qn[:, SEQ:TOK])[:, :, LS - 1:LS].rearrange("p b o -> p (b o)"))\
                  .then_inc(lru_step, 1)
                ahead_unit(3)
                for s, dst in ((0, gg), (1, ug)):
                    if s == 1:
                        dve.wait_ge(s_applied, j * NCH + NCH)
                    for c in range(NCH):
                        cols = slice(c * CH, (c + 1) * CH)
                        dve.wait_ge(act_evicted, j * 21 + (2 * NT + 16 + 3 * s + c))
                        nc.vector.tensor_tensor(dst[:, cols], dst[:, cols], sig[:, c, :], ALU.mult)\
                          .then_inc(gate_applied, 1)
                    ahead_unit(4 + s)
                dve.wait_ge(gate_applied, j * 6 + 6)
                nc.vector.tensor_tensor(gg[:, :], gg[:, :], qn[:, :], ALU.mult).then_inc(merge_step, 1)
                dve.wait_ge(merge_step, j + 1)
                dve.wait_ge(spilled, j * 16 + 16)
                nc.vector.tensor_tensor(merged[:, :], gg[:, :], ug[:, :], ALU.add).then_inc(merged_ready, 1)
            with dve.Fori(0, KT) as j:
                mix(j)

            for k in range(KT):
                dve.wait_ge(m_hi_ready, k + 1)
                nc.vector.tensor_tensor(xn_lo[:, k, :], merged_in[:, k, :], xn_hi[:, k, :].bitcast(F32),
                                        ALU.subtract).then_inc(m_lo_ready, 1)
            dve.wait_ge(x_back, 16)
            for p in range(KT // 2):
                dve.wait_ge(out_mm, p + 1)
                for o in range(2):
                    for c in range(NCH):
                        add_gated(bank[3 * o + c], GATEM, 2 * p + o, c, KT * GROUPS + 2 * p + o + 1, o)
                for n in (U_OUT + 2 * p + 6, U_OUT + 2 * p + 7):
                    if p < KT // 2 - 1:
                        split_lo(dve, n, n % 2, n % RING)
            dve.wait_ge(x_written, XW_OUT)
            for c in range(NCH):
                reciprocal(2, c)
            for c in range(NCH):
                modulate_chunk(2, c, SHIFT2, SCALE2)
                if c == 0:
                    for n in (U_OUT + 12, U_OUT + 13):
                        split_lo(dve, n, n % 2, n % RING)
            dve.wait_ge(xn_lo_ready, 3 * NCH * KT)
            ffn(U_FFN2, 6 * GROUPS, XW_OUT, KT * GROUPS + KT, GATE2, False)

        @block.tensor
        def _(pe):
            pe.wait_ge(rows_loaded, 16 * 13)
            pe.wait_ge(const_ready, 1)
            pe.wait_ge(c_silu, 1)
            nc.tensor.transpose(bank[6][:, 0:NVEC], vrow[:, :], ident[0:NVEC, 0:NVEC])
            nc.tensor.transpose(bank[6][:, 128:128 + NADA], brow[:, :], ident[0:NADA, 0:NADA])
            for k in range(KT):
                nc.tensor.transpose(bank[7][:, 256 + k * 32:256 + (k + 1) * 32], hrow[:, k * P:(k + 1) * P],
                                    ident[0:32, 0:32])
                last = nc.tensor.transpose(bank[7][:, k * NSEQ:(k + 1) * NSEQ], csil[:, k * P:(k + 1) * P],
                                           ident[0:NSEQ, 0:NSEQ])
            last.then_inc(rows_turned, 1)
            def x_turn(t):
                pe.wait_ge(x_loaded, 48 * (t + 1))
                for s in range(3):
                    for b in range(2):
                        if t > 0:
                            pe.wait_ge(x_written, 6 * (t - 1) + 2 * s + b + 1)
                        for k in range(4):
                            last = nc.tensor.transpose(bank[2 * s + b][:, k * P:(k + 1) * P],
                                                       xrow[:, s, (4 * b + k) * P:(4 * b + k + 1) * P], ident[:, :])
                        last.then_inc(x_turned, 1)
            def first_vector(v):
                pe.wait_ge(ada_loaded[v % 2], 16 * (v // 2 + 1))
                for o in range(KT):
                    for k in range(KT):
                        last = nc.tensor.matmul(bank[3 + v][:, o * NSEQ:(o + 1) * NSEQ],
                                                w_ada_sb[:, v % 2, k, o * P:(o + 1) * P], cT[:, k, 0:NSEQ],
                                                start=k == 0, stop=k == KT - 1)
                last.then_inc(ada_mm, 1)

            def sums(i, c):
                pos = max(p for p, (cc, _) in enumerate(squares_order(i)) if cc == c)
                pe.wait_ge(acc_added, added(i, pos + 1))
                if c == 2:
                    pe.wait_ge(std_ready, i * NCH + 1)
                nc.tensor.matmul(bank[6 + c % 2][:, 0:CH], ones[:, :], acc[:, c, :], start=True, stop=True)\
                  .then_inc(sumsq_mm, 1)

            pe.wait_ge(rows_copied, 1)
            for t in range(3):
                x_turn(t)
            pe.wait_ge(x_written, XW_IN)
            first_vector(0)
            for c in range(NCH):
                sums(0, c)
            first_vector(1)
            first_vector(2)

            def column_job(out, slot, cols, mov_hi, mov_lo):
                for k in range(KT):
                    last = product(pe, out, w_hi[:, slot, k * P:(k + 1) * P], w_lo[:, slot, k * P:(k + 1) * P],
                                   mov_hi[:, k, cols], mov_lo[:, k, cols], k == 0, k == KT - 1)
                return last

            def ffn(i, base, h0, xw0, with_ada):
                def group(g, ada_piece=False, first=False, tail=None):
                    n = g * 6 + base

                    def piece(r):
                        if not ada_piece:
                            return
                        pe.wait_ge(piece_lo_ready, g * 8 + r + 2)
                        for kk in range(2):
                            for part in (ada_hi, ada_lo):
                                k = 2 * (r % 4) + kk
                                last = nc.tensor.matmul(bank[6][0:2 * NSEQ, :], c_parts[:, k, :],
                                                        part[:, kk * HALF:(kk + 1) * HALF],
                                                        start=k == 0 and part is ada_hi,
                                                        stop=k == KT - 1 and part is ada_lo,
                                                        skip_group_check=True)
                        last.then_inc(ada_mm, 1)

                    def fold_half(half):
                        if not ada_piece:
                            return
                        pe.wait_ge(ada_row_ready, g * 2 + half + 1)
                        for b in range(4):
                            o = (4 * half + b) * NSEQ
                            last = nc.tensor.matmul(bank[7][:, o:o + NSEQ], ada_row[:, b * P:(b + 1) * P], fold[:, :],
                                                    start=True, stop=True)
                        last.then_inc(ada_folded, 1)
                    for f in range(2):
                        for c in range(NCH):
                            pe.wait_ge(xn_lo_ready, (i * NCH + c + 1) * KT)
                            for u, done in ((0, gate_mm), (1, up_mm)):
                                q = 2 * f + u
                                pe.wait_ge(w_lo_ready, n + (q + 1))
                                b = 3 * u + c
                                if f == 0:
                                    pe.wait_ge(x_written, g * 24 + (xw0 - 5 + b))
                                elif u == 0:
                                    pe.wait_ge(silu_ready, g * 6 + (h0 + c + 1))
                                else:
                                    pe.wait_ge(h_full, g * 6 + (h0 + c + 1))
                                column_job(bank[b][:, 0:CH], (base + q) % RING, slice(c * CH, (c + 1) * CH),
                                           xn_hi, xn_lo).then_inc(done, 1)
                            piece(NCH * f + c)
                            if NCH * f + c == 4:
                                fold_half(0)
                    pe.wait_ge(w_lo_ready, n + 6)
                    for c in range(NCH):
                        pe.wait_ge(h_lo_ready, g * 6 + (h0 + NCH + c + 1))
                        for o in range(KT):
                            m = c * KT + o
                            if m < 3:
                                pe.wait_ge(silu_ready, g * 6 + (h0 + 3 + m + 1))
                            elif m < 6:
                                pe.wait_ge(h_full, g * 6 + (h0 + m + 1))
                            else:
                                pe.wait_ge(x_written, g * 24 + (xw0 + m - 5))
                            for f in range(2):
                                slot = (base + 4 + f) % RING
                                cols = slice(c * CH, (c + 1) * CH)
                                last = product(pe, bank[m % RING][:, 0:CH], w_hi[:, slot, o * P:(o + 1) * P],
                                               w_lo[:, slot, o * P:(o + 1) * P], h_hi[:, f, cols],
                                               h_lo[:, f, cols], f == 0, f == 1)
                            last.then_inc(down_mm, 1)
                            if tail is not None and c == NCH - 1 and o == 1:
                                sums(tail, 0)
                        if c < NCH - 1:
                            piece(6 + c)
                    fold_half(1)
                    if tail is not None:
                        sums(tail, 1)
                if with_ada:
                    with pe.Fori(0, LATER) as g:
                        group(g, ada_piece=True)
                    with pe.Fori(LATER, GROUPS - 1) as g:
                        group(g)
                    group(GROUPS - 1, tail=1)
                else:
                    with pe.Fori(0, GROUPS - 1) as g:
                        group(g)
                    group(GROUPS - 1, tail=3)

            ffn(0, U_FFN1, 0, XW_IN, True)

            for half in range(2):
                for t in range(NT):
                    m = half * NT + t
                    pe.wait_ge(xn_lo_ready, (NCH + t // NCH + 1) * KT)
                    if m >= RING:
                        pe.wait_ge(act_evicted, m + 1 - RING)
                    else:
                        pe.wait_ge(x_written, XW_FFN1)
                    cols = slice(t * P, (t + 1) * P)
                    for k in range(KT):
                        n = U_V + 4 * half + k // 2
                        if t == 0 and k % 2 == 0:
                            pe.wait_ge(w_lo_ready, n + 1)
                        w = slice((k % 2) * HALF, (k % 2 + 1) * HALF)
                        last = product(pe, bank[m % RING][:, :], xn_hi[:, k, cols], xn_lo[:, k, cols],
                                       w_hi[:, n % RING, w], w_lo[:, n % RING, w], k == 0, k == KT - 1)
                    last.then_inc(v_mm, 1)
                    if m == 1:
                        sums(1, 2)
                if half == 0:
                    for w, src in enumerate((ws_raw, wd_raw)):
                        pe.wait_ge(ws_masked, w + 1)
                        for b in range(2):
                            if w == 1:
                                pe.wait_ge(ws_lo_ready, b + 1)
                            for h in range(4):
                                last = nc.tensor.transpose(bank[6 + b][:, h * P:(h + 1) * P], src[:, 4 * b + h, :],
                                                           ident[:, :])
                            last.then_inc(ws_turned, 1)
            pe.wait_ge(ws_lo_ready, 4)

            def mix(j):
                def free(m):
                    if m < 21:
                        pe.wait_ge(act_evicted, j * 21 + (13 + m))
                    else:
                        pe.wait_ge(s_evicted, j * NCH + (m - 20))

                def section(m, q):
                    pe.wait_ge(w_lo_ready, j * 6 + (U_MIX + q + 1))
                    for c in range(NCH):
                        free(m + c)
                        column_job(bank[(m + c) % RING][:, 0:CH], (U_MIX + q) % RING,
                                   slice(c * CH, (c + 1) * CH), xn_hi, xn_lo).then_inc(mix_mm, 1)
                section(0, 0)
                section(3, 1)
                section(6, 2)
                pe.wait_ge(w_lo_ready, j * 6 + (U_MIX + 4))
                pe.wait_ge(xc_lo_ready, j + 1)
                slot = (U_MIX + 3) % RING
                for c in range(NCH):
                    cols = slice(c * CH, (c + 1) * CH)
                    for g in range(2):
                        m = 9 + 2 * c + g
                        free(m)
                        w = slice(g * P, (g + 1) * P)
                        product(pe, bank[m % RING][:, 0:CH], w_hi[:, slot, w], w_lo[:, slot, w], s_hi[:, cols],
                                s_lo[:, cols], True, True).then_inc(mix_mm, 1)
                pe.wait_ge(vn_lo_ready, j + 1)
                for c in range(NCH):
                    free(15 + c)
                    for s in range(3):
                        t = 3 * c + s
                        cols = slice(t * P, (t + 1) * P)
                        w = int(t == NT - 1)
                        last = product(pe, bank[(15 + c) % RING][:, s * P:(s + 1) * P], s_hi[:, cols], s_lo[:, cols],
                                       ws_hi[:, w, ds(j, 1), :].rearrange("p o t -> p (o t)"),
                                       ws_lo[:, w, ds(j, 1), :].rearrange("p o t -> p (o t)"), True, True)
                    last.then_inc(s_mm, 1)
                section(18, 4)
                section(21, 5)
            with pe.Fori(0, KT) as j:
                mix(j)

            pe.wait_ge(act_evicted, 2 * NT + 21 * KT)
            for p in range(KT // 2):
                pe.wait_ge(w_lo_ready, U_OUT + 2 * p + 2)
                for k in range(KT):
                    pe.wait_ge(m_lo_ready, k + 1)
                    for o in range(2):
                        slot = (U_OUT + 2 * p + o) % RING
                        rows = slice(k * P, (k + 1) * P)
                        for c in range(NCH):
                            if p > 0 and k == 0:
                                pe.wait_ge(x_written, XW_FFN1 + 6 * (p - 1) + 3 * o + c + 1)
                            cols = slice(c * CH, (c + 1) * CH)
                            last = product(pe, bank[3 * o + c][:, 0:CH], w_hi[:, slot, rows], w_lo[:, slot, rows],
                                           xn_hi[:, k, cols], xn_lo[:, k, cols], k == 0, k == KT - 1)
                last.then_inc(out_mm, 1)
            for c in range(NCH):
                sums(2, c)
            ffn(2, U_FFN2, 6 * GROUPS, XW_OUT, False)
            pe.wait_ge(x_written, XW_FFN2)
            for b in range(2):
                for k in range(4):
                    last = nc.tensor.transpose(bank[b][0:TAIL, k * P:(k + 1) * P], tails[:, 4 * b + k, :], ident[:, :])
                last.then_inc(rows_turned, 1)
            for c in range(NCH):
                pe.wait_ge(xf_ready, (3 * NCH + c + 1) * KT)
                if c == NCH - 1:
                    pe.wait_ge(xs_step, 2 * KT * 4)
                for s in range(3):
                    t = 3 * c + s
                    for b in range(2):
                        m = 2 * t + b
                        if t == 0:
                            pe.wait_ge(tail_ready, b + 1)
                        if m >= RING:
                            pe.wait_ge(yrow_dve if b else yrow_act, t - 2)
                        for k in range(4):
                            last = nc.tensor.transpose(bank[m % RING][:, k * P:(k + 1) * P],
                                                       yT[:, 4 * b + k, s * P:(s + 1) * P], ident[:, :])
                        last.then_inc(y_turned, 1)
                if c == 0:
                    sums(3, 2)
    return nc


_OUTS = (("y_prompt", (1, SEQ, D)), ("y_sample", (NS, LS, D)), ("conv_prompt", (1, 1, HIST, D)),
         ("rglru_prompt", (1, 1, D)), ("sgu_v_prompt", (1, 1, P, D)), ("conv_sample", (1, NS, HIST, D)),
         ("rglru_sample", (1, NS, D)), ("sgu_v_sample", (1, NS, LS, D)))


def kernel(**inputs):
    import concourse.bacc as bacc
    from concourse.bass_utils import run_bass_kernel_spmd

    nc = bacc.Bacc("TRN2", target_bir_lowering=False, num_devices=1, dynamic_dma_scratch_size=1024)
    arrays, ins, outs = {}, {}, {}
    for name, a in inputs.items():
        arrays[f"in_{name}"] = np.ascontiguousarray(a)
        ins[name] = nc.dram_tensor(f"in_{name}", a.shape, F32, kind="ExternalInput").ap()
    for name, shape in _OUTS:
        outs[name] = nc.dram_tensor(f"out_{name}", shape, F32, kind="ExternalOutput").ap()
    build(nc, ins, outs)
    r = run_bass_kernel_spmd(nc, [arrays], core_ids=[0])
    return tuple(r.results[0][f"out_{name}"] for name, _ in _OUTS)
```

```python
import numpy as np
import concourse.bass as bass
from concourse import mybir

F32 = mybir.dt.float32
F32R = mybir.dt.float32r
ALU = mybir.AluOpType
ACT = mybir.ActivationFunctionType
ds = bass.ds

P = 128
D = 1024
KT = D // P
SEQ = 1024
NS, LS = 8, 16
NSEQ = 1 + NS
TOK = SEQ + NS * LS
CH = 384
NCH = TOK // CH
PC2 = SEQ - 2 * CH
NT = TOK // P
WS_AFTER = NT + 4
SPATIAL = -(-NT // 2)
S_BANKS = (6, 7, 0, 1, 2)
DFF = 2816
NF = DFF // P
GROUPS = NF // 2
TAPS = 4
HIST = TAPS - 1
EPS = 1e-6
FIRST = 3
LATER = 11 - FIRST
UNIT = D
RING = 6
NADA = 11 * KT
HALF = D // 2
TAIL = NSEQ + HIST * NSEQ

U_FFN1 = 0
U_V = U_FFN1 + 6 * GROUPS
U_MIX = U_V + 8
U_OUT = U_MIX + 6 * KT
U_FFN2 = U_OUT + 8
U_END = U_FFN2 + 6 * GROUPS

SHIFT1, SCALE1, GATE1, SHIFTM, SCALEM, GATEM, SHIFT2, SCALE2, GATE2, SHIFTF, SCALEF = range(11)
FIRST_HALVES = [(v, half) for v in (SCALE1, SHIFT1, GATE1) for half in range(2)]
V_G1, V_GM, V_G2, V_GF, V_BCONV, V_WCONV, V_BA, V_BX, V_LAM = 0, 8, 16, 24, 32, 40, 72, 80, 88
NVEC = 96

XW_IN = 2 * NT
XW_FFN1 = XW_IN + 24 * GROUPS
XW_OUT = XW_FFN1 + 24
XW_FFN2 = XW_OUT + 24 * GROUPS


def build(nc, ins, outs):
    cursor = [1152]

    def at(name, shape, dtype=F32, offset=None):
        size = 4 * int(np.prod(shape[1:]))
        if offset is None:
            offset = cursor[0]
            cursor[0] += -(-size // 32) * 32
        return nc.alloc_sbuf_tensor_at(name, shape, dtype, offset=offset, align_bytes=32)

    ident = at("ident", [P, P])
    ones = at("ones", [P, P])
    ada = at("ada", [P, NADA, NSEQ])
    vecT = at("vecT", [P, NVEC])
    badaT = at("badaT", [P, NADA])
    cT = at("cT", [P, KT, NSEQ + 1])
    histT = at("histT", [P, KT, 32])
    blk = at("blk", [P, 3])
    epst = at("epst", [P, 8])
    tails = at("tails", [P, KT, TAIL])
    mv = at("mv", [P, NT, 2])
    vstd = at("vstd", [P, NT + 1])
    bnst = at("bnst", [P, NT, 2, 6])
    raw_at = cursor[0]
    raw = at("raw", [P, 2, UNIT])
    ring_at = cursor[0]
    w_hi = at("w_hi", [P, RING, UNIT], F32R)
    w_lo = at("w_lo", [P, RING, UNIT], F32R)
    xn_at = cursor[0]
    xn_hi = at("xn_hi", [P, KT, TOK], F32R)
    xn_lo = at("xn_lo", [P, KT, TOK], F32R)
    region = cursor[0]

    x = at("x", [P, KT, TOK])
    h_at = cursor[0]
    h_hi = at("h_hi", [P, 2, TOK], F32R)
    h_lo = at("h_lo", [P, 2, TOK], F32R)
    silu = at("silu", [P, 2, CH])
    hfull = at("hfull", [P, 2, CH])
    sq = at("sq", [P, 3, CH])
    acc = at("acc", [P, NCH, CH])
    gtmp = at("gtmp", [P, 2, P])
    ada_raw = at("ada_raw", [P, UNIT])
    ada_hi = at("ada_hi", [P, UNIT], F32R)
    ada_lo = at("ada_lo", [P, UNIT], F32R)
    ada_row = at("ada_row", [2 * NSEQ, HALF])
    c_parts = at("c_parts", [P, KT, 2 * NSEQ], F32R)
    fold = at("fold", [2 * NSEQ, NSEQ])
    end_ffn = cursor[0]
    tbuf, xfull = silu, hfull
    yT = at("yT", [P, NCH, KT, CH], offset=xn_at)
    yrow = at("yrow", [P, NT, D], offset=xn_at + 4 * NCH * KT * CH)
    tailrow = at("tailrow", [TAIL, D], offset=raw_at)
    w_ada_sb = at("w_ada_sb", [P, 4, KT, HALF], offset=xn_at)
    rg_sb = at("rg_sb", [P, KT, 2, P], offset=xn_at + 8 * KT * D)
    first = [ring_at]

    def over_ring(name, shape):
        offset = first[0]
        first[0] += 4 * int(np.prod(shape[1:]))
        assert first[0] <= xn_at
        return at(name, shape, offset=offset)
    xrow = over_ring("xrow", [P, NT, D])
    vrow = over_ring("vrow", [NVEC, P])
    brow = over_ring("brow", [NADA, P])
    crow = over_ring("crow", [NSEQ, D])
    hrow = over_ring("hrow", [32, D])
    spw = over_ring("spw", [P, 6, KT])

    cursor[0] = region
    bsb = at("bsb", [P, KT, P])
    ws_parts = at("ws_parts", [P, 2, KT, 2, P], F32R)
    xr = at("xr", [P, HIST + SEQ + NS * (HIST + LS) + 1])
    v_at = cursor[0]
    gg = at("gg", [P, TOK])
    ug = at("ug", [P, TOK])
    ww = at("ww", [P, TOK])
    ii = at("ii", [P, TOK])
    qn = at("qn", [P, TOK])
    rt = at("rt", [P, TOK])
    v_in = at("v_in", [P, TOK])
    sig = at("sig", [P, NCH, CH])
    merged = at("merged", [P, TOK])
    sb = at("sb", [P, 2, 2 * P])
    v_end = cursor[0] = v_at + 4 * (NT * D + 2 * D)
    v_all = at("v_all", [P, NT, D], offset=v_at)
    lng = at("lng", [P, D], offset=v_at + 4 * NT * D)
    lnb = at("lnb", [P, D], offset=v_at + 4 * (NT + 1) * D)
    xc = at("xc", [P, TOK])
    s_hi = at("s_hi", [P, TOK], F32R)
    s_lo = at("s_lo", [P, TOK], F32R)
    spare_at = cursor[0]
    ws_raw = at("ws_raw", [P, KT, P], offset=spare_at)
    wd_raw = at("wd_raw", [P, KT, P], offset=v_end + 4 * TOK)
    ii_at, rt_at, v_in_at = (v_at + 4 * TOK * b for b in (3, 5, 6))
    xc_at, s_hi_at, s_lo_at = (v_end + 4 * TOK * b for b in range(3))
    assert ii_at >= region + 4 * KT * TOK
    merged_in = [at(f"merged_in{k}", [P, TOK], offset=offset)
                 for k, offset in enumerate((spare_at, v_in_at, xc_at, s_hi_at, s_lo_at, rt_at, ii_at))] + [merged]
    assert max(end_ffn, spare_at + 4 * TOK) <= nc.sbuf_usable_end

    bank = [nc.alloc_psum_tensor(f"bank{i}", [P, 512], F32) for i in range(8)]

    x_dram = nc.dram_tensor("x_dram", [P, KT, TOK], F32).ap()
    vn_dram = nc.dram_tensor("vn_dram", [NT, P, D], F32).ap()
    merged_dram = nc.dram_tensor("merged_dram", [KT, P, TOK], F32).ap()
    rg_dram = nc.dram_tensor("rg_dram", [KT, P, 2 * P], F32).ap()

    def sem(name):
        return nc.alloc_semaphore(name)

    raw_loaded = [sem(f"raw_loaded{i}") for i in range(2)]
    ada_loaded = [sem(f"ada_loaded{i}") for i in range(4)]
    piece_loaded = sem("piece_loaded")
    c_loaded = sem("c_loaded")
    x_loaded = [sem(f"x_loaded{i}") for i in range(3)]
    rows_loaded = sem("rows_loaded")
    rg_loaded = sem("rg_loaded")
    rg_stored = sem("rg_stored")
    ws_loaded = sem("ws_loaded")
    spilled = sem("spilled")
    vn_stored = [sem(f"vn_stored{b}") for b in range(3)]
    v_loaded = sem("v_loaded")
    x_back = sem("x_back")
    merged_back = [sem(f"merged_back{k}") for k in range(KT - 1)]
    y_stored = sem("y_stored")
    state_stored = sem("state_stored")
    rows_turned = sem("rows_turned")
    x_turned = sem("x_turned")
    ada_mm = sem("ada_mm")
    ada_folded = sem("ada_folded")
    sumsq_mm = sem("sumsq_mm")
    gate_mm = sem("gate_mm")
    up_mm = sem("up_mm")
    down_mm = sem("down_mm")
    v_mm = sem("v_mm")
    ws_turned = sem("ws_turned")
    mix_mm = sem("mix_mm")
    s_mm = sem("s_mm")
    out_mm = sem("out_mm")
    y_turned = sem("y_turned")
    w_hi_ready = sem("w_hi_ready")
    c_silu = sem("c_silu")
    sp_exp = sem("sp_exp")
    squared = sem("squared")
    std_ready = sem("std_ready")
    xf_ready = sem("xf_ready")
    piece_hi_ready = sem("piece_hi_ready")
    ada_row_ready = sem("ada_row_ready")
    xn_hi_ready = sem("xn_hi_ready")
    silu_ready = sem("silu_ready")
    h_hi_ready = sem("h_hi_ready")
    act_evicted = sem("act_evicted")
    vstd_ready = sem("vstd_ready")
    ws_hi_ready = sem("ws_hi_ready")
    xc_hi_ready = sem("xc_hi_ready")
    vn_hi_ready = sem("vn_hi_ready")
    w_ready = sem("w_ready")
    root_ready = sem("root_ready")
    m_hi_ready = sem("m_hi_ready")
    yrow_act = sem("yrow_act")
    w_lo_ready = sem("w_lo_ready")
    rows_copied = sem("rows_copied")
    ada_ready = sem("ada_ready")
    piece_lo_ready = sem("piece_lo_ready")
    sp_step = sem("sp_step")
    mod_step = sem("mod_step")
    x_written = sem("x_written")
    rstd_ready = sem("rstd_ready")
    t_ready = sem("t_ready")
    xs_step = sem("xs_step")
    xn_lo_ready = sem("xn_lo_ready")
    h_full = sem("h_full")
    h_lo_ready = sem("h_lo_ready")
    gated_tmp = sem("gated_tmp")
    v_stats = sem("v_stats")
    v_moments = sem("v_moments")
    v_rstd = sem("v_rstd")
    v_centred = sem("v_centred")
    v_scaled = sem("v_scaled")
    vn_ready = sem("vn_ready")
    ws_lo_ready = sem("ws_lo_ready")
    xr_free = sem("xr_free")
    conv_step = sem("conv_step")
    xc_lo_ready = sem("xc_lo_ready")
    vn_lo_ready = sem("vn_lo_ready")
    s_step = sem("s_step")
    s_evicted = sem("s_evicted")
    s_applied = sem("s_applied")
    lru_step = sem("lru_step")
    gate_applied = sem("gate_applied")
    merge_step = sem("merge_step")
    merged_ready = sem("merged_ready")
    m_lo_ready = sem("m_lo_ready")
    yrow_dve = sem("yrow_dve")
    tail_ready = sem("tail_ready")
    const_ready = sem("const_ready")
    acc_added = sem("acc_added")
    const_step = sem("const_step")
    rg_zeroed = sem("rg_zeroed")
    wd_zeroed = sem("wd_zeroed")
    inputs_gated = sem("inputs_gated")
    branch_gated = sem("branch_gated")
    ws_masked = sem("ws_masked")

    def samples(ap):
        return ap.rearrange("p (b l) -> p b l", b=NS)

    def per_sample(v, k):
        return ada[:, v * KT + k, 1:NSEQ].unsqueeze(2).broadcast_to([P, NS, LS])

    def prompt_scalar(v, k):
        return ada[:, v * KT + k, 0:1]

    def split_hi(act, n, par, slot):
        act.wait_ge(raw_loaded[par], raw_count(n, par))
        nc.scalar.activation(w_hi[:, slot, :], raw[:, par, :], ACT.Copy).then_inc(w_hi_ready, 1)

    def split_lo(dve, n, par, slot):
        dve.wait_ge(w_hi_ready, n + 1)
        nc.vector.tensor_tensor(w_lo[:, slot, :], raw[:, par, :], w_hi[:, slot, :].bitcast(F32),
                                ALU.subtract).then_inc(w_lo_ready, 1)

    def raw_count(n, par):
        if isinstance(n, int):
            return 16 * (n // 2 + 1)
        return n * 8 + (16 - 8 * par)

    def product(pe, out, hi, lo, mov_hi, mov_lo, first, last):
        nc.tensor.matmul(out, hi, mov_hi, start=first, stop=False, skip_group_check=True)
        nc.tensor.matmul(out, hi, mov_lo, start=False, stop=False, skip_group_check=True)
        return nc.tensor.matmul(out, lo, mov_hi, start=False, stop=last, skip_group_check=True)

    def squares_order(i):
        if i == 2:
            return ([(c, k) for k in range(KT - 2) for c in range(NCH)]
                    + [(c, k) for c in range(NCH) for k in (KT - 2, KT - 1)])
        return [(c, k) for c in range(NCH) for k in range(KT)]

    def added(i, pos):
        return i * NCH * (KT - 1) + sum(k > 0 for _, k in squares_order(i)[:pos])

    def residual_written(i, c, k):
        if i == 0:
            return 6 * (c + 1)
        if i == 2:
            if k >= KT - 2:
                return XW_OUT - 6 + 2 * c + k % 2 + 1
            return XW_FFN1 + 6 * (k // 2) + 3 * (k % 2) + c + 1
        return (XW_FFN1 if i == 1 else XW_FFN2) - KT * (NCH - c) + k + 1

    def columns(w, col, width=P):
        return w.rearrange("(k p) n -> p k n", p=P)[:, :, ds(col, width)]

    def add_squares(pool, i):
        for pos, (c, k) in enumerate(squares_order(i)):
            if k == 0:
                continue
            pool.wait_ge(squared, i * NCH * KT + pos + 1)
            if added(i, pos):
                pool.wait_ge(acc_added, added(i, pos))
            nc.gpsimd.tensor_tensor(acc[:, c, :], acc[:, c, :], sq[:, pos % 3, :], ALU.add).then_inc(acc_added, 1)

    def tile_rows(sp, t):
        rows = ins["x_prompt"].rearrange("b (n s) d -> s (b n) d", s=P)
        prompt = min(3 * t + 3, NT - 1)
        sp.dma_start(xrow[:, 3 * t:prompt, :], rows[:, 3 * t:prompt, :]).then_inc(x_loaded[t], 16)
        if prompt < 3 * t + 3:
            sp.dma_start(xrow[:, NT - 1, :], ins["x_sample"].rearrange("b s d -> (b s) d")).then_inc(x_loaded[t], 16)

    def xr_samples(t):
        return t[:, HIST + SEQ:HIST + SEQ + NS * (HIST + LS)].rearrange("p (b l) -> p b l", b=NS)

    block = nc.Block()
    with block:

        @block.sync
        def _(sp):
            def unit(n, par, src, dst=None):
                if not isinstance(n, int) or n >= 2:
                    sp.wait_ge(w_lo_ready, n - 1)
                dst = raw[:, par, :] if dst is None else dst
                sp.dma_start(dst, src).then_inc(raw_loaded[par], 16)

            def wide(par):
                return raw[:, par, :].rearrange("p (k n) -> p k n", k=KT)

            sp.dma_start(crow[0:1, :], ins["c_prompt"]).then_inc(c_loaded, 16)
            sp.dma_start(crow[1:NSEQ, :], ins["c_sample"]).then_inc(c_loaded, 16)
            w_ada = ins["w_ada"].rearrange("o k n -> (o k) n")
            for t in range(3):
                tile_rows(sp, t)

            def ada_half(n):
                v, half = FIRST_HALVES[n]
                if n >= 4:
                    sp.wait_ge(ada_mm, n - 3)
                sp.dma_start(w_ada_sb[:, n % 4], columns(w_ada, v * D + half * HALF, HALF))\
                  .then_inc(ada_loaded[n % 4], 16)
            sp.wait_ge(x_loaded[1], 16)
            gate_up = [ins[f"w_ffn1_{w}"].rearrange("o k n -> (o k) n") for w in ("gate", "up")]
            ada_half(0)
            ada_half(1)
            unit(0, 0, columns(gate_up[0], 0), wide(0))
            unit(1, 1, columns(gate_up[1], 0), wide(1))
            ada_half(2)
            ada_half(3)
            ada_half(4)
            ada_half(5)
            sp.wait_ge(rg_loaded, 64)
            sp.dma_start(rg_dram.rearrange("k p n -> p k n"),
                         rg_sb[:, :, :, :].rearrange("p k g n -> p k (g n)")).then_inc(rg_stored, 16)
            unit(2, 0, columns(gate_up[0], P), wide(0))
            unit(3, 1, columns(gate_up[1], P), wide(1))

            def ffn_units(base, name):
                gate, up, down = (ins[f"w_{name}_{w}"].rearrange("o k n -> (o k) n") for w in ("gate", "up", "down"))

                def group(g, ada_cols=None):
                    n = base + g * 6
                    col = g * (2 * P)

                    def units(*qs):
                        for q in qs:
                            f = (q // 2) % 2 if q < 4 else q - 4
                            if q >= 4:
                                unit(n + q, f, down[ds(col + f * P, P), :])
                            else:
                                unit(n + q, q % 2, columns((gate, up)[q % 2], col + f * P), wide(q % 2))

                    def pieces(*rs):
                        if ada_cols is None:
                            return
                        w, first, c0 = ada_cols
                        for r in rs:
                            sp.wait_ge(piece_lo_ready, g * 8 + r + 1)
                            src = w.rearrange("(k p) n -> p k n", p=P)[:, 2 * (r % 4):2 * (r % 4) + 2,
                                                                      ds((g - first) * D + c0 + (r // 4) * HALF, HALF)]
                            sp.dma_start(ada_raw[:, :].rearrange("p (k n) -> p k n", k=2), src)\
                              .then_inc(piece_loaded, 16)
                    return units, pieces

                def ahead(g, ada_cols=None):
                    units, _ = group(g + 1)
                    _, pieces = group(g, ada_cols)
                    pieces(0, 1)
                    units(0, 1)
                    pieces(2, 3, 4, 5)
                    units(2, 3)
                    pieces(6, 7)
                    units(4, 5)
                group(0)[0](*range(4 if base == 0 else 0, 6))
                if base == 0:
                    with sp.Fori(0, 9 - FIRST) as g:
                        ahead(g, (w_ada, 0, FIRST * D))
                    with sp.Fori(9 - FIRST, LATER) as g:
                        ahead(g, (ins["w_ada_final"], 9 - FIRST, 0))
                    with sp.Fori(LATER, GROUPS - 1) as g:
                        ahead(g)
                else:
                    with sp.Fori(0, GROUPS - 1) as g:
                        ahead(g)

            ffn_units(U_FFN1, "ffn1")

            w_in = ins["w_in"].rearrange("o k n -> (o k) n")
            w_v = w_in.rearrange("(k p) n -> p k n", p=P)
            for q in range(8):
                half, kp = divmod(q, 4)
                unit(U_V + q, q % 2, w_v[:, 2 * kp:2 * kp + 2, 3 * D + half * HALF:3 * D + (half + 1) * HALF],
                     raw[:, q % 2, :].rearrange("p (k n) -> p k n", k=2))
                if q == 5:
                    sp.wait_ge(x_written, XW_FFN1)
                    sp.dma_start(x_dram, x[:, :, :]).then_inc(spilled, 16)
                    sp.wait_ge(t_ready, 2 * NCH * KT)
                    sp.wait_ge(xn_lo_ready, 2 * NCH * KT)
                    sp.wait_ge(spilled, 16)
                    sp.dma_start(lng[:, :], ins["ln_v_g"].broadcast_to([P, D])).then_inc(ws_loaded, 16)
                    sp.dma_start(lnb[:, :], ins["ln_v_b"].broadcast_to([P, D])).then_inc(ws_loaded, 16)
                    sp.dma_start(bsb[:, :, :].rearrange("p h t -> p (h t)"),
                                 ins["b_spatial"].rearrange("o h t -> o (h t)").broadcast_to([P, D]))\
                      .then_inc(ws_loaded, 16)
                    sp.dma_start(ws_raw[:, :, :], ins["w_spatial"].rearrange("o h t s -> t (o h) s"))\
                      .then_inc(ws_loaded, 16)
                    sp.wait_ge(wd_zeroed, 1)
                    for b in range(NS):
                        sp.dma_start(wd_raw[b * LS:(b + 1) * LS, :, b * LS:(b + 1) * LS],
                                     ins["w_spatial"].rearrange("o h t s -> t (o h) s")[0:LS, :, 0:LS])\
                          .then_inc(ws_loaded, 16)

            def mix_units(j):
                n = U_MIX + j * 6
                for q, sec in ((0, 0), (1, 1), (2, 2)):
                    unit(n + q, q % 2, columns(w_in, sec * D + j * P), wide(q % 2))
                if not isinstance(j, int) or j > 0:
                    sp.wait_ge(vn_lo_ready, j)
                sp.dma_start(v_in[:, :].rearrange("p (t c) -> p t c", t=NT),
                             vn_dram.rearrange("t p n -> p t n")[:, :, ds(j * P, P)]).then_inc(v_loaded, 16)
                unit(n + 3, 1, rg_dram.rearrange("k p n -> (k p) n")[ds(j * P, P), :], raw[:, 1, 0:2 * P])
                for q, sec in ((4, 4), (5, 5)):
                    unit(n + q, q % 2, columns(w_in, sec * D + j * P), wide(q % 2))

            def store_merged(j):
                sp.wait_ge(merged_ready, j + 1)
                sp.dma_start(merged_dram.rearrange("k p n -> (k p) n")[ds(j * P, P), :],
                             merged[:, :]).then_inc(spilled, 16)

            n = U_MIX
            for q, sec in ((0, 0), (1, 1), (2, 2)):
                unit(n + q, q % 2, columns(w_in, sec * D), wide(q % 2))
            sp.wait_ge(rg_stored, 16)
            unit(n + 3, 1, rg_dram[0], raw[:, 1, 0:2 * P])

            def store_vn(b):
                sp.wait_ge(vn_ready, 3 * b + 3)
                sp.dma_start(vn_dram.rearrange("t p n -> p t n")[:, 3 * b:3 * b + 3, :], v_all[:, 3 * b:3 * b + 3, :])\
                  .then_inc(vn_stored[b], 16)
            store_vn(0)
            store_vn(1)
            unit(n + 4, 0, columns(w_in, 4 * D), wide(0))
            unit(n + 5, 1, columns(w_in, 5 * D), wide(1))
            store_vn(2)
            sp.dma_start(outs["sgu_v_prompt"].rearrange("o b s d -> (o b s) d"), v_all[:, NT - 2, :])\
              .then_inc(vn_stored[2], 16)
            sp.dma_start(outs["sgu_v_sample"].rearrange("o b s d -> (o b s) d"), v_all[:, NT - 1, :])\
              .then_inc(vn_stored[2], 16)
            sp.wait_ge(vn_stored[0], 16)
            sp.wait_ge(vn_stored[1], 16)
            sp.wait_ge(vn_stored[2], 48)
            sp.dma_start(v_in[:, :].rearrange("p (t c) -> p t c", t=NT),
                         vn_dram.rearrange("t p n -> p t n")[:, :, 0:P]).then_inc(v_loaded, 16)
            mix_units(1)
            with sp.Fori(2, KT) as j:
                store_merged(j - 2)
                mix_units(j)
            store_merged(KT - 2)
            w_out = ins["w_out"].rearrange("o k n -> (o k) n")
            for q in range(RING - 1):
                unit(U_OUT + q, q % 2, columns(w_out, q * P), wide(q % 2))
            sp.wait_ge(spilled, 16 * (1 + KT - 1))
            last = KT - 1
            for k, (done, count) in enumerate((
                    (None, 0),
                    (vn_lo_ready, KT),
                    (inputs_gated, KT),
                    (s_mm, SPATIAL * KT), (s_mm, SPATIAL * KT),
                    (lru_step, last * 8 + 5),
                    (lru_step, last * 8 + 7))):
                if done is not None:
                    sp.wait_ge(done, count)
                if k == 3:
                    unit(U_OUT + RING - 1, 1, columns(w_out, (RING - 1) * P), wide(1))
                sp.dma_start(merged_in[k][:, :], merged_dram[k]).then_inc(merged_back[k], 16)
            sp.wait_ge(merged_ready, KT)
            sp.dma_start(x[:, :, :], x_dram).then_inc(x_back, 16)
            for q in range(RING, KT):
                unit(U_OUT + q, q % 2, columns(w_out, q * P), wide(q % 2))
            ffn_units(U_FFN2, "ffn2")
            sp.wait_ge(tail_ready, 2)
            sp.dma_start(outs["rglru_prompt"].rearrange("o b d -> (o b) d"), tailrow[0:1, :]).then_inc(state_stored, 16)
            sp.dma_start(outs["rglru_sample"].rearrange("o b d -> (o b) d"), tailrow[1:NSEQ, :])\
              .then_inc(state_stored, 16)
            sp.dma_start(outs["conv_prompt"].rearrange("o b w d -> (o b w) d"), tailrow[NSEQ:NSEQ + HIST, :])\
              .then_inc(state_stored, 16)
            sp.dma_start(outs["conv_sample"].rearrange("o b w d -> (o b w) d"), tailrow[NSEQ + HIST:TAIL, :])\
              .then_inc(state_stored, 16)
            for t in range(NT):
                sp.wait_ge(yrow_act, t + 1)
                sp.wait_ge(yrow_dve, t + 1)
                dst = (outs["y_prompt"].rearrange("b s d -> (b s) d")[t * P:(t + 1) * P, :] if t < NT - 1
                       else outs["y_sample"].rearrange("b s d -> (b s) d"))
                sp.dma_start(dst, yrow[:, t, :]).then_inc(y_stored, 16)
            sp.wait_ge(state_stored, 16 * 4)
            sp.wait_ge(y_stored, 16 * NT)

        @block.gpsimd
        def _(pool):
            nc.gpsimd.memset(ident[:, :], 0.0).then_inc(const_step, 1)
            nc.gpsimd.memset(ones[:, :], 1.0).then_inc(const_step, 1)
            nc.gpsimd.memset(epst[:, 0:1], EPS).then_inc(const_step, 1)
            pool.wait_ge(const_step, 3)
            nc.gpsimd.affine_select(out=ident[:, :], in_=ident[:, :], compare_op=ALU.not_equal, fill=1.0,
                                    base=0, pattern=[[-1, P]], channel_multiplier=1).then_inc(const_ready, 1)
            nc.gpsimd.memset(rg_sb[:, :, :, :], 0.0).then_inc(rg_zeroed, 1)
            add_squares(pool, 0)
            add_squares(pool, 1)
            pool.wait_ge(xn_lo_ready, 2 * NCH * KT)
            pool.wait_ge(spilled, 16)
            nc.gpsimd.memset(wd_raw[:, :, :], 0.0).then_inc(wd_zeroed, 1)
            pool.wait_ge(ws_loaded, 16 * (4 + NS))
            for w in (ws_raw, wd_raw):
                nc.gpsimd.affine_select(out=w[:, :, :], in_=w[:, :, :], compare_op=ALU.is_ge, fill=0.0,
                                        base=0, pattern=[[0, KT], [-1, P]], channel_multiplier=1)\
                  .then_inc(ws_masked, 1)
            with pool.Fori(0, KT) as j:
                pool.wait_ge(act_evicted, j * 21 + (2 * NT + 15))
                nc.gpsimd.tensor_tensor(ii[:, :], ii[:, :], xc[:, :], ALU.mult).then_inc(inputs_gated, 1)
                for c in range(NCH):
                    cols = slice(c * CH, (c + 1) * CH)
                    pool.wait_ge(act_evicted, j * 21 + (2 * NT + 16 + c))
                    nc.gpsimd.tensor_tensor(gg[:, cols], gg[:, cols], sig[:, c, :], ALU.mult).then_inc(branch_gated, 1)
            add_squares(pool, 2)
            add_squares(pool, 3)

        @block.scalar
        def _(act):
            act.wait_ge(c_loaded, 32)
            nc.scalar.activation(crow[:, :], crow[:, :], ACT.Silu).then_inc(c_silu, 1)
            for dst, src in ((vrow[V_G1:V_G1 + 8, :], ins["g_ffn1"].rearrange("o (k p) -> (o k) p", p=P)),
                             (vrow[V_GM:V_GM + 8, :], ins["g_mix"].rearrange("o (k p) -> (o k) p", p=P)),
                             (vrow[V_G2:V_G2 + 8, :], ins["g_ffn2"].rearrange("o (k p) -> (o k) p", p=P)),
                             (vrow[V_GF:V_GF + 8, :], ins["g_final"].rearrange("(k p) -> k p", p=P)),
                             (vrow[V_BCONV:V_BCONV + 8, :], ins["b_conv"].rearrange("o (k p) -> (o k) p", p=P)),
                             (vrow[V_WCONV:V_WCONV + 32, :], ins["w_conv"].rearrange("o w (k p) -> (o w k) p", p=P)),
                             (vrow[V_BA:V_BA + 8, :], ins["b_rg_a"].rearrange("o (k p) -> (o k) p", p=P)),
                             (vrow[V_BX:V_BX + 8, :], ins["b_rg_x"].rearrange("o (k p) -> (o k) p", p=P)),
                             (vrow[V_LAM:V_LAM + 8, :], ins["rg_lambda"].rearrange("o (k p) -> (o k) p", p=P)),
                             (brow[0:9 * KT, :], ins["b_ada"].rearrange("o (k p) -> (o k) p", p=P)),
                             (brow[9 * KT:NADA, :], ins["b_ada_final"].rearrange("(k p) -> k p", p=P)),
                             (hrow[0:24, :], ins["cache_conv"].rearrange("o b w d -> (o b w) d")),
                             (hrow[24:32, :], ins["state_rglru"].rearrange("o b d -> (o b) d"))):
                act.dma_start(dst, src).then_inc(rows_loaded, 16)
            act.wait_ge(rows_copied, 1)
            nc.scalar.activation(c_parts[:, :, 0:NSEQ], cT[:, :, 0:NSEQ], ACT.Copy).then_inc(c_silu, 1)

            def squares(i, lo, hi):
                for pos, (c, k) in list(enumerate(squares_order(i)))[lo:hi]:
                    act.wait_ge(x_written, residual_written(i, c, k))
                    if pos >= 3 and k > 0 and added(i, pos - 2) > 0:
                        act.wait_ge(acc_added, added(i, pos - 2))
                    dst = sq[:, pos % 3, :] if k > 0 else acc[:, c, :]
                    nc.scalar.activation(dst, x[:, k, c * CH:(c + 1) * CH], ACT.Square).then_inc(squared, 1)

            def root(i, c):
                act.wait_ge(sumsq_mm, i * NCH + c + 1)
                nc.scalar.activation(acc[:, c, :], bank[6 + c % 2][:, 0:CH], ACT.Sqrt,
                                     scale=1.0 / D, bias=epst[:, 0:1]).then_inc(std_ready, 1)

            def modulate(i, c, v_shift, v_scale, final=False, blocks=range(KT)):
                width = CH if c < NCH - 1 else PC2
                for k in blocks:
                    n = (i * NCH + c) * KT + k
                    act.wait_ge(t_ready, n + 1)
                    if not final:
                        nc.scalar.activation(xfull[:, k % 2, 0:width], tbuf[:, k % 2, 0:width], ACT.Identity,
                                             scale=prompt_scalar(v_scale, k), bias=prompt_scalar(v_shift, k))
                    dst = yT[:, c, k, 0:width] if final else xn_hi[:, k, c * CH:c * CH + width]
                    op = nc.scalar.activation(dst, tbuf[:, k % 2, 0:width], ACT.Identity,
                                              scale=prompt_scalar(v_scale, k), bias=prompt_scalar(v_shift, k))
                    if final:
                        op.then_inc(xf_ready, 1)
                        continue
                    if c == NCH - 1:
                        act.wait_ge(xs_step, (i * KT + k + 1) * 2)
                        op = nc.scalar.activation(xn_hi[:, k, SEQ:TOK], xfull[:, k % 2, PC2:CH], ACT.Copy)
                    op.then_inc(xn_hi_ready, 1)

            def norm_in_tail(i, v_shift, v_scale, final=False):
                squares(i, 0, KT + 3)
                root(i, 0)
                squares(i, KT + 3, KT + 6)
                for k in range(KT):
                    modulate(i, 0, v_shift, v_scale, final, blocks=(k,))
                    squares(i, KT + 6 + k, KT + 7 + k)
                root(i, 1)
                squares(i, 2 * KT + 6, 3 * KT)
                root(i, 2)
                for c in (1, 2):
                    modulate(i, c, v_shift, v_scale, final)
                    if final:
                        out_rows(c - 1)
                if final:
                    out_rows(NCH - 1)

            def out_rows(c):
                for s in range(NCH):
                    t = NCH * c + s
                    act.wait_ge(y_turned, 2 * t + 1)
                    nc.scalar.activation(yrow[:, t, 0:HALF], bank[(2 * t) % RING][:, :], ACT.Copy)\
                      .then_inc(yrow_act, 1)

            def ffn(base, h0, with_ada):
                def group(g, ada_piece=False, tail=None):
                    def ahead_units(*qs):
                        for q in qs:
                            split_hi(act, g * 6 + (base + RING + q), q % 2, (base + q) % RING)

                    def piece(r):
                        if not ada_piece:
                            return
                        act.wait_ge(ada_mm, g * 8 + (2 * FIRST + r))
                        if r == 4 or r == 8:
                            nc.scalar.activation(ada_row[:, :], bank[6][0:2 * NSEQ, :], ACT.Copy)\
                              .then_inc(ada_row_ready, 1)
                        if r < 8:
                            act.wait_ge(piece_loaded, g * 128 + 16 * (r + 1))
                            nc.scalar.activation(ada_hi[:, :], ada_raw[:, :], ACT.Copy).then_inc(piece_hi_ready, 1)
                    for q in range(6):
                        f, c = divmod(q, NCH)
                        if q == 0:
                            piece(0)
                        act.wait_ge(gate_mm, g * 6 + (h0 + q + 1))
                        if q >= 2:
                            act.wait_ge(h_full, g * 6 + (h0 + q - 1))
                        nc.scalar.activation(silu[:, q % 2, :], bank[c][:, 0:CH], ACT.Silu).then_inc(silu_ready, 1)
                        act.wait_ge(h_full, g * 6 + (h0 + q + 1))
                        nc.scalar.activation(h_hi[:, f, c * CH:(c + 1) * CH], hfull[:, q % 2, :], ACT.Copy)\
                          .then_inc(h_hi_ready, 1)
                        if q == 2 and not (tail and tail[0] == 3):
                            ahead_units(0, 1)
                        if q >= 2:
                            piece(q - 1)
                    piece(5)
                    if not (tail and tail[0] == 3):
                        ahead_units(2, 3)
                    piece(6)
                    piece(7)
                    piece(8)
                    if tail:
                        norm_in_tail(*tail)
                    if not (tail and tail[0] == 3):
                        act.wait_ge(down_mm, g * 24 + (h0 * 4 + 24))
                        ahead_units(4, 5)
                if with_ada:
                    with act.Fori(0, LATER) as g:
                        group(g, ada_piece=True)
                    with act.Fori(LATER, GROUPS - 1) as g:
                        group(g)
                    group(GROUPS - 1, tail=(1, SHIFTM, SCALEM))
                else:
                    with act.Fori(0, GROUPS - 1) as g:
                        group(g)
                    group(GROUPS - 1, tail=(3, SHIFTF, SCALEF, True))

            def first_rows(n):
                act.wait_ge(ada_mm, n + 1)
                if n > 0:
                    act.wait_ge(ada_folded, n)
                nc.scalar.activation(ada_row[0:NSEQ, :], bank[3 + n % 2][0:NSEQ, :], ACT.Copy)\
                  .then_inc(ada_row_ready, 1)

            def first_splits(*ns):
                for n in ns:
                    split_hi(act, n, n % 2, n % RING)
            squares(0, 0, KT)
            act.wait_ge(rg_zeroed, 1)
            for g, name in enumerate(("w_rg_a", "w_rg_x")):
                for h in range(2):
                    src = ins[name].rearrange("o (k h) i j -> h i (o k) j", h=2)[h]
                    act.dma_start(rg_sb[64 * h:64 * h + 64, :, g, 64 * h:64 * h + 64], src).then_inc(rg_loaded, 16)
            act.wait_ge(sp_step, 1)
            nc.scalar.activation(spw[:, 1, :], spw[:, 0, :], ACT.Exp, scale=-1.0).then_inc(sp_exp, 1)
            squares(0, KT, 2 * KT)
            first_rows(0)
            squares(0, 2 * KT, 3 * KT)
            first_rows(1)
            root(0, 0)
            act.wait_ge(x_turned, XW_IN)
            first_splits(0, 1)
            first_rows(2)
            root(0, 1)
            first_rows(3)
            first_rows(4)
            root(0, 2)
            first_rows(5)
            act.wait_ge(mod_step, 1)
            act.wait_ge(ada_mm, 2 * FIRST)
            act.wait_ge(ada_ready, 4)
            for c in range(NCH):
                modulate(0, c, SHIFT1, SCALE1)
                if c > 0:
                    first_splits(2 * c, 2 * c + 1)
            ffn(U_FFN1, 0, True)
            act.wait_ge(spilled, 16)
            act.wait_ge(xn_lo_ready, 2 * NCH * KT)

            def v_deviation(b):
                act.wait_ge(v_moments, 3 * b + 3)
                nc.scalar.activation(vstd[:, 3 * b:3 * b + 3], mv[:, 3 * b:3 * b + 3, 1], ACT.Sqrt,
                                     bias=epst[:, 0:1]).then_inc(vstd_ready, 1)
            for half in range(2):
                for t in range(NT):
                    m = half * NT + t
                    act.wait_ge(v_mm, m + 1)
                    nc.scalar.activation(v_all[:, t, half * HALF:(half + 1) * HALF], bank[m % RING][:, :],
                                         ACT.Gelu_apprx_tanh).then_inc(act_evicted, 1)
                    if half == 1 and t in (2, 5):
                        v_deviation(t // 3)
                    if m == WS_AFTER:
                        for w in range(2):
                            for b in range(2):
                                act.wait_ge(ws_turned, 2 * w + b + 1)
                                nc.scalar.activation(
                                    ws_parts[:, w, 4 * b:4 * b + 4, 0, :],
                                    bank[6 + b][:, :].rearrange("p (h t) -> p h t", h=4), ACT.Copy)\
                                  .then_inc(ws_hi_ready, 1)
                if half == 0:
                    for n in range(U_V + 6, U_V + 10):
                        split_hi(act, n, n % 2, n % RING)
            for n in range(U_V + 10, U_V + 14):
                if n == U_V + 12:
                    v_deviation(2)
                split_hi(act, n, n % 2, n % RING)

            def mix(j):
                def evicts(m, dst, src_bank, func, **kw):
                    return nc.scalar.activation(dst, src_bank, func, **kw).then_inc(act_evicted, 1)

                def section(first, count):
                    act.wait_ge(mix_mm, j * 21 + (first + count))

                def ahead_unit(q):
                    n = j * 6 + (U_MIX + RING + q)
                    split_hi(act, n, q % 2, (U_MIX + q) % RING)

                act.wait_ge(xr_free, j + 2)
                for c in range(NCH):
                    section(c, 1)
                    if c < NCH - 1:
                        evicts(c, xr[:, HIST + c * CH:HIST + (c + 1) * CH], bank[c][:, 0:CH], ACT.Copy)
                    else:
                        nc.scalar.activation(xr[:, HIST + c * CH:HIST + SEQ], bank[c][:, 0:PC2], ACT.Copy)
                        evicts(c, xr_samples(xr)[:, :, HIST:HIST + LS], samples(bank[c][:, PC2:CH]), ACT.Copy)
                ahead_unit(0)
                section(3, 1)
                act.wait_ge(vn_stored[0], 16)
                evicts(3, gg[:, 0:CH], bank[3][:, 0:CH], ACT.Gelu_apprx_tanh)
                act.wait_ge(conv_step, j * 8 + 8)
                nc.scalar.activation(s_hi[:, :], xc[:, :], ACT.Copy).then_inc(xc_hi_ready, 1)
                for c in (1, 2):
                    section(3 + c, 1)
                    evicts(3 + c, gg[:, c * CH:(c + 1) * CH], bank[3 + c][:, 0:CH], ACT.Gelu_apprx_tanh)
                ahead_unit(1)
                for c in range(NCH):
                    section(6 + c, 1)
                    evicts(6 + c, ug[:, c * CH:(c + 1) * CH], bank[c][:, 0:CH], ACT.Gelu_apprx_tanh)
                ahead_unit(2)
                act.wait_ge(vn_stored[1], 16)
                for c in range(NCH):
                    cols = slice(c * CH, (c + 1) * CH)
                    section(9 + 2 * c, 1)
                    evicts(9, ww[:, cols], bank[(9 + 2 * c) % RING][:, 0:CH], ACT.Sigmoid,
                           bias=blk[:, 0:1])
                    section(10 + 2 * c, 1)
                    evicts(10, ii[:, cols], bank[(10 + 2 * c) % RING][:, 0:CH], ACT.Sigmoid,
                           bias=blk[:, 1:2])
                act.wait_ge(v_loaded, j * 16 + 16)
                nc.scalar.activation(s_hi[:, :], v_in[:, :], ACT.Copy).then_inc(vn_hi_ready, 1)
                act.wait_ge(act_evicted, j * 21 + (2 * NT + 15))
                nc.scalar.activation(ww[:, :], ww[:, :], ACT.Tanh, scale=blk[:, 2:3]).then_inc(w_ready, 1)
                act.wait_ge(w_ready, j + 1)
                act.wait_ge(vn_stored[2], 48)
                nc.scalar.activation(rt[:, :], ww[:, :], ACT.Sqrt, scale=4.0).then_inc(root_ready, 1)
                ahead_unit(3)
                for s in range(2):
                    for c in range(NCH):
                        section(15 + 3 * s + c, 1)
                        if s == 1:
                            act.wait_ge(branch_gated, j * NCH + (c + 1))
                        evicts(18 + 3 * s + c, sig[:, c, :], bank[3 + c][:, 0:CH], ACT.Sigmoid)
                    ahead_unit(4 + s)
            with act.Fori(0, KT) as j:
                mix(j)

            for k in range(KT):
                if k < KT - 1:
                    act.wait_ge(merged_back[k], 16)
                else:
                    act.wait_ge(merged_ready, KT)
                nc.scalar.activation(xn_hi[:, k, :], merged_in[k][:, :], ACT.Copy).then_inc(m_hi_ready, 1)
            act.wait_ge(m_lo_ready, KT)
            for p in range(KT // 2 - 1):
                act.wait_ge(out_mm, p + 1)
                squares(2, 6 * p, 6 * p + 6)
                for n in (U_OUT + 2 * p + 6, U_OUT + 2 * p + 7):
                    split_hi(act, n, n % 2, n % RING)
            squares(2, 18, 20)
            root(2, 0)
            modulate(2, 0, SHIFT2, SCALE2, blocks=range(0, 4))
            squares(2, 20, 22)
            modulate(2, 0, SHIFT2, SCALE2, blocks=range(4, KT))
            root(2, 1)
            squares(2, 22, 24)
            for n in (U_OUT + 12, U_OUT + 13):
                act.wait_ge(out_mm, KT // 2 + 2)
                split_hi(act, n, n % 2, n % RING)
            root(2, 2)
            modulate(2, 1, SHIFT2, SCALE2)
            modulate(2, 2, SHIFT2, SCALE2)
            ffn(U_FFN2, 6 * GROUPS, False)

        @block.vector
        def _(dve):
            dve.wait_ge(rows_turned, 1)
            nc.vector.tensor_copy(cT[:, :, 0:NSEQ],
                                  bank[7][:, 0:KT * NSEQ].rearrange("p (k n) -> p k n", k=KT))\
              .then_inc(rows_copied, 1)
            dve.wait_ge(rows_copied, 1)
            dve.wait_ge(c_silu, 2)
            nc.vector.tensor_tensor(c_parts[:, :, NSEQ:2 * NSEQ], cT[:, :, 0:NSEQ],
                                    c_parts[:, :, 0:NSEQ].bitcast(F32), ALU.subtract).then_inc(piece_lo_ready, 1)

            def x_in(t):
                for s in range(3):
                    for b in range(2):
                        dve.wait_ge(x_turned, 6 * t + 2 * s + b + 1)
                        tile = 3 * t + s
                        nc.vector.tensor_copy(
                            x[:, 4 * b:4 * b + 4, tile * P:(tile + 1) * P],
                            bank[2 * s + b][:, :].rearrange("p (k n) -> p k n", k=4)).then_inc(x_written, 1)
            x_in(0)
            x_in(1)
            dve.wait_ge(rows_turned, 2)
            nc.vector.tensor_copy(vecT[:, :], bank[6][:, 0:NVEC])
            nc.vector.tensor_copy(badaT[:, :], bank[6][:, 128:128 + NADA])
            nc.vector.tensor_copy(histT[:, :, :], bank[6][:, 256:512].rearrange("p (k n) -> p k n", k=KT))\
              .then_inc(rows_copied, 1)
            dve.wait_ge(rows_copied, 2)
            nc.vector.tensor_tensor(fold[:, :], ident[0:2 * NSEQ, 0:NSEQ], ident[0:2 * NSEQ, NSEQ:2 * NSEQ], ALU.add)
            lam = vecT[:, V_LAM:V_LAM + KT]
            steps = [0]

            def step(ins_):
                steps[0] += 1
                ins_.then_inc(sp_step, 1)

            def after():
                dve.wait_ge(sp_step, steps[0])
            nc.vector.tensor_scalar(spw[:, 5, :], lam, -1.0, 0.0, ALU.mult, ALU.max)
            step(nc.vector.scalar_tensor_tensor(spw[:, 0, :], lam, -1.0, lam, ALU.mult, ALU.max))
            x_in(2)
            dve.wait_ge(sp_exp, 1)
            step(nc.vector.tensor_scalar(spw[:, 2, :], spw[:, 1, :], 2.0, None, ALU.add))
            after()
            step(nc.vector.reciprocal(spw[:, 3, :], spw[:, 2, :]))
            after()
            step(nc.vector.tensor_tensor(spw[:, 0, :], spw[:, 1, :], spw[:, 3, :], ALU.mult))
            after()
            step(nc.vector.tensor_tensor(spw[:, 1, :], spw[:, 0, :], spw[:, 0, :], ALU.mult))
            after()
            step(nc.vector.tensor_scalar(spw[:, 2, :], spw[:, 1, :], 1.0 / 17, 1.0 / 15, ALU.mult, ALU.add))
            for d in (13, 11, 9, 7, 5, 3, 1):
                after()
                step(nc.vector.tensor_tensor(spw[:, 3, :], spw[:, 2, :], spw[:, 1, :], ALU.mult))
                after()
                step(nc.vector.tensor_scalar(spw[:, 2, :], spw[:, 3, :], 1.0 / d, None, ALU.add))
            after()
            step(nc.vector.scalar_tensor_tensor(spw[:, 3, :], spw[:, 2, :], 2.0, spw[:, 0, :], ALU.mult, ALU.mult))
            after()
            step(nc.vector.tensor_tensor(spw[:, 4, :], spw[:, 3, :], spw[:, 5, :], ALU.add))
            after()
            step(nc.vector.tensor_scalar(lam, spw[:, 4, :], 4.0, None, ALU.mult))

            gains = {SCALE1: V_G1, SCALEM: V_GM, SCALE2: V_G2, SCALEF: V_GF}

            def scale_gain(v):
                a = ada[:, v * KT:(v + 1) * KT, :]
                g = vecT[:, gains[v]:gains[v] + KT]
                nc.vector.scalar_tensor_tensor(a, a, 1.0, g.unsqueeze(2).broadcast_to([P, KT, NSEQ]),
                                               ALU.add, ALU.mult).then_inc(mod_step, 1)

            def first_half(n):
                v, half = FIRST_HALVES[n]
                dve.wait_ge(ada_folded, n + 1)
                blocks = slice(v * KT + 4 * half, v * KT + 4 * half + 4)
                nc.vector.tensor_tensor(
                    ada[:, blocks, :],
                    bank[n % 3][:, 0:4 * NSEQ].rearrange("p (k n) -> p k n", k=4),
                    badaT[:, blocks].unsqueeze(2).broadcast_to([P, 4, NSEQ]), ALU.add).then_inc(ada_ready, 1)

            def reciprocal(i, c):
                dve.wait_ge(std_ready, i * NCH + c + 1)
                nc.vector.reciprocal(acc[:, c, :], acc[:, c, :]).then_inc(rstd_ready, 1)

            def modulate(i, c, k, v_shift, v_scale, final=False):
                cols = slice(c * CH, (c + 1) * CH)
                n = (i * NCH + c) * KT + k
                if k < KT:
                    if k == 0:
                        dve.wait_ge(rstd_ready, i * NCH + c + 1)
                    if final:
                        if c * KT + k >= 2:
                            dve.wait_ge(xf_ready, c * KT + k - 1)
                    elif n >= 2:
                        dve.wait_ge(xn_lo_ready, n - 1)
                    nc.vector.tensor_tensor(tbuf[:, k % 2, :], x[:, k, cols], acc[:, c, :], ALU.mult)\
                      .then_inc(t_ready, 1)
                if k > 0 and not final:
                    dve.wait_ge(xn_hi_ready, n)
                    nc.vector.tensor_tensor(xn_lo[:, k - 1, cols], xfull[:, (k - 1) % 2, :],
                                            xn_hi[:, k - 1, cols].bitcast(F32), ALU.subtract)\
                      .then_inc(xn_lo_ready, 1)
                if k < KT:
                    if c == NCH - 1:
                        dve.wait_ge(t_ready, n + 1)
                        s0 = (i * KT + k) * 2
                        ts = samples(tbuf[:, k % 2, PC2:CH])
                        nc.vector.tensor_tensor(ts, ts, per_sample(v_scale, k), ALU.mult).then_inc(xs_step, 1)
                        dve.wait_ge(xs_step, s0 + 1)
                        dst = yT[:, c, k, PC2:CH] if final else xfull[:, k % 2, PC2:CH]
                        nc.vector.tensor_tensor(samples(dst), ts, per_sample(v_shift, k), ALU.add)\
                          .then_inc(xs_step, 1)

            def modulate_chunk(i, c, *vs):
                for k in range(KT + 1):
                    modulate(i, c, k, *vs)

            def out_rows(c):
                for s in range(NCH):
                    t = NCH * c + s
                    dve.wait_ge(y_turned, 2 * t + 2)
                    nc.vector.tensor_copy(yrow[:, t, HALF:D], bank[(2 * t + 1) % RING][:, :])\
                      .then_inc(yrow_dve, 1)

            def add_gated(ps, v, o, c, tmp_count, tmp_slot):
                if c < NCH - 1:
                    cols = slice(c * CH, (c + 1) * CH)
                    nc.vector.scalar_tensor_tensor(x[:, o, cols], ps[:, 0:CH], prompt_scalar(v, o), x[:, o, cols],
                                                   ALU.mult, ALU.add).then_inc(x_written, 1)
                    return
                nc.vector.tensor_tensor(samples(gtmp[:, tmp_slot, :]), samples(ps[:, PC2:CH]), per_sample(v, o),
                                        ALU.mult).then_inc(gated_tmp, 1)
                nc.vector.scalar_tensor_tensor(x[:, o, c * CH:SEQ], ps[:, 0:PC2], prompt_scalar(v, o),
                                               x[:, o, c * CH:SEQ], ALU.mult, ALU.add)
                dve.wait_ge(gated_tmp, tmp_count)
                nc.vector.tensor_tensor(x[:, o, SEQ:TOK], x[:, o, SEQ:TOK], gtmp[:, tmp_slot, :], ALU.add)\
                  .then_inc(x_written, 1)

            def ffn(base, h0, xw0, tmp0, v_gate, with_ada):
                def group(g, ada_piece=False, tail=None):
                    ahead = not (tail and tail[0] == 3)

                    def ahead_units(*qs):
                        if ahead:
                            for q in qs:
                                split_lo(dve, g * 6 + (base + RING + q), q % 2, (base + q) % RING)

                    def piece(r):
                        if ada_piece:
                            dve.wait_ge(piece_hi_ready, g * 8 + r + 1)
                            nc.vector.tensor_tensor(ada_lo[:, :], ada_raw[:, :], ada_hi[:, :].bitcast(F32),
                                                    ALU.subtract).then_inc(piece_lo_ready, 1)

                    def vector_half(half):
                        if ada_piece:
                            dve.wait_ge(ada_folded, g * 2 + (2 * FIRST + half + 1))
                            o = g * KT + (FIRST * KT + 4 * half)
                            nc.vector.tensor_tensor(
                                ada[:, ds(o, 4), :],
                                bank[7][:, half * 4 * NSEQ:(half + 1) * 4 * NSEQ].rearrange("p (k n) -> p k n", k=4),
                                badaT[:, ds(o, 4)].unsqueeze(2).broadcast_to([P, 4, NSEQ]), ALU.add)\
                              .then_inc(ada_ready, 1)
                    for q in range(6):
                        f, c = divmod(q, NCH)
                        cols = slice(c * CH, (c + 1) * CH)
                        if q == 0:
                            piece(0)
                        dve.wait_ge(up_mm, g * 6 + (h0 + q + 1))
                        dve.wait_ge(silu_ready, g * 6 + (h0 + q + 1))
                        if q >= 2:
                            dve.wait_ge(h_lo_ready, g * 6 + (h0 + q - 1))
                        nc.vector.scalar_tensor_tensor(hfull[:, q % 2, :], silu[:, q % 2, :], 0.5,
                                                       bank[3 + c][:, 0:CH], ALU.mult, ALU.mult).then_inc(h_full, 1)
                        dve.wait_ge(h_hi_ready, g * 6 + (h0 + q + 1))
                        nc.vector.tensor_tensor(h_lo[:, f, cols], hfull[:, q % 2, :],
                                                h_hi[:, f, cols].bitcast(F32), ALU.subtract)\
                          .then_inc(h_lo_ready, 1)
                        if q == 2:
                            ahead_units(0, 1)
                        if q >= 2:
                            piece(q - 1)
                    dve.wait_ge(h_lo_ready, g * 6 + (h0 + 6))
                    dve.wait_ge(x_written, g * 24 + xw0)
                    for c in range(NCH):
                        for o in range(KT):
                            m = c * KT + o
                            dve.wait_ge(down_mm, g * 24 + (h0 * 4 + m + 1))
                            add_gated(bank[m % RING], v_gate, o, c, g * KT + (tmp0 + o + 1), o % 2)
                            if m in (3, 7, 11):
                                piece(5 + m // 4)
                            if m == 9:
                                vector_half(0)
                            if tail and m == KT + 4:
                                reciprocal(tail[0], 0)
                            elif tail and KT + 4 < m <= 2 * KT + 5:
                                modulate(tail[0], 0, m - (KT + 5), *tail[1:])
                        if c == 0:
                            ahead_units(2, 3)
                    vector_half(1)
                    if tail:
                        dve.wait_ge(x_written, xw0 + 24 * GROUPS)
                        for c in (1, 2):
                            reciprocal(tail[0], c)
                        if tail[0] == 3:
                            state_rows()
                        for c in (1, 2):
                            modulate_chunk(tail[0], c, *tail[1:])
                            if tail[0] == 3:
                                out_rows(c - 1)
                        if tail[0] == 3:
                            out_rows(NCH - 1)
                    ahead_units(4, 5)
                if with_ada:
                    with dve.Fori(0, LATER) as g:
                        group(g, ada_piece=True)
                    dve.wait_ge(ada_ready, 2 * (FIRST + LATER))
                    for v in (SCALEM, SCALE2, SCALEF):
                        scale_gain(v)
                    with dve.Fori(LATER, GROUPS - 1) as g:
                        group(g)
                    dve.wait_ge(mod_step, 4)
                    group(GROUPS - 1, tail=(1, SHIFTM, SCALEM))
                else:
                    with dve.Fori(0, GROUPS - 1) as g:
                        group(g)
                    group(GROUPS - 1, tail=(3, SHIFTF, SCALEF, True))

            def state_rows():
                dve.wait_ge(w_lo_ready, U_END)
                for b in range(2):
                    dve.wait_ge(rows_turned, 3 + b)
                    nc.vector.tensor_copy(tailrow[:, b * HALF:(b + 1) * HALF], bank[b][0:TAIL, :])\
                      .then_inc(tail_ready, 1)

            dve.wait_ge(x_written, XW_IN)
            dve.wait_ge(sp_step, steps[0])
            first_half(0)
            first_half(1)
            dve.wait_ge(ada_ready, 2)
            scale_gain(SCALE1)
            reciprocal(0, 0)

            def first_splits(*ns):
                for n in ns:
                    split_lo(dve, n, n % 2, n % RING)
            first_splits(0, 1)
            first_half(2)
            reciprocal(0, 1)
            first_half(3)
            first_half(4)
            reciprocal(0, 2)
            first_half(5)
            dve.wait_ge(mod_step, 1)
            dve.wait_ge(rg_stored, 16)
            for c in range(NCH):
                modulate_chunk(0, c, SHIFT1, SCALE1)
                if c > 0:
                    first_splits(2 * c, 2 * c + 1)
            dve.wait_ge(ada_ready, 2 * FIRST)
            dve.wait_ge(xn_lo_ready, NCH * KT)
            ffn(U_FFN1, 0, XW_IN, 0, GATE1, True)

            def normalise_v(b):
                tiles = range(3 * b, 3 * b + 3)
                dve.wait_ge(v_stats, NT + 3 * b + 3)
                for t in tiles:
                    nc.vector.bn_aggr(mv[:, t, :], bnst[:, t, :, :]).then_inc(v_moments, 1)
                dve.wait_ge(vstd_ready, b + 1)
                nc.vector.reciprocal(vstd[:, 3 * b:3 * b + 3], vstd[:, 3 * b:3 * b + 3]).then_inc(v_rstd, 1)
                dve.wait_ge(v_rstd, b + 1)
                for t in tiles:
                    nc.vector.tensor_scalar(v_all[:, t, :], v_all[:, t, :], mv[:, t, 0:1], vstd[:, t:t + 1],
                                            ALU.subtract, ALU.mult).then_inc(v_centred, 1)
                for t in tiles:
                    dve.wait_ge(v_centred, t + 1)
                    nc.vector.tensor_tensor(v_all[:, t, :], v_all[:, t, :], lng[:, :], ALU.mult).then_inc(v_scaled, 1)
                for t in tiles:
                    dve.wait_ge(v_scaled, t + 1)
                    nc.vector.tensor_tensor(v_all[:, t, :], v_all[:, t, :], lnb[:, :], ALU.add).then_inc(vn_ready, 1)

            for half in range(2):
                if half == 1:
                    dve.wait_ge(ws_loaded, 16 * (4 + NS))
                for t in range(NT):
                    dve.wait_ge(act_evicted, half * NT + t + 1)
                    nc.vector.bn_stats(bnst[:, t, half, :], v_all[:, t, half * HALF:(half + 1) * HALF])\
                      .then_inc(v_stats, 1)
                    if half * NT + t == WS_AFTER:
                        for w in range(2):
                            for b in range(2):
                                dve.wait_ge(ws_hi_ready, 2 * w + b + 1)
                                nc.vector.tensor_tensor(
                                    ws_parts[:, w, 4 * b:4 * b + 4, 1, :],
                                    bank[6 + b][:, :].rearrange("p (h t) -> p h t", h=4),
                                    ws_parts[:, w, 4 * b:4 * b + 4, 0, :].bitcast(F32),
                                    ALU.subtract).then_inc(ws_lo_ready, 1)
                    if half == 1 and t in (2, 5):
                        normalise_v(t // 3)
                if half == 0:
                    for n in range(U_V + 6, U_V + 10):
                        split_lo(dve, n, n % 2, n % RING)
            dve.wait_ge(ws_lo_ready, 4)
            nc.vector.memset(vstd[:, NT:NT + 1], 0.0).then_inc(s_evicted, SPATIAL)
            for n in range(U_V + 10, U_V + 12):
                split_lo(dve, n, n % 2, n % RING)
            normalise_v(2)
            for n in range(U_V + 12, U_V + 14):
                split_lo(dve, n, n % 2, n % RING)
            dve.wait_ge(vn_ready, NT)
            nc.vector.memset(xr[:, 0:HIST], 0.0).then_inc(xr_free, 1)

            def mix(j):
                def ahead_unit(q):
                    split_lo(dve, j * 6 + (U_MIX + RING + q), q % 2, (U_MIX + q) % RING)
                xs = xr_samples(xr)
                nc.vector.tensor_copy(blk[:, :], vecT[:, V_BA:V_BA + 3 * KT].rearrange(
                    "p (v k) -> p v k", k=KT)[:, :, ds(j, 1)].rearrange("p v o -> p (v o)"))
                nc.vector.tensor_copy(xs[:, :, 0:HIST],
                                      histT[:, ds(j, 1), 0:NS * HIST].rearrange("p o (b w) -> p (o b) w", b=NS))\
                  .then_inc(xr_free, 1)
                dve.wait_ge(act_evicted, j * 21 + (2 * NT + NCH))
                dve.wait_ge(xr_free, j + 2)
                for w in range(TAPS):
                    tap = vecT[:, ds(j + (V_WCONV + w * KT), 1)]
                    if w > 0:
                        dve.wait_ge(conv_step, j * 8 + 2 * w)
                    pairs = ((xc[:, 0:SEQ], xr[:, w:w + SEQ]), (samples(xc[:, SEQ:TOK]), xs[:, :, w:w + LS]))
                    for dst, src in pairs:
                        if w == 0:
                            nc.vector.tensor_scalar(dst, src, tap, vecT[:, ds(j + V_BCONV, 1)],
                                                    ALU.mult, ALU.add).then_inc(conv_step, 1)
                        else:
                            nc.vector.scalar_tensor_tensor(dst, src, tap, dst, ALU.mult, ALU.add)\
                              .then_inc(conv_step, 1)
                tail = tails[:, ds(j, 1), :].rearrange("p o n -> p (o n)")
                nc.vector.tensor_copy(tail[:, NSEQ:NSEQ + HIST], xr[:, SEQ:SEQ + HIST])
                nc.vector.tensor_copy(tail[:, NSEQ + HIST:TAIL].rearrange("p (b w) -> p b w", b=NS),
                                      xs[:, :, LS:LS + HIST])
                ahead_unit(0)
                dve.wait_ge(xc_hi_ready, j + 1)
                nc.vector.tensor_tensor(s_lo[:, :], xc[:, :], s_hi[:, :].bitcast(F32), ALU.subtract)\
                  .then_inc(xc_lo_ready, 1)
                ahead_unit(1)
                ahead_unit(2)
                dve.wait_ge(vn_hi_ready, j + 1)
                nc.vector.tensor_tensor(s_lo[:, :], v_in[:, :], s_hi[:, :].bitcast(F32), ALU.subtract)\
                  .then_inc(vn_lo_ready, 1)
                dve.wait_ge(w_ready, j + 1)
                nc.vector.tensor_scalar(qn[:, :], ww[:, :], 1.0, -1.0, ALU.add, ALU.mult).then_inc(lru_step, 1)
                dve.wait_ge(lru_step, j * 8 + 1)
                nc.vector.reciprocal(qn[:, :], qn[:, :]).then_inc(lru_step, 1)
                ahead_unit(3)
                bias = bsb[:, ds(j, 1), :]
                for b in range(SPATIAL):
                    dve.wait_ge(s_mm, j * SPATIAL + (b + 1))
                    tiles = min(2, NT - 2 * b)
                    parts = bank[S_BANKS[b]][:, 0:tiles * 2 * P].rearrange("p (t a l) -> p t a l", t=tiles, a=2)
                    slot = sb[:, b % 2, 0:tiles * P].rearrange("p (t l) -> p t l", t=tiles)
                    if b < SPATIAL - 1:
                        nc.vector.tensor_tensor(slot, parts[:, :, 1, :], bias.broadcast_to([P, tiles, P]),
                                                ALU.add).then_inc(s_step, 1)
                    else:
                        nc.vector.tensor_tensor(samples(sb[:, b % 2, 0:P]), samples(parts[:, 0, 1, :]),
                                                bias[:, :, 0:LS].broadcast_to([P, NS, LS]), ALU.add)\
                          .then_inc(s_step, 1)
                    dve.wait_ge(s_step, j * SPATIAL + (b + 1))
                    nc.vector.tensor_tensor(slot, slot, parts[:, :, 0, :], ALU.add).then_inc(s_evicted, 1)
                    dve.wait_ge(s_evicted, j * SPATIAL + (SPATIAL + b + 1))
                    cols = slice(2 * b * P, (2 * b + tiles) * P)
                    nc.vector.tensor_tensor(ug[:, cols], ug[:, cols], sb[:, b % 2, 0:tiles * P], ALU.mult)\
                      .then_inc(s_applied, 1)
                ahead_unit(4)
                dve.wait_ge(root_ready, j + 1)
                dve.wait_ge(lru_step, j * 8 + 2)
                nc.vector.scalar_tensor_tensor(rt[:, :], rt[:, :], -1.0, qn[:, :], ALU.mult, ALU.mult)\
                  .then_inc(lru_step, 1)
                nc.vector.scalar_tensor_tensor(ww[:, :], ww[:, :], 1.0, qn[:, :], ALU.subtract, ALU.mult)\
                  .then_inc(lru_step, 1)
                dve.wait_ge(lru_step, j * 8 + 3)
                dve.wait_ge(inputs_gated, j + 1)
                nc.vector.tensor_tensor(ii[:, :], ii[:, :], rt[:, :], ALU.mult).then_inc(lru_step, 1)
                dve.wait_ge(lru_step, j * 8 + 5)
                nc.vector.tensor_tensor_scan(qn[:, 0:SEQ], ww[:, 0:SEQ], ii[:, 0:SEQ], 0.0, ALU.mult, ALU.add)\
                  .then_inc(lru_step, 1)
                for b in range(NS):
                    cols = slice(SEQ + b * LS, SEQ + (b + 1) * LS)
                    ins_ = nc.vector.tensor_tensor_scan(
                        qn[:, cols], ww[:, cols], ii[:, cols],
                        histT[:, ds(j, 1), NS * HIST + b:NS * HIST + b + 1].rearrange("p o n -> p (o n)"),
                        ALU.mult, ALU.add)
                ins_.then_inc(lru_step, 1)
                dve.wait_ge(lru_step, j * 8 + 7)
                nc.vector.tensor_copy(tail[:, 0:1], qn[:, SEQ - 1:SEQ])
                nc.vector.tensor_copy(tail[:, 1:NSEQ],
                                      samples(qn[:, SEQ:TOK])[:, :, LS - 1:LS].rearrange("p b o -> p (b o)"))\
                  .then_inc(lru_step, 1)
                dve.wait_ge(s_applied, j * SPATIAL + SPATIAL)
                for c in range(NCH):
                    cols = slice(c * CH, (c + 1) * CH)
                    dve.wait_ge(act_evicted, j * 21 + (2 * NT + 19 + c))
                    nc.vector.tensor_tensor(ug[:, cols], ug[:, cols], sig[:, c, :], ALU.mult).then_inc(gate_applied, 1)
                dve.wait_ge(gate_applied, j * NCH + NCH)
                dve.wait_ge(branch_gated, j * NCH + NCH)
                nc.vector.tensor_tensor(gg[:, :], gg[:, :], qn[:, :], ALU.mult).then_inc(merge_step, 1)
                dve.wait_ge(merge_step, j + 1)
                dve.wait_ge(spilled, j * 16 + 16)
                nc.vector.tensor_tensor(merged[:, :], gg[:, :], ug[:, :], ALU.add).then_inc(merged_ready, 1)
                ahead_unit(5)
            with dve.Fori(0, KT) as j:
                mix(j)

            for k in range(KT):
                dve.wait_ge(m_hi_ready, k + 1)
                nc.vector.tensor_tensor(xn_lo[:, k, :], merged_in[k][:, :], xn_hi[:, k, :].bitcast(F32),
                                        ALU.subtract).then_inc(m_lo_ready, 1)
            dve.wait_ge(m_lo_ready, KT)
            dve.wait_ge(x_back, 16)
            for p in range(KT // 2 - 1):
                dve.wait_ge(out_mm, p + 1)
                for o in range(2):
                    for c in range(NCH):
                        add_gated(bank[3 * o + c], GATEM, 2 * p + o, c, KT * GROUPS + 2 * p + o + 1, o)
                for n in (U_OUT + 2 * p + 6, U_OUT + 2 * p + 7):
                    split_lo(dve, n, n % 2, n % RING)

            def last_pair(c):
                dve.wait_ge(out_mm, KT // 2 + c)
                for o in range(2):
                    add_gated(bank[3 * o + c], GATEM, KT - 2 + o, c, KT * GROUPS + KT - 2 + o + 1, o)
            last_pair(0)
            reciprocal(2, 0)
            dve.wait_ge(x_written, XW_OUT - 4)
            for k in range(4):
                modulate(2, 0, k, SHIFT2, SCALE2)
            last_pair(1)
            for k in range(4, KT + 1):
                modulate(2, 0, k, SHIFT2, SCALE2)
            last_pair(2)
            reciprocal(2, 1)
            for n in (U_OUT + 12, U_OUT + 13):
                split_lo(dve, n, n % 2, n % RING)
            reciprocal(2, 2)
            dve.wait_ge(x_written, XW_OUT)
            for c in (1, 2):
                modulate_chunk(2, c, SHIFT2, SCALE2)
            dve.wait_ge(xn_lo_ready, 3 * NCH * KT)
            ffn(U_FFN2, 6 * GROUPS, XW_OUT, KT * GROUPS + KT, GATE2, False)

        @block.tensor
        def _(pe):
            pe.wait_ge(const_ready, 1)
            pe.wait_ge(c_silu, 1)
            for k in range(KT):
                last = nc.tensor.transpose(bank[7][:, k * NSEQ:(k + 1) * NSEQ], crow[:, k * P:(k + 1) * P],
                                           ident[0:NSEQ, 0:NSEQ])
            last.then_inc(rows_turned, 1)

            def x_turn(t):
                pe.wait_ge(x_loaded[t], 16 * (1 + t // 2))
                for s in range(3):
                    for b in range(2):
                        if t > 0:
                            pe.wait_ge(x_written, 6 * (t - 1) + 2 * s + b + 1)
                        for k in range(4):
                            last = nc.tensor.transpose(bank[2 * s + b][:, k * P:(k + 1) * P],
                                                       xrow[:, 3 * t + s, (4 * b + k) * P:(4 * b + k + 1) * P],
                                                       ident[:, :])
                        last.then_inc(x_turned, 1)
            x_turn(0)
            x_turn(1)
            pe.wait_ge(rows_loaded, 16 * 13)
            nc.tensor.transpose(bank[6][:, 0:NVEC], vrow[:, :], ident[0:NVEC, 0:NVEC])
            nc.tensor.transpose(bank[6][:, 128:128 + NADA], brow[:, :], ident[0:NADA, 0:NADA])
            for k in range(KT):
                last = nc.tensor.transpose(bank[6][:, 256 + k * 32:256 + (k + 1) * 32], hrow[:, k * P:(k + 1) * P],
                                           ident[0:32, 0:32])
            last.then_inc(rows_turned, 1)
            x_turn(2)

            def first_half(n):
                pe.wait_ge(ada_loaded[n % 4], 16 * (n // 4 + 1))
                if n >= 2:
                    pe.wait_ge(ada_row_ready, n - 1)
                for k in range(KT):
                    last = nc.tensor.matmul(bank[3 + n % 2][0:NSEQ, :], cT[:, k, 0:NSEQ], w_ada_sb[:, n % 4, k, :],
                                            start=k == 0, stop=k == KT - 1)
                last.then_inc(ada_mm, 1)

            def first_turn(n):
                pe.wait_ge(ada_row_ready, n + 1)
                if n >= 3:
                    pe.wait_ge(ada_ready, n - 2)
                for b in range(4):
                    last = nc.tensor.transpose(bank[n % 3][:, b * NSEQ:(b + 1) * NSEQ],
                                               ada_row[0:NSEQ, b * P:(b + 1) * P],
                                               ident[0:NSEQ, 0:NSEQ])
                last.then_inc(ada_folded, 1)

            def sums(i, c):
                pos = max(p for p, (cc, _) in enumerate(squares_order(i)) if cc == c)
                pe.wait_ge(acc_added, added(i, pos + 1))
                if c == 2:
                    pe.wait_ge(std_ready, i * NCH + 1)
                nc.tensor.matmul(bank[6 + c % 2][:, 0:CH], ones[:, :], acc[:, c, :], start=True, stop=True)\
                  .then_inc(sumsq_mm, 1)

            pe.wait_ge(rows_copied, 2)
            pe.wait_ge(x_written, XW_IN)
            first_half(0)
            first_half(1)
            first_turn(0)
            sums(0, 0)
            first_half(2)
            first_turn(1)
            sums(0, 1)
            first_half(3)
            first_turn(2)
            first_half(4)
            first_turn(3)
            sums(0, 2)
            first_half(5)
            first_turn(4)
            first_turn(5)

            def column_job(out, slot, cols, mov_hi, mov_lo):
                for k in range(KT):
                    last = product(pe, out, w_hi[:, slot, k * P:(k + 1) * P], w_lo[:, slot, k * P:(k + 1) * P],
                                   mov_hi[:, k, cols], mov_lo[:, k, cols], k == 0, k == KT - 1)
                return last

            def ffn(i, base, h0, xw0, with_ada):
                def group(g, ada_piece=False, first=False, tail=None):
                    n = g * 6 + base

                    def piece(r):
                        if not ada_piece:
                            return
                        pe.wait_ge(piece_lo_ready, g * 8 + r + 2)
                        for kk in range(2):
                            for part in (ada_hi, ada_lo):
                                k = 2 * (r % 4) + kk
                                last = nc.tensor.matmul(bank[6][0:2 * NSEQ, :], c_parts[:, k, :],
                                                        part[:, kk * HALF:(kk + 1) * HALF],
                                                        start=k == 0 and part is ada_hi,
                                                        stop=k == KT - 1 and part is ada_lo,
                                                        skip_group_check=True)
                        last.then_inc(ada_mm, 1)

                    def fold_half(half):
                        if not ada_piece:
                            return
                        pe.wait_ge(ada_row_ready, g * 2 + (2 * FIRST + half + 1))
                        for b in range(4):
                            o = (4 * half + b) * NSEQ
                            last = nc.tensor.matmul(bank[7][:, o:o + NSEQ], ada_row[:, b * P:(b + 1) * P], fold[:, :],
                                                    start=True, stop=True)
                        last.then_inc(ada_folded, 1)
                    for f in range(2):
                        for c in range(NCH):
                            pe.wait_ge(xn_lo_ready, (i * NCH + c + 1) * KT)
                            for u, done in ((0, gate_mm), (1, up_mm)):
                                q = 2 * f + u
                                pe.wait_ge(w_lo_ready, n + (q + 1))
                                b = 3 * u + c
                                if f == 0:
                                    pe.wait_ge(x_written, g * 24 + (xw0 - 5 + b))
                                elif u == 0:
                                    pe.wait_ge(silu_ready, g * 6 + (h0 + c + 1))
                                else:
                                    pe.wait_ge(h_full, g * 6 + (h0 + c + 1))
                                column_job(bank[b][:, 0:CH], (base + q) % RING, slice(c * CH, (c + 1) * CH),
                                           xn_hi, xn_lo).then_inc(done, 1)
                            if NCH * f + c >= 2:
                                piece(NCH * f + c - 2)
                    pe.wait_ge(w_lo_ready, n + 6)
                    for c in range(NCH):
                        pe.wait_ge(h_lo_ready, g * 6 + (h0 + NCH + c + 1))
                        for o in range(KT):
                            m = c * KT + o
                            if m < 3:
                                pe.wait_ge(silu_ready, g * 6 + (h0 + 3 + m + 1))
                            elif m < 6:
                                pe.wait_ge(h_full, g * 6 + (h0 + m + 1))
                            else:
                                pe.wait_ge(x_written, g * 24 + (xw0 + m - 5))
                            for f in range(2):
                                slot = (base + 4 + f) % RING
                                cols = slice(c * CH, (c + 1) * CH)
                                last = product(pe, bank[m % RING][:, 0:CH], w_hi[:, slot, o * P:(o + 1) * P],
                                               w_lo[:, slot, o * P:(o + 1) * P], h_hi[:, f, cols],
                                               h_lo[:, f, cols], f == 0, f == 1)
                            last.then_inc(down_mm, 1)
                            if m in (3, 7, 11, 15):
                                piece(4 + m // 4)
                            if m == 7:
                                fold_half(0)
                            if tail is not None and m == KT + 3:
                                sums(tail, 0)
                            if tail is not None and m == 2 * KT + 5:
                                sums(tail, 1)
                    fold_half(1)
                    if tail is not None:
                        sums(tail, 2)
                if with_ada:
                    with pe.Fori(0, LATER) as g:
                        group(g, ada_piece=True)
                    with pe.Fori(LATER, GROUPS - 1) as g:
                        group(g)
                    group(GROUPS - 1, tail=1)
                else:
                    with pe.Fori(0, GROUPS - 1) as g:
                        group(g)
                    group(GROUPS - 1, tail=3)

            pe.wait_ge(ada_ready, 2 * FIRST)
            ffn(0, U_FFN1, 0, XW_IN, True)

            for half in range(2):
                for t in range(NT):
                    m = half * NT + t
                    pe.wait_ge(xn_lo_ready, (NCH + t // NCH + 1) * KT)
                    if m >= RING:
                        pe.wait_ge(act_evicted, m + 1 - RING)
                    else:
                        pe.wait_ge(x_written, XW_FFN1)
                    cols = slice(t * P, (t + 1) * P)
                    for k in range(KT):
                        n = U_V + 4 * half + k // 2
                        if t == 0 and k % 2 == 0:
                            pe.wait_ge(w_lo_ready, n + 1)
                        w = slice((k % 2) * HALF, (k % 2 + 1) * HALF)
                        last = product(pe, bank[m % RING][:, :], xn_hi[:, k, cols], xn_lo[:, k, cols],
                                       w_hi[:, n % RING, w], w_lo[:, n % RING, w], k == 0, k == KT - 1)
                    last.then_inc(v_mm, 1)
                    if m == WS_AFTER:
                        for w, src in enumerate((ws_raw, wd_raw)):
                            pe.wait_ge(ws_masked, w + 1)
                            for b in range(2):
                                if w == 1:
                                    pe.wait_ge(ws_lo_ready, b + 1)
                                for h in range(4):
                                    last = nc.tensor.transpose(bank[6 + b][:, h * P:(h + 1) * P], src[:, 4 * b + h, :],
                                                               ident[:, :])
                                last.then_inc(ws_turned, 1)
            pe.wait_ge(ws_lo_ready, 4)

            def mix(j):
                def free(m):
                    if m < 3:
                        pe.wait_ge(s_evicted, j * SPATIAL + (m + 3))
                    else:
                        pe.wait_ge(act_evicted, j * 21 + (2 * NT - 5 + m))

                def section(m, q):
                    pe.wait_ge(w_lo_ready, j * 6 + (U_MIX + q + 1))
                    for c in range(NCH):
                        free(m + c)
                        column_job(bank[(m + c) % RING][:, 0:CH], (U_MIX + q) % RING,
                                   slice(c * CH, (c + 1) * CH), xn_hi, xn_lo).then_inc(mix_mm, 1)
                section(0, 0)
                section(3, 1)
                section(6, 2)
                pe.wait_ge(w_lo_ready, j * 6 + (U_MIX + 4))
                pe.wait_ge(xc_lo_ready, j + 1)
                slot = (U_MIX + 3) % RING
                for c in range(NCH):
                    cols = slice(c * CH, (c + 1) * CH)
                    for g in range(2):
                        m = 9 + 2 * c + g
                        free(m)
                        w = slice(g * P, (g + 1) * P)
                        product(pe, bank[m % RING][:, 0:CH], w_hi[:, slot, w], w_lo[:, slot, w], s_hi[:, cols],
                                s_lo[:, cols], True, True).then_inc(mix_mm, 1)
                section(15, 4)
                pe.wait_ge(vn_lo_ready, j + 1)
                for b in range(SPATIAL):
                    if b < 2:
                        pe.wait_ge(s_evicted, j * SPATIAL + (b + 1))
                    else:
                        free(16 + b)
                    for t in range(2 * b, min(2 * b + 2, NT)):
                        cols = slice(t * P, (t + 1) * P)
                        w = ws_parts[:, int(t == NT - 1), ds(j, 1), :, :].rearrange("p o a t -> p (o a t)")
                        out = bank[S_BANKS[b]][:, (t % 2) * 2 * P:(t % 2 + 1) * 2 * P]
                        nc.tensor.matmul(out, s_hi[:, cols], w, start=True, stop=False, skip_group_check=True)
                        last = nc.tensor.matmul(out, s_lo[:, cols], w, start=False, stop=True,
                                                skip_group_check=True)
                    last.then_inc(s_mm, 1)
                section(21, 5)
            with pe.Fori(0, KT) as j:
                mix(j)

            pe.wait_ge(act_evicted, 2 * NT + 21 * KT)
            pe.wait_ge(s_evicted, SPATIAL * (KT + 1))
            for p in range(KT // 2 - 1):
                pe.wait_ge(w_lo_ready, U_OUT + 2 * p + 2)
                for k in range(KT):
                    pe.wait_ge(m_lo_ready, k + 1)
                    for o in range(2):
                        slot = (U_OUT + 2 * p + o) % RING
                        rows = slice(k * P, (k + 1) * P)
                        for c in range(NCH):
                            if p > 0 and k == 0:
                                pe.wait_ge(x_written, XW_FFN1 + 6 * (p - 1) + 3 * o + c + 1)
                            cols = slice(c * CH, (c + 1) * CH)
                            last = product(pe, bank[3 * o + c][:, 0:CH], w_hi[:, slot, rows], w_lo[:, slot, rows],
                                           xn_hi[:, k, cols], xn_lo[:, k, cols], k == 0, k == KT - 1)
                last.then_inc(out_mm, 1)
            pe.wait_ge(w_lo_ready, U_OUT + KT)
            for c in range(NCH):
                for o in range(2):
                    pe.wait_ge(x_written, XW_OUT - 12 + 3 * o + c + 1)
                    last = column_job(bank[3 * o + c][:, 0:CH], (U_OUT + KT - 2 + o) % RING,
                                      slice(c * CH, (c + 1) * CH), xn_hi, xn_lo)
                    if c == 1 and o == 0:
                        sums(2, 0)
                last.then_inc(out_mm, 1)
            sums(2, 1)
            sums(2, 2)
            pe.wait_ge(x_written, XW_OUT)
            ffn(2, U_FFN2, 6 * GROUPS, XW_OUT, False)
            pe.wait_ge(x_written, XW_FFN2)
            for b in range(2):
                for k in range(4):
                    last = nc.tensor.transpose(bank[b][0:TAIL, k * P:(k + 1) * P], tails[:, 4 * b + k, :], ident[:, :])
                last.then_inc(rows_turned, 1)
            for c in range(NCH):
                pe.wait_ge(xf_ready, (c + 1) * KT)
                if c == NCH - 1:
                    pe.wait_ge(xs_step, 2 * KT * 4)
                for s in range(3):
                    t = 3 * c + s
                    for b in range(2):
                        m = 2 * t + b
                        if t == 0:
                            pe.wait_ge(tail_ready, b + 1)
                        if m >= RING:
                            pe.wait_ge(yrow_dve if b else yrow_act, t - 2)
                        for k in range(4):
                            last = nc.tensor.transpose(bank[m % RING][:, k * P:(k + 1) * P],
                                                       yT[:, c, 4 * b + k, s * P:(s + 1) * P], ident[:, :])
                        last.then_inc(y_turned, 1)
    return nc


_OUTS = (("y_prompt", (1, SEQ, D)), ("y_sample", (NS, LS, D)), ("conv_prompt", (1, 1, HIST, D)),
         ("rglru_prompt", (1, 1, D)), ("sgu_v_prompt", (1, 1, P, D)), ("conv_sample", (1, NS, HIST, D)),
         ("rglru_sample", (1, NS, D)), ("sgu_v_sample", (1, NS, LS, D)))


def kernel(**inputs):
    import concourse.bacc as bacc
    from concourse.bass_utils import run_bass_kernel_spmd

    nc = bacc.Bacc("TRN2", target_bir_lowering=False, num_devices=1, dynamic_dma_scratch_size=1024)
    arrays, ins, outs = {}, {}, {}
    for name, a in inputs.items():
        arrays[f"in_{name}"] = np.ascontiguousarray(a)
        ins[name] = nc.dram_tensor(f"in_{name}", a.shape, F32, kind="ExternalInput").ap()
    for name, shape in _OUTS:
        outs[name] = nc.dram_tensor(f"out_{name}", shape, F32, kind="ExternalOutput").ap()
    build(nc, ins, outs)
    r = run_bass_kernel_spmd(nc, [arrays], core_ids=[0])
    return tuple(r.results[0][f"out_{name}"] for name, _ in _OUTS)
```
